# Optimizing a Trainium2 kernel written in Bass

```python
import jax, jax.numpy as jnp
from jax import lax
import numpy as np
import math

D_MODEL = 1024
BATCH = 1
SEQ = 512
DEPTH = 1

N_MEM = 256
D_MIX = D_MODEL
HEAD_DIM = 64
RET_WIDTH = D_MIX // 2
RWKV_WIDTH = D_MIX - RET_WIDTH
RET_HEADS = RET_WIDTH // HEAD_DIM
RWKV_HEADS = RWKV_WIDTH // HEAD_DIM
RET_CHUNK = 128
ROPE_BASE = 10000.0
DECAY_LORA = 64
AAA_LORA = 64
GATE_LORA = 160
RET_PROJ = 4 * RET_WIDTH
RWKV_PROJ = 3 * RWKV_WIDTH + DECAY_LORA + AAA_LORA + GATE_LORA
D_IN_PROJ = RET_PROJ + RWKV_PROJ
XATTN_HEADS = 4
XATTN_HEAD_DIM = D_MODEL // XATTN_HEADS
D_FF = 4 * D_MODEL
RMS_EPS = 1e-6
GN_EPS_RET = 1e-5
GN_EPS_RWKV = 64e-5


def rmsnorm(x, g):
    xf = x.astype(jnp.float32)
    y = xf * lax.rsqrt(jnp.mean(jnp.square(xf), axis=-1, keepdims=True) + RMS_EPS)
    return (y * g.astype(jnp.float32)).astype(x.dtype)

def head_group_norm(y, w, b, eps):
    B, S, H, d = y.shape
    yf = y.astype(jnp.float32)
    mu = jnp.mean(yf, axis=-1, keepdims=True)
    var = jnp.mean(jnp.square(yf - mu), axis=-1, keepdims=True)
    yn = ((yf - mu) * lax.rsqrt(var + eps)).reshape(B, S, H * d)
    return yn * w.astype(jnp.float32) + b.astype(jnp.float32)

def rope(x, positions):
    d = x.shape[-1]
    half = d // 2
    inv_freq = ROPE_BASE ** (-jnp.arange(half, dtype=jnp.float32) / half)
    ang = positions.astype(jnp.float32)[..., None] * inv_freq
    cos = jnp.cos(ang)[:, :, None, :]
    sin = jnp.sin(ang)[:, :, None, :]
    xf = x.astype(jnp.float32)
    x1, x2 = xf[..., :half], xf[..., half:]
    return jnp.concatenate([x1 * cos - x2 * sin, x2 * cos + x1 * sin], axis=-1)

def retention_chunkwise(q, k, v):
    B, S, H, d = q.shape
    C = RET_CHUNK
    N = S // C
    log_g = jnp.log(1.0 - 2.0 ** (-5.0 - jnp.arange(H, dtype=jnp.float32)))
    idx = jnp.arange(C, dtype=jnp.float32)
    diff = idx[:, None] - idx[None, :]
    causal = diff >= 0
    dmask = jnp.where(causal[None], jnp.exp(log_g[:, None, None] * jnp.where(causal, diff, 0.0)[None]), 0.0)
    xi = jnp.exp(log_g[:, None] * (idx + 1.0)[None])
    zeta = jnp.exp(log_g[:, None] * (C - 1.0 - idx)[None])
    g_chunk = jnp.exp(log_g * C)
    qc = q.reshape(B, N, C, H, d)
    kc = k.reshape(B, N, C, H, d)
    vc = v.reshape(B, N, C, H, d)
    s = jnp.einsum('bnihd,bnjhd->bnhij', qc, kc) * dmask[None, None]
    intra = jnp.einsum('bnhij,bnjhe->bnihe', s, vc)
    kv = jnp.einsum('bnjhd,hj,bnjhe->bnhde', kc, zeta, vc)

    def step(R, kv_n):
        return R * g_chunk[None, :, None, None] + kv_n, R

    _, R_prev = lax.scan(step, jnp.zeros((B, H, d, d), jnp.float32), jnp.moveaxis(kv, 1, 0))
    R_prev = jnp.moveaxis(R_prev, 0, 1)
    inter = jnp.einsum('bnihd,hi,bnhde->bnihe', qc, xi, R_prev)
    return (intra + inter).reshape(B, S, H, d)

def retention_mixer(p, positions, gn_w, gn_b):
    B, S, _ = p.shape
    q, k, v, g = jnp.split(p, 4, axis=-1)
    q = rope(q.reshape(B, S, RET_HEADS, HEAD_DIM), positions)
    k = rope(k.reshape(B, S, RET_HEADS, HEAD_DIM), positions) * (HEAD_DIM ** -0.5)
    v = v.reshape(B, S, RET_HEADS, HEAD_DIM).astype(jnp.float32)
    y = retention_chunkwise(q, k, v)
    return jax.nn.silu(g.astype(jnp.float32)) * head_group_norm(y, gn_w, gn_b, GN_EPS_RET)

def token_shift(p, mu):
    prev = jnp.pad(p, ((0, 0), (1, 0), (0, 0)))[:, :-1]
    return p + (prev - p) * mu

def wkv7_scan(r, w, k, v, a_vec, b_vec):
    B, S, H, d = r.shape

    def step(state, inp):
        r_t, w_t, k_t, v_t, a_t, b_t = inp
        sa = jnp.einsum('bhvk,bhk->bhv', state, a_t)
        state = (state * w_t[:, :, None, :] + sa[..., None] * b_t[:, :, None, :]
                 + v_t[..., None] * k_t[:, :, None, :])
        return state, jnp.einsum('bhvk,bhk->bhv', state, r_t)

    xs = (jnp.moveaxis(r, 1, 0), jnp.moveaxis(w, 1, 0), jnp.moveaxis(k, 1, 0),
          jnp.moveaxis(v, 1, 0), jnp.moveaxis(a_vec, 1, 0), jnp.moveaxis(b_vec, 1, 0))
    _, y = lax.scan(step, jnp.zeros((B, H, d, d), jnp.float32), xs)
    return jnp.moveaxis(y, 0, 1)

def rwkv7_mixer(p, mu, w0, w_up, a0, a_up, g_up, k_k, k_a, r_k, gn_w, gn_b):
    B, S, _ = p.shape
    H, d, W = RWKV_HEADS, HEAD_DIM, RWKV_WIDTH
    p = token_shift(p.astype(jnp.float32), mu.astype(jnp.float32))
    r, k, v, w_lr, a_lr, g_lr = jnp.split(
        p, [W, 2 * W, 3 * W, 3 * W + DECAY_LORA, 3 * W + DECAY_LORA + AAA_LORA], axis=-1)
    w_log = -jax.nn.softplus(-(w0 + jnp.tanh(w_lr) @ w_up)) - 0.5
    decay = jnp.exp(-jnp.exp(w_log))
    a = jax.nn.sigmoid(a0 + a_lr @ a_up)
    g = jax.nn.sigmoid(g_lr) @ g_up
    kk = (k * k_k).reshape(B, S, H, d)
    kk = kk / jnp.maximum(jnp.sqrt(jnp.sum(jnp.square(kk), axis=-1, keepdims=True)), 1e-12)
    k = k * (1.0 + (a - 1.0) * k_a)
    rh = r.reshape(B, S, H, d)
    kh = k.reshape(B, S, H, d)
    vh = v.reshape(B, S, H, d)
    ah = a.reshape(B, S, H, d)
    y = wkv7_scan(rh, decay.reshape(B, S, H, d), kh, vh, -kk, kk * ah)
    y = head_group_norm(y, gn_w, gn_b, GN_EPS_RWKV)
    bonus = jnp.sum(rh * kh * r_k.astype(jnp.float32), axis=-1, keepdims=True) * vh
    return (y + bonus.reshape(B, S, W)) * g

def memory_cross_attention(h, mem_n, w_q, w_kv, w_o):
    B, S, _ = h.shape
    M = mem_n.shape[1]
    q = (h @ w_q).reshape(B, S, XATTN_HEADS, XATTN_HEAD_DIM)
    k, v = jnp.split(mem_n @ w_kv, 2, axis=-1)
    k = k.reshape(B, M, XATTN_HEADS, XATTN_HEAD_DIM)
    v = v.reshape(B, M, XATTN_HEADS, XATTN_HEAD_DIM)
    s = jnp.einsum('bshd,bmhd->bhsm', q.astype(jnp.float32), k.astype(jnp.float32)) * (XATTN_HEAD_DIM ** -0.5)
    prob = jax.nn.softmax(s, axis=-1).astype(v.dtype)
    o = jnp.einsum('bhsm,bmhd->bshd', prob, v).reshape(B, S, D_MODEL)
    return o @ w_o

def first_inputs(seed: int = 0) -> dict:
    key = jax.random.key(seed)
    ks = jax.random.split(key, 32)
    f32 = jnp.float32
    L = DEPTH

    def nrm(k, shape, scale):
        return jax.random.normal(k, shape, f32) * scale

    def gain(k, shape):
        return 1.0 + 0.05 * jax.random.normal(k, shape, f32)

    x = jax.random.normal(ks[0], (BATCH, SEQ, D_MODEL), f32)
    mem = jax.random.normal(ks[1], (BATCH, N_MEM, D_MODEL), f32)
    positions = jnp.broadcast_to(jnp.arange(SEQ, dtype=jnp.int32)[None], (BATCH, SEQ))
    return {
        "x": x,
        "mem": mem,
        "positions": positions,
        "norm_mix": gain(ks[2], (L, D_MODEL)),
        "w_in": nrm(ks[3], (L, D_MODEL, D_IN_PROJ), D_MODEL ** -0.5),
        "ret_gn_w": gain(ks[4], (L, RET_WIDTH)),
        "ret_gn_b": nrm(ks[5], (L, RET_WIDTH), 0.02),
        "rwkv_mu": jax.random.uniform(ks[6], (L, RWKV_PROJ), f32),
        "rwkv_w0": jax.random.uniform(ks[7], (L, RWKV_WIDTH), f32, -6.5, -1.5),
        "rwkv_w_up": nrm(ks[8], (L, DECAY_LORA, RWKV_WIDTH), 0.1 * DECAY_LORA ** -0.5),
        "rwkv_a0": nrm(ks[9], (L, RWKV_WIDTH), 0.1),
        "rwkv_a_up": nrm(ks[10], (L, AAA_LORA, RWKV_WIDTH), 0.1 * AAA_LORA ** -0.5),
        "rwkv_g_up": nrm(ks[11], (L, GATE_LORA, RWKV_WIDTH), GATE_LORA ** -0.5),
        "rwkv_k_k": 0.85 + 0.05 * jax.random.normal(ks[12], (L, RWKV_WIDTH), f32),
        "rwkv_k_a": gain(ks[13], (L, RWKV_WIDTH)),
        "rwkv_r_k": nrm(ks[14], (L, RWKV_HEADS, HEAD_DIM), 0.1),
        "rwkv_gn_w": gain(ks[15], (L, RWKV_WIDTH)),
        "rwkv_gn_b": nrm(ks[16], (L, RWKV_WIDTH), 0.02),
        "w_out": nrm(ks[17], (L, D_MIX, D_MODEL), D_MIX ** -0.5),
        "norm_xattn": gain(ks[18], (L, D_MODEL)),
        "norm_mem": gain(ks[19], (L, D_MODEL)),
        "xattn_w_q": nrm(ks[20], (L, D_MODEL, D_MODEL), D_MODEL ** -0.5),
        "xattn_w_kv": nrm(ks[21], (L, D_MODEL, 2 * D_MODEL), D_MODEL ** -0.5),
        "xattn_w_o": nrm(ks[22], (L, D_MODEL, D_MODEL), D_MODEL ** -0.5),
        "norm_mlp": gain(ks[23], (L, D_MODEL)),
        "mlp_w_up": nrm(ks[24], (L, D_MODEL, D_FF), D_MODEL ** -0.5),
        "mlp_w_down": nrm(ks[25], (L, D_FF, D_MODEL), D_FF ** -0.5),
        "norm_final": gain(ks[26], (D_MODEL,)),
    }

def first_block(x, mem, positions, norm_mix, w_in, ret_gn_w, ret_gn_b, rwkv_mu, rwkv_w0,
              rwkv_w_up, rwkv_a0, rwkv_a_up, rwkv_g_up, rwkv_k_k, rwkv_k_a, rwkv_r_k,
              rwkv_gn_w, rwkv_gn_b, w_out, norm_xattn, norm_mem, xattn_w_q, xattn_w_kv,
              xattn_w_o, norm_mlp, mlp_w_up, mlp_w_down, norm_final):
    dt = x.dtype
    for l in range(DEPTH):
        h = rmsnorm(x, norm_mix[l])
        p = h @ w_in[l]
        y_ret = retention_mixer(p[..., :RET_PROJ], positions, ret_gn_w[l], ret_gn_b[l])
        y_rwkv = rwkv7_mixer(p[..., RET_PROJ:], rwkv_mu[l], rwkv_w0[l], rwkv_w_up[l], rwkv_a0[l],
                             rwkv_a_up[l], rwkv_g_up[l], rwkv_k_k[l], rwkv_k_a[l], rwkv_r_k[l],
                             rwkv_gn_w[l], rwkv_gn_b[l])
        y = jnp.concatenate([y_ret, y_rwkv], axis=-1).astype(dt)
        x = x + y @ w_out[l]
        x = x + memory_cross_attention(rmsnorm(x, norm_xattn[l]), rmsnorm(mem, norm_mem[l]),
                                       xattn_w_q[l], xattn_w_kv[l], xattn_w_o[l])
        h = rmsnorm(x, norm_mlp[l])
        x = x + jnp.square(jax.nn.relu(h @ mlp_w_up[l])) @ mlp_w_down[l]
    return rmsnorm(x, norm_final)


GRID_W = 64
N_Q_HEADS = 8
N_KV_HEADS = 2
GQA_GROUP = N_Q_HEADS // N_KV_HEADS
ATTN_WIDTH = N_Q_HEADS * HEAD_DIM
KV_WIDTH = N_KV_HEADS * HEAD_DIM
Q_BLOCK = 128
AXIAL_DIM = HEAD_DIM // 2
ROPE_THETA = 10000.0
CHUNK = 128
N_GROUPS = 8
GMLP_WIDTH = 512
GROUP_DIM = GMLP_WIDTH // N_GROUPS
N_BRANCHES = 2
EPS = 1e-6

IN_SIZES = (ATTN_WIDTH, KV_WIDTH, KV_WIDTH, ATTN_WIDTH,
            GMLP_WIDTH, GMLP_WIDTH, GMLP_WIDTH, N_BRANCHES * D_MODEL)
IN_WIDTH = sum(IN_SIZES)
IN_SPLITS = tuple(int(s) for s in np.cumsum(IN_SIZES)[:-1])


def rmsnorm_2(x, gain):
    x32 = x.astype(jnp.float32)
    y = x32 * lax.rsqrt(jnp.mean(x32 * x32, axis=-1, keepdims=True) + EPS)
    return (y * gain.astype(jnp.float32)).astype(x.dtype)

def layernorm(x, gain, bias):
    x32 = x.astype(jnp.float32)
    mu = jnp.mean(x32, axis=-1, keepdims=True)
    var = jnp.mean(jnp.square(x32 - mu), axis=-1, keepdims=True)
    y = (x32 - mu) * lax.rsqrt(var + EPS)
    return (y * gain.astype(jnp.float32) + bias.astype(jnp.float32)).astype(x.dtype)

def rope_half(x, ang):
    n = x.shape[-1] // 2
    x1, x2 = x[..., :n], x[..., n:]
    cos, sin = jnp.cos(ang).astype(x.dtype), jnp.sin(ang).astype(x.dtype)
    return jnp.concatenate([x1 * cos - x2 * sin, x1 * sin + x2 * cos], axis=-1)

def axial_rope(x, row_ang, col_ang):
    return jnp.concatenate([rope_half(x[..., :AXIAL_DIM], row_ang),
                            rope_half(x[..., AXIAL_DIM:], col_ang)], axis=-1)

def block_attention(q, k, v):
    B, S = q.shape[0], q.shape[1]
    n_blk = S // Q_BLOCK
    scale = 1.0 / math.sqrt(HEAD_DIM)
    qb = q.reshape(B, n_blk, Q_BLOCK, N_KV_HEADS, GQA_GROUP, HEAD_DIM).transpose(1, 0, 3, 4, 2, 5)
    kt = k.transpose(0, 2, 1, 3)
    vt = v.transpose(0, 2, 1, 3)

    def one_block(q_blk):
        s = jnp.einsum('bhgqd,bhkd->bhgqk', q_blk, kt).astype(jnp.float32) * scale
        p = jax.nn.softmax(s, axis=-1).astype(vt.dtype)
        return jnp.einsum('bhgqk,bhkd->bhgqd', p, vt)

    o = lax.map(one_block, qb)
    return o.transpose(1, 0, 4, 2, 3, 5).reshape(B, S, ATTN_WIDTH)

def hybrid_layer(x, norm_gain, w_in, q_gain, k_gain, w_proj_attn,
                 ln_v_gain, ln_v_bias, w_spatial, b_spatial, w_proj_gmlp,
                 b_merge, w_out):
    B, S, _ = x.shape
    rows = S // GRID_W
    h = rmsnorm_2(x, norm_gain)
    z = jnp.einsum('bsd,de->bse', h, w_in)
    q, k, v, gate_a, u_in, v_in, gate_b, g_merge = jnp.split(z, IN_SPLITS, axis=-1)

    row_idx = jnp.repeat(jnp.arange(rows, dtype=jnp.float32), GRID_W)
    col_idx = jnp.tile(jnp.arange(GRID_W, dtype=jnp.float32), rows)
    inv_freq = ROPE_THETA ** (-jnp.arange(0, AXIAL_DIM, 2, dtype=jnp.float32) / AXIAL_DIM)
    row_ang = (row_idx[:, None] * inv_freq)[:, None, :]
    col_ang = (col_idx[:, None] * inv_freq)[:, None, :]
    q = axial_rope(rmsnorm_2(q.reshape(B, S, N_Q_HEADS, HEAD_DIM), q_gain), row_ang, col_ang)
    k = axial_rope(rmsnorm_2(k.reshape(B, S, N_KV_HEADS, HEAD_DIM), k_gain), row_ang, col_ang)
    v = v.reshape(B, S, N_KV_HEADS, HEAD_DIM)
    attn = block_attention(q, k, v) * jax.nn.silu(gate_a)
    y_a = jnp.einsum('bse,ed->bsd', attn, w_proj_attn)

    u = jax.nn.gelu(u_in)
    vv = layernorm(jax.nn.gelu(v_in), ln_v_gain, ln_v_bias)
    vv = vv.reshape(B, S // CHUNK, CHUNK, N_GROUPS, GROUP_DIM)
    v_mix = jnp.einsum('gij,bcjgd->bcigd', w_spatial, vv) + b_spatial.T[:, :, None]
    gm = u * v_mix.reshape(B, S, GMLP_WIDTH) * jax.nn.silu(gate_b)
    y_b = jnp.einsum('bse,ed->bsd', gm, w_proj_gmlp)

    g = jax.nn.sigmoid(g_merge.reshape(B, S, N_BRANCHES, D_MODEL) + b_merge)
    y = g[:, :, 0, :] * y_a + g[:, :, 1, :] * y_b
    return x + jnp.einsum('bsd,de->bse', y, w_out)

def second_inputs(seed: int = 0) -> dict:
    key = jax.random.key(seed)
    ks = jax.random.split(key, 16)
    L = DEPTH
    nrm = lambda k, shape, fan: jax.random.normal(k, shape, jnp.float32) * (fan ** -0.5)
    return {
        "x": jax.random.normal(ks[0], (BATCH, SEQ, D_MODEL), jnp.float32),
        "norm_gain": 1.0 + 0.05 * jax.random.normal(ks[1], (L, D_MODEL), jnp.float32),
        "w_in": nrm(ks[2], (L, D_MODEL, IN_WIDTH), D_MODEL),
        "q_gain": 1.0 + 0.05 * jax.random.normal(ks[3], (L, HEAD_DIM), jnp.float32),
        "k_gain": 1.0 + 0.05 * jax.random.normal(ks[4], (L, HEAD_DIM), jnp.float32),
        "w_proj_attn": nrm(ks[5], (L, ATTN_WIDTH, D_MODEL), ATTN_WIDTH),
        "ln_v_gain": 1.0 + 0.05 * jax.random.normal(ks[6], (L, GMLP_WIDTH), jnp.float32),
        "ln_v_bias": 0.02 * jax.random.normal(ks[7], (L, GMLP_WIDTH), jnp.float32),
        "w_spatial": nrm(ks[8], (L, N_GROUPS, CHUNK, CHUNK), CHUNK),
        "b_spatial": 1.0 + 0.05 * jax.random.normal(ks[9], (L, N_GROUPS, CHUNK), jnp.float32),
        "w_proj_gmlp": nrm(ks[10], (L, GMLP_WIDTH, D_MODEL), GMLP_WIDTH),
        "b_merge": 0.02 * jax.random.normal(ks[11], (L, N_BRANCHES, D_MODEL), jnp.float32),
        "w_out": nrm(ks[12], (L, D_MODEL, D_MODEL), D_MODEL),
        "final_gain": 1.0 + 0.05 * jax.random.normal(ks[13], (D_MODEL,), jnp.float32),
    }

def second_block(x, norm_gain, w_in, q_gain, k_gain, w_proj_attn, ln_v_gain, ln_v_bias,
              w_spatial, b_spatial, w_proj_gmlp, b_merge, w_out, final_gain):
    for l in range(DEPTH):
        x = hybrid_layer(x, norm_gain[l], w_in[l], q_gain[l], k_gain[l], w_proj_attn[l],
                         ln_v_gain[l], ln_v_bias[l], w_spatial[l], b_spatial[l],
                         w_proj_gmlp[l], b_merge[l], w_out[l])
    return rmsnorm_2(x, final_gain)


def setup_inputs(seed=0):
    out = dict(first_inputs(seed))
    for name, value in second_inputs(seed + 1).items():
        if name != "x":
            out[name + "_2"] = value
    return out


def reference(
    x, mem, positions, norm_mix, w_in, ret_gn_w, ret_gn_b, rwkv_mu, rwkv_w0, rwkv_w_up, rwkv_a0,
    rwkv_a_up, rwkv_g_up, rwkv_k_k, rwkv_k_a, rwkv_r_k, rwkv_gn_w, rwkv_gn_b, w_out, norm_xattn,
    norm_mem, xattn_w_q, xattn_w_kv, xattn_w_o, norm_mlp, mlp_w_up, mlp_w_down, norm_final,
    norm_gain_2, w_in_2, q_gain_2, k_gain_2, w_proj_attn_2, ln_v_gain_2, ln_v_bias_2,
    w_spatial_2, b_spatial_2, w_proj_gmlp_2, b_merge_2, w_out_2, final_gain_2,
):
    x = first_block(
        x, mem, positions, norm_mix, w_in, ret_gn_w, ret_gn_b, rwkv_mu, rwkv_w0, rwkv_w_up,
        rwkv_a0, rwkv_a_up, rwkv_g_up, rwkv_k_k, rwkv_k_a, rwkv_r_k, rwkv_gn_w, rwkv_gn_b,
        w_out, norm_xattn, norm_mem, xattn_w_q, xattn_w_kv, xattn_w_o, norm_mlp, mlp_w_up,
        mlp_w_down, norm_final,
    )
    return second_block(
        x, norm_gain_2, w_in_2, q_gain_2, k_gain_2, w_proj_attn_2, ln_v_gain_2, ln_v_bias_2,
        w_spatial_2, b_spatial_2, w_proj_gmlp_2, b_merge_2, w_out_2, final_gain_2,
    )


_drawn_inputs = setup_inputs


def setup_inputs(seed=0):
    import zlib

    import numpy as np

    out = dict(_drawn_inputs(seed))
    spreads = {}
    factors = {'ret_gn_w': 2.723,
     'ret_gn_b': 6.482,
     'rwkv_w_up': 8.0,
     'rwkv_a0': 3.494,
     'rwkv_a_up': 3.492,
     'rwkv_k_k': 3.133,
     'rwkv_k_a': 2.795,
     'rwkv_gn_w': 3.045,
     'rwkv_gn_b': 7.68,
     'norm_xattn': 8.0,
     'norm_mem': 7.067,
     'q_gain_2': 8.0,
     'k_gain_2': 8.0,
     'ln_v_gain_2': 5.943,
     'ln_v_bias_2': 29.169,
     'b_spatial_2': 5.532,
     'b_merge_2': 8.0}
    for name, (base, spread) in spreads.items():
        noise = np.random.default_rng([zlib.crc32(name.encode()), seed]).standard_normal(out[name].shape)
        drawn = base * np.exp(spread * noise) if base else spread * noise
        out[name] = __import__('jax').numpy.asarray(drawn.astype(out[name].dtype))
    for name, factor in factors.items():
        out[name] = (out[name] * factor).astype(out[name].dtype)
    return out
```

```python
import concourse.bass as bass
from concourse import mybir
from concourse.alu_op_type import AluOpType as ALU
from contextlib import ExitStack

P = 128
T = 512
DM = 1024
KC = DM // P
TT = T // P
HD = 64
MEM = 256
XH = 4
CH = 64
NCH = T // CH
RH = 8
NF = 4
EXP_HALF = 0.6065306597126334
QH = 8
NGRP = 8
MLP_Q = 4

S_RQ, S_RK, S_RV, S_RG = 0, 4, 8, 12
S_WA, S_G0, S_G1 = 16, 17, 18
S_K, S_R, S_V = 19, 23, 27
S_WOUT = 31
S_MK, S_MV = 39, 47
S_XQ, S_XO = 55, 63
S_MLP = 71
S_VIN = S_MLP + MLP_Q * 16
S_V2, S_K2, S_Q2 = S_VIN + 4, S_VIN + 5, S_VIN + 6
S_U, S_GA, S_GB, S_MERGE = S_Q2 + 4, S_Q2 + 8, S_Q2 + 12, S_Q2 + 16
S_OUT2 = S_MERGE + 24
NSLAB = S_OUT2 + 8

PARAMS = [("norm_mix", 8), ("ret_gn_w", 4), ("ret_gn_b", 4), ("mu", 15), ("a0", 4), ("k_k", 4), ("k_a", 4),
          ("r_k", 4), ("gn_w", 4), ("gn_b", 4), ("norm_xattn", 8), ("norm_mem", 8), ("norm_mlp", 8),
          ("norm_final", 8), ("norm_gain_2", 8), ("q_gain", 1), ("k_gain", 1), ("b_merge", 16), ("final_gain", 8)]
CONSTS = [("ident", 128), ("ones", 128), ("blockones", 128), ("center", 128), ("swap_ret", 128), ("swap_ax", 128),
          ("cum_inc", 128), ("cum_exc", 128), ("mask_strict", 128), ("mask_inc", 128), ("mask_pair", 128),
          ("mask_level", 5 * 128), ("sel", 50), ("spread", 5 * 128), ("spread_q", 5 * 128), ("ident2", 64),
          ("eps6", 1), ("eps5", 1), ("eps64", 1), ("inv_freq", 1)]


def columns(table):
    at, out = 0, {}
    for name, n in table:
        out[name] = (at, at + n)
        at += n
    return out, at


def hybrid_blocks(nc, ins, out):
    F32, F32R = mybir.dt.float32, mybir.dt.float32r
    ACT = mybir.ActivationFunctionType
    AX = mybir.AxisListType
    cst, n_cst = columns(CONSTS)
    par, n_par = columns(PARAMS)

    ctx = ExitStack()
    with ctx:
        sems = {}

        def S(name):
            if name not in sems:
                sems[name] = ctx.enter_context(nc.semaphore(name))
            return sems[name]

        base = -(-nc.sbuf_base // 1024) * 1024

        def at(name, kib, shape, dtype=F32):
            return nc.alloc_sbuf_tensor_at(name, shape, dtype, offset=base + int(kib * 1024))

        fence = ctx.enter_context(nc.sbuf_tensor("fence", [P, (206 * 1024) // 4], F32))
        del fence
        psum = [ctx.enter_context(nc.psum_tensor(f"bank{i}", [P, 512], F32)) for i in range(8)]

        consts = at("consts", 0, [P, n_cst])
        params = at("params", 13.5, [P, n_par])
        small = at("small", 14, [P, 512])

        def C(name, a=0, n=None):
            lo, hi = cst[name]
            return consts[:, lo + a:(hi if n is None else lo + a + n)]

        def V(name, j=0):
            return params[:, par[name][0] + j:par[name][0] + j + 1]

        w_raw = at("w_raw", 16, [P, 2, KC * P])
        w_hi = at("w_hi", 24, [P, 2, KC * P], F32R)
        w_lo = at("w_lo", 32, [P, 2, KC * P], F32R)
        rstd = at("rstd", 40, [P, T])
        a_hi = at("a_hi", 62, [P, KC, T], F32R)
        a_lo = at("a_lo", 78, [P, KC, T], F32R)

        cos_r = at("cos_r", 42, [P, T])
        sin_r = at("sin_r", 44, [P, T])
        lora = at("lora", 46, [P, 512])
        g_up = at("g_up", 48, [P, 2, 512])
        w0_row = at("w0_row", 52, [1, 512])
        decay = at("decay", 94, [P, RH, T])
        x_in = at("x_in", 110, [P, KC, T])
        qk = at("qk", 110, [P, 8, T])
        v_ret = at("v_ret", 126, [P, TT, 512])
        trig = at("trig", 126, [P, 4, T])
        pos = at("pos", 134, [P, T], mybir.dt.int32)
        rg = at("rg", 134, [P, NF, T])
        sq_in = at("sq_in", 142, [P, KC, T])
        low = at("low", 142, [P, 3, T])
        tmp = at("tmp", 148, [P, 2, T])
        s_ret = at("s_ret", 142, [P, 2, 1280])
        kx = at("kx", 152, [P, NF, T])
        rx = at("rx", 160, [P, NF, T])
        vx = at("vx", 168, [P, NF, T])
        ax = at("ax", 176, [P, NF, T])
        gx = at("gx", 184, [P, NF, T])
        lw = at("lw", 192, [P, TT, 512])
        shift = at("shift", 200, [P, 2, T + 1])
        kk = at("kk", 62, [P, NF, T])
        e_inc = at("e_inc", 70, [P, NF, T])
        e_neg = at("e_neg", 78, [P, NF, T])
        e_exc = at("e_exc", 86, [P, NF, T])
        bh = at("bh", 54, [P, NF, T])
        pt = at("pt", 200, [P, 2, T])
        kh = at("kh", 46, [P, NF, T])
        sqk = at("sqk", 54, [P, NF, T])
        rn = at("rn", 40, [P, T])
        bon = at("bon", 192, [P, NF, T])
        sc = small[:, 0:NF * NCH].rearrange("p (f c) -> p f c", f=NF)
        sr = small[:, 32:64].rearrange("p (f c) -> p f c", f=NF)
        one_ka = small[:, 64:68]
        r_tok = small[:, 68:76]
        gsd = at("gsd", 42, [P, T])
        grn = at("grn", 44, [P, T])
        a_tok = at("a_tok", 94, [P, TT, 512])
        b_tok = at("b_tok", 102, [P, TT, 512])
        k_tok = at("k_tok", 110, [P, TT, 512])
        v_tok = at("v_tok", 118, [P, TT, 512])
        RB = at("RB", 70, [P, 4, T])
        RK = at("RK", 78, [P, 4, T])
        AB = at("AB", 86, [P, 4, T])
        X = at("X", 126, [P, 4, T])
        XT = at("XT", 142, [P, 4, T])
        PX = at("PX", 168, [P, 4, T])
        GH = at("GH", 40, [P, 4, TT, 2, HD])
        ST = at("ST", 48, [P, NCH, 2, HD])
        QT = at("QT", 52, [P, 2, T])
        BC = at("BC", 56, [P, 2, NCH, HD])
        AT = at("AT", 200, [P, 2, NCH, HD])
        hsd = at("hsd", 86, [P, T])
        hrn = at("hrn", 88, [P, T])

        x_res = at("x_res", 110, [P, KC, T])
        b_hi = at("b_hi", 126, [P, KC, T], F32R)
        b_lo = at("b_lo", 142, [P, KC, T], F32R)
        sqb = at("sqb", 42, [P, 2, T])
        mem_in = at("mem_in", 158, [P, KC, MEM])
        mem_sq = at("mem_sq", 166, [P, KC, MEM])
        mem_hi = at("mem_hi", 190, [P, KC, MEM], F32R)
        mem_lo = at("mem_lo", 198, [P, KC, MEM], F32R)
        mem_k = at("mem_k", 174, [P, KC, MEM])
        mem_v = at("mem_v", 182, [P, MEM // P, DM])
        mem_rs = at("mem_rs", 46, [P, MEM])
        xq = at("xq", 158, [P, KC, T])
        prob = at("prob", 190, [P, 2, TT, MEM])
        prob_t = at("prob_t", 198, [P, 2, MEM // P, T])
        m_hi = at("m_hi", 158, [P, KC, T], F32R)
        m_lo = at("m_lo", 174, [P, KC, T], F32R)
        m_mid = at("m_mid", 190, [P, 2, T])
        m_tok = small[:, 76:80]
        neg_max = small[:, 80:84]
        p_sum = small[:, 84:88]
        p_inv = small[:, 88:92]
        gain_12 = small[:, 92:100]
        rs_all = at("rs_all", 46, [P, T])
        rs_tmp = at("rs_tmp", 48, [P, T])
        v2 = at("v2", 50, [P, TT, P])
        qk2 = at("qk2", 52, [P, 5, T])
        rn2 = at("rn2", 48, [P, T])
        vv = at("vv", 94, [P, TT, 512])
        u2 = at("u2", 102, [P, NF, T])
        ga = at("ga", 158, [P, NF, T])
        gb = at("gb", 166, [P, NF, T])
        ln = at("ln", 174, [P, 2, 512])
        spatial = at("spatial", 178, [P, NGRP, P])
        axial = at("axial", 182, [P, 2, T])
        b_row = at("b_row", 186, [1, NGRP * P])
        sq10 = at("sq10", 190, [P, 5, T])
        tmp2 = at("tmp2", 200, [P, 2, T])
        p2 = at("p2", 190, [P, 2, 2, T])
        p2_t = at("p2_t", 198, [P, TT, T])
        r2_tok = small[:, 100:108]
        ln_stats = small[:, 108:132]
        ln_mv = small[:, 132:140]
        ln_rs = small[:, 140:144]
        max2 = small[:, 144:146]
        sum2 = small[:, 146:148]
        inv2 = small[:, 148:150]
        gate = at("gate", 174, [P, 4, T])
        y_mid = at("y_mid", 182, [P, 2, T])
        y_hi = at("y_hi", 94, [P, KC, T], F32R)
        y_lo = at("y_lo", 158, [P, KC, T], F32R)
        o_fin = at("o_fin", 174, [P, 2, T])

        block = ctx.enter_context(nc.Block())
        W = ins["weights"]

        @block.sync
        def _(sp):
            for s in range(NSLAB):
                if s >= 2:
                    sp.wait_ge(S("w_lo_ready"), s - 1)
                sp.dma_start(w_raw[:, s % 2, :], W[s]).then_inc(S(f"w_loaded{s % 2}"), 16)
            for n in range(KC):
                sp.wait_ge(S("out_ready"), n + 1)
                sp.dma_start(out[:, n, :], o_fin[:, n % 2, :]).then_inc(S(f"out_stored{n % 2}"), 16)
            for i in range(2):
                sp.wait_ge(S(f"out_stored{i}"), 16 * (KC // 2))

        @block.gpsimd
        def _(pool):
            for s in range(NSLAB):
                pool.wait_ge(S("w_hi_ready"), s + 1)
                nc.gpsimd.tensor_tensor(w_lo[:, s % 2, :], w_raw[:, s % 2, :], w_hi[:, s % 2, :].bitcast(F32),
                                        ALU.subtract).then_inc(S("w_lo_ready"), 1)

        @block.scalar
        def _(act):
            copy, exp, sigmoid, square, sqrt = ACT.Copy, ACT.Exp, ACT.Sigmoid, ACT.Square, ACT.Sqrt
            marks, last = {}, []

            def A(name):
                marks[name] = marks.get(name, 0) + 1
                last[:] = [name, marks[name]]
                return S(name)

            def actv(o, a, f, **kw):
                if last:
                    act.wait_ge(S(last[0]), last[1])
                return nc.scalar.activation(o, a, f, **kw)


            def split_hi(s):
                if s >= NSLAB:
                    return
                act.wait_ge(S(f"w_loaded{s % 2}"), 16 * (s // 2 + 1))
                if s >= 2:
                    act.wait_ge(S("slab_done"), s - 1)
                actv(w_hi[:, s % 2, :], w_raw[:, s % 2, :], copy).then_inc(A("w_hi_ready"), 1)

            act.dma_start(params[:], ins["params"]).then_inc(S("params_loaded"), 16)
            act.dma_start(pos[:], ins["pos"]).then_inc(S("pos_loaded"), 16)
            act.dma_start(consts[:], ins["consts"]).then_inc(S("consts_loaded"), 16)
            for i in range(4):
                act.dma_start(x_in[:, 2 * i:2 * i + 2, :], ins["x"][:, 2 * i:2 * i + 2, :]).then_inc(S(f"x_loaded{i}"), 16)
            act.dma_start(lora[:], ins["lora"]).then_inc(S("lora_loaded"), 16)
            act.dma_start(g_up[:], ins["g_up"]).then_inc(S("lora_loaded"), 16)
            act.dma_start(w0_row[:], ins["rows"][:, 0:512]).then_inc(S("lora_loaded"), 16)
            act.dma_start(decay[:], ins["decay"]).then_inc(S("decay_loaded"), 16)

            act.wait_ge(S("params_loaded"), 16)
            act.wait_ge(S("angle_ready"), 1)
            actv(sin_r[:], trig[:, 0, :], ACT.Sin).then_inc(A("act_step"), 1)
            actv(trig[:, 1, :], trig[:, 0, :], ACT.Sin, scale=0.5).then_inc(A("sines_ready"), 1)
            split_hi(0)
            split_hi(1)
            for kc in range(KC):
                act.wait_ge(S(f"x_loaded{kc // 2}"), 16)
                actv(a_hi[:, kc, :], x_in[:, kc, :], copy, scale=V("norm_mix", kc)).then_inc(A("a_hi_ready"), 1)
                actv(sq_in[:, kc, :], x_in[:, kc, :], square).then_inc(A("xn_sq"), 1)
            for s in range(S_WOUT):
                split_hi(s + 2)
                if s == 0:
                    act.wait_ge(S("consts_loaded"), 16)
                    act.wait_ge(S("ssq_done"), 1)
                    actv(rstd[:], psum[7][:], sqrt, bias=C("eps6"), scale=1.0 / DM).then_inc(A("rms_ready"), 1)
                if s == S_WA + 1:
                    for f in range(NF):
                        act.wait_ge(S("tile_taken"), S_RG + f + 1)
                        actv(rg[:, f, :], rg[:, f, :], ACT.Silu).then_inc(A("silu_ready"), 1)
                if s == S_WA + 2:
                    act.wait_ge(S("low_ready"), 1)
                    actv(low[0:HD, 0, :], low[0:HD, 0, :], ACT.Tanh).then_inc(A("low_act"), 1)
                    for j in (1, 2):
                        act.wait_ge(S("low_ready"), j + 1)
                        actv(low[:, j, :], low[:, j, :], sigmoid).then_inc(A("low_act"), 1)
                if s == S_K + 1:
                    for t in range(TT):
                        act.wait_ge(S("lora_done"), t + 1)
                        actv(lw[:, t, :], psum[2 + t % 2][:], sigmoid).then_inc(A("lora_ready"), 1)
                if s == S_K + 2:
                    for f in range(NF):
                        act.wait_ge(S("lora_done"), TT + f + 1)
                        actv(ax[:, f, :], psum[4 + f % 2][:], sigmoid, bias=V("a0", f)).then_inc(A("lora_ready"), 1)
                if s == S_K + 3:
                    for f in range(NF):
                        act.wait_ge(S("lora_done"), TT + NF + f + 1)
                        actv(gx[:, f, :], psum[6 + f % 2][:], copy).then_inc(A("lora_ready"), 1)

            act.wait_ge(S("slab_done"), S_WOUT)
            for f in range(NF):
                act.wait_ge(S("kk0_ready"), f + 1)
                actv(sqk[:, f, :], kk[:, f, :], square).then_inc(A("sqk_ready"), 1)
            act.wait_ge(S("kss_done"), 1)
            actv(rn[0:8, :], psum[4][0:8, :], sqrt).then_inc(A("kn_ready"), 1)

            def exps(f):
                act.wait_ge(S("cum_done"), f + 1)
                bi, be = psum[2 * (f % 2)], psum[2 * (f % 2) + 1]
                actv(e_inc[:, f, :], bi[:], exp).then_inc(A("act_step"), 1)
                actv(e_neg[:, f, :], bi[:], exp, scale=-1.0).then_inc(A("act_step"), 1)
                actv(e_exc[:, f, :], be[:], exp).then_inc(A("exps_ready"), 1)

            exps(0)
            exps(1)
            exps(2)
            exps(3)
            for f in range(NF):
                act.wait_ge(S("y_ret_step"), 2 * f + 2)
                actv(qk[:, f, :], psum[6 + f % 2][:], copy).then_inc(A("y_ret_out"), 1)
            for f in range(NF):
                act.wait_ge(S("gn_cent_done"), f + 1)
                actv(qk[:, 4 + f, :], psum[2 + f][:], copy).then_inc(A("gn_cent"), 1)
                actv(qk[:, f, :], psum[2 + f][:], square).then_inc(A("gn_sq"), 1)
            act.wait_ge(S("gn_var_done"), 1)
            actv(gsd[0:8, :], psum[6][0:8, :], sqrt, bias=C("eps5")[0:8], scale=1.0 / HD).then_inc(A("gn_sd"), 1)

            n = 0
            for q, dst in enumerate((a_tok, b_tok, k_tok, v_tok)):
                for t in range(TT):
                    n += 1
                    act.wait_ge(S("tok_done"), n)
                    actv(dst[:, t, :], psum[(n - 1) % 8][:], copy).then_inc(A("tok_ready"), 1)
            for g in range(2):
                for j in range(4):
                    act.wait_ge(S("u_done"), 4 * g + j + 1)
                    actv(GH[:, j, :, 1, :], psum[2 * j][:, 0:256].rearrange("p (t e) -> p t e", t=TT),
                                         copy).then_inc(A("u_ready"), 1)
                    act.wait_ge(S("x0_done"), 4 * g + j + 1)
                    actv(X[:, j, :], psum[2 * j + 1][:], copy).then_inc(A("x0_ready"), 1)
                for lv in range(4):
                    for j in range(4):
                        act.wait_ge(S("xt_done"), 4 * (4 * g + lv) + j + 1)
                        actv(XT[:, j, :], psum[2 * j][:], copy).then_inc(A("xt_ready"), 1)
                for j in range(4):
                    act.wait_ge(S("gh_done"), 4 * g + j + 1)
                    actv(GH[:, j].rearrange("p t k e -> p (t k e)"), psum[2 * j][:], copy).then_inc(A("gh_ready"), 1)
                for i in range(2):
                    act.wait_ge(S("bc_done"), 2 * g + i + 1)
                    for u, n in ((0, 4), (1, 3)):
                        actv(BC[:, i].rearrange("p (t u) e -> p t u e", u=2)[:, 0:n, u, :],
                             psum[(5, 1)[i] + 2 * u][:, 0:n * HD].rearrange("p (c e) -> p c e", c=n),
                             copy).then_inc(A("bc_ready"), 1)
                for i in range(2):
                    act.wait_ge(S("y_rwkv_done"), 2 * g + i + 1)
                    actv(rx[:, 2 * g + i, :], psum[2 + 4 * i][:], copy).then_inc(A("y_rwkv_out"), 1)
            for i in range(4):
                act.dma_start(x_res[:, 2 * i:2 * i + 2, :], ins["x"][:, 2 * i:2 * i + 2, :]).then_inc(S(f"x_loaded{i}"), 16)
            for f in range(NF):
                act.wait_ge(S("gn_cent_done"), NF + f + 1)
                actv(kx[:, f, :], psum[4 + f][:], copy).then_inc(A("gn_cent"), 1)
                actv(ax[:, f, :], psum[4 + f][:], square).then_inc(A("gn_sq"), 1)
            act.wait_ge(S("gn_var_done"), 1 + 1)
            actv(hsd[0:8, :], psum[0][0:8, :], sqrt, bias=C("eps64")[0:8], scale=1.0 / HD).then_inc(A("gn_sd"), 1)
            for c in range(KC):
                if c < 4:
                    actv(a_hi[:, c, :], rg[:, c, :], copy).then_inc(A("a_hi_ready"), 1)
                else:
                    act.wait_ge(S("y_ready"), c - 3)
                    actv(a_hi[:, c, :], kx[:, c - 4, :], copy).then_inc(A("a_hi_ready"), 1)
            act.wait_ge(S("a_lo_ready"), 2 * KC)
            act.dma_start(mem_in[:], ins["mem"]).then_inc(S("mem_loaded"), 16)

            act.wait_ge(S("mem_loaded"), 16)
            for kc in range(KC):
                actv(mem_hi[:, kc, :], mem_in[:, kc, :], copy, scale=V("norm_mem", kc)).then_inc(A("mem_hi_ready"), 1)
                actv(mem_sq[:, kc, :], mem_in[:, kc, :], square).then_inc(A("mem_sq_ready"), 1)

            def residual(s0, gain, k0):
                for n in range(KC):
                    split_hi(s0 + n + 2)
                    act.wait_ge(S("tile_taken"), s0 + n + 1)
                    if n >= 2:
                        act.wait_ge(S("sq_used"), k0 + n - 1)
                    actv(sqb[:, n % 2, :], x_res[:, n, :], square).then_inc(A("sq_ready"), 1)
                    actv(b_hi[:, n, :], x_res[:, n, :], copy, scale=V(gain, n)).then_inc(A("b_hi_ready"), 1)

            def xattn_act(h):
                for t in range(TT):
                    act.wait_ge(S("xmax_ready"), 2 * h + t // 2 + 1)
                    actv(prob[:, h % 2, t, :], psum[2 + t // 2][:, (t % 2) * MEM:(t % 2 + 1) * MEM], exp,
                         bias=neg_max[:, t:t + 1], accum_out=p_sum[:, t:t + 1]).then_inc(A("xexp_ready"), 1)
                for m in range(MEM // P):
                    act.wait_ge(S("xprob_t_done"), 2 * h + m + 1)
                    actv(prob_t[:, h % 2, m, :], psum[4 + m][:], copy).then_inc(A("xprob_t_ready"), 1)
                for d in range(2):
                    act.wait_ge(S("xo_done"), 2 * h + d + 1)
                    actv(a_hi[:, 2 * h + d, :], psum[6 + d][:], copy).then_inc(A("a_hi_ready"), 1)

            residual(S_WOUT, "norm_xattn", 0)
            act.wait_ge(S("ssq_done"), 1 + 1)
            actv(rstd[:], psum[7][:], sqrt, bias=C("eps6"), scale=1.0 / DM).then_inc(A("rms_ready"), 1)
            for s in range(S_MK, S_XQ):
                split_hi(s + 2)
                if s == S_MK:
                    act.wait_ge(S("mem_ssq_done"), 1)
                    actv(mem_rs[:], psum[6][:, 0:MEM], sqrt, bias=C("eps6"), scale=1.0 / DM).then_inc(A("mem_rms"), 1)
            for s in range(S_XQ, S_XO):
                split_hi(s + 2)
                if (s - S_XQ) % 2 == 1:
                    h = (s - S_XQ) // 2
                    if h >= 1:
                        xattn_act(h - 1)
            xattn_act(XH - 1)
            residual(S_XO, "norm_mlp", KC - 1)
            act.wait_ge(S("ssq_done"), 1 + 2)
            actv(rstd[:], psum[7][:], sqrt, bias=C("eps6"), scale=1.0 / DM).then_inc(A("rms_ready"), 1)
            for q in range(MLP_Q):
                for n in range(KC):
                    split_hi(S_MLP + 16 * q + n + 2)
                    act.wait_ge(S("m_ready"), KC * q + n + 1)
                    actv(m_hi[:, n, :], m_mid[:, n % 2, :], copy).then_inc(A("m_hi_ready"), 1)
                for n in range(KC):
                    split_hi(S_MLP + 16 * q + 8 + n + 2)
                    if q == MLP_Q - 1:
                        act.wait_ge(S("tile_taken"), S_MLP + 16 * q + 8 + n + 1)
                        if n == 0:
                            act.wait_ge(S("gain_12_ready"), 1)
                        if n >= 1:
                            act.wait_ge(S("sq_used"), 2 * (KC - 1) + n)
                        actv(sqb[:, 0, :], x_res[:, n, :], square).then_inc(A("sq_ready"), 1)
                        actv(sqb[:, 1, :], x_res[:, n, :], square, scale=V("norm_final", n)).then_inc(A("sq3_ready"), 1)
                        actv(a_hi[:, n, :], x_res[:, n, :], copy, scale=gain_12[:, n:n + 1]).then_inc(A("a_hi_ready"), 1)
            act.dma_start(ln[:], ins["ln"]).then_inc(S("tables_loaded"), 16)
            act.dma_start(spatial[:], ins["spatial"]).then_inc(S("tables_loaded"), 16)
            act.dma_start(axial[:], ins["axial"]).then_inc(S("tables_loaded"), 16)
            act.dma_start(b_row[:], ins["rows"][:, 512:1536]).then_inc(S("tables_loaded"), 16)
            act.wait_ge(S("ssq_done"), 3 + 1)
            actv(rstd[:], psum[7][:], sqrt, bias=C("eps6"), scale=1.0 / DM).then_inc(A("rms_ready"), 1)
            act.wait_ge(S("mid_var_ready"), 1)
            actv(rs_all[:], rs_tmp[:], sqrt, bias=C("eps6"), scale=1.0 / DM).then_inc(A("rms3_ready"), 1)
            for s in range(S_VIN, S_MERGE):
                split_hi(s + 2)
                if s == S_V2:
                    for t in range(TT):
                        act.wait_ge(S("tile_taken"), S_V2)
                        actv(vv[:, t, :], vv[:, t, :], ACT.Gelu_apprx_tanh).then_inc(A("gelu_ready"), 1)
                if s == S_K2 + 1:
                    act.wait_ge(S("ln_mv_ready"), TT)
                    actv(ln_rs, ln_mv.rearrange("p (t k) -> p t k", k=2)[:, :, 1], sqrt, bias=C("eps6")).then_inc(A("ln_sd"), 1)
                if S_K2 <= s < S_U:
                    f = (s - S_K2 + 4) % 5
                    act.wait_ge(S("tile_taken"), s + 1)
                    actv(sq10[:, f, :], qk2[:, f, :], square).then_inc(A("sq10_ready"), 1)
                if s == S_U + 1:
                    act.wait_ge(S("qk_ss_done"), 1)
                    actv(rn2[0:10, :], psum[2][0:10, :], sqrt, bias=C("eps6")[0:10], scale=1.0 / HD).then_inc(A("qk_sd"), 1)
                if S_GA <= s < S_GB:
                    f = s - S_GA
                    act.wait_ge(S("tile_taken"), S_U + f + 1)
                    actv(u2[:, f, :], u2[:, f, :], ACT.Gelu_apprx_tanh).then_inc(A("gelu_ready"), 1)
            for f in range(NF):
                act.wait_ge(S("tile_taken"), S_GA + f + 1)
                actv(ga[:, f, :], ga[:, f, :], ACT.Silu).then_inc(A("silu_ready"), 1)
            for f in range(NF):
                act.wait_ge(S("tile_taken"), S_GB + f + 1)
                actv(gb[:, f, :], gb[:, f, :], ACT.Silu).then_inc(A("silu_ready"), 1)
            for f in range(NF):
                act.wait_ge(S("gm_ready"), f + 1)
                actv(b_hi[:, NF + f, :], tmp2[:, f % 2, :], copy).then_inc(A("branch_hi"), 1)

            def attn_exp(i):
                for k in range(2):
                    act.wait_ge(S("max2_ready"), 2 * i + k + 1)
                    if i >= 2 and k == 0:
                        act.wait_ge(S("p2_t_done"), i - 1)
                    actv(p2[:, i % 2, k, :], psum[2 + k][:], exp, bias=max2[:, k:k + 1],
                         accum_out=sum2[:, k:k + 1]).then_inc(A("exp2_ready"), 1)

            def attn_t(i):
                for k in range(2):
                    act.wait_ge(S("p2_t_done"), i + 1)
                    if i % 2 == 0 and i >= 2 and k == 0:
                        act.wait_ge(S("o2_done"), i // 2)
                    actv(p2_t[:, 2 * k:2 * k + 2, (i % 2) * 256:(i % 2) * 256 + 256],
                         psum[4 + k][:].rearrange("p (c t) -> p c t", c=2), copy).then_inc(A("p2_t_ready"), 1)

            for i in range(2 * QH + 1):
                if i < 2 * QH:
                    attn_exp(i)
                if i >= 1:
                    attn_t(i - 1)
            for f in range(NF):
                act.wait_ge(S("oa_ready"), f + 1)
                actv(b_hi[:, f, :], ga[:, f, :], copy).then_inc(A("branch_hi"), 1)
            for n in range(KC):
                for k in range(3):
                    s = S_MERGE + 3 * n + k
                    split_hi(s + 2)
                    if k < 2:
                        act.wait_ge(S("tile_taken"), s + 1)
                        actv(gate[:, 2 * (n % 2) + k, :], gate[:, 2 * (n % 2) + k, :], sigmoid,
                             bias=V("b_merge", KC * k + n)).then_inc(A("gate_ready"), 1)
                act.wait_ge(S("y_mid_ready"), n + 1)
                actv(y_hi[:, n, :], y_mid[:, 0, :], copy).then_inc(A("ym_hi"), 1)
            for n in range(KC):
                split_hi(S_OUT2 + n + 2)
                act.wait_ge(S("tile_taken"), S_OUT2 + n + 1)
                if n >= 2:
                    act.wait_ge(S("sq_used"), 3 * (KC - 1) + n - 1)
                actv(sqb[:, n % 2, :], x_res[:, n, :], square).then_inc(A("sq_ready"), 1)
            act.wait_ge(S("ssq_done"), 4 + 1)
            actv(rstd[:], psum[7][:], sqrt, bias=C("eps6"), scale=1.0 / DM).then_inc(A("rms_ready"), 1)

        @block.vector
        def _(dve):
            marks, last = {}, []

            def D(name):
                marks[name] = marks.get(name, 0) + 1
                last[:] = [name, marks[name]]
                return S(name)

            def hold():
                if last:
                    dve.wait_ge(S(last[0]), last[1])

            def step(ins):
                return ins.then_inc(D("dve_step"), 1)

            def tt(o, a, b, op):
                hold()
                return nc.vector.tensor_tensor(o, a, b, op)

            def ts(o, a, s1, s2, op0, op1=ALU.bypass):
                hold()
                return nc.vector.tensor_scalar(o, a, s1, s2, op0, op1)

            def stt(o, a, s1, b, op0, op1):
                hold()
                return nc.vector.scalar_tensor_tensor(out=o, in0=a, scalar=s1, in1=b, op0=op0, op1=op1)

            def cp(o, a):
                hold()
                return nc.vector.tensor_copy(o, a)

            def recip(o, a):
                hold()
                return nc.vector.reciprocal(o, a)

            c1, two_pi = 6.28125, 6.283185307179586
            magic = 1.5 * 2.0 ** 23
            step(nc.vector.memset(shift[:, :, 0:1], 0.0))
            step(nc.vector.memset(sc[:, :, NCH - 1:NCH], 1.0))
            dve.wait_ge(S("pos_loaded"), 16)
            dve.wait_ge(S("consts_loaded"), 16)
            step(cp(trig[:, 0, :], pos[:]))
            step(ts(trig[:, 1, :], trig[:, 0, :], C("inv_freq"), None, ALU.mult))
            step(ts(trig[:, 2, :], trig[:, 1, :], 1.0 / two_pi, magic, ALU.mult, ALU.add))
            step(ts(trig[:, 3, :], trig[:, 2, :], -magic, None, ALU.add))
            step(stt(trig[:, 1, :], trig[:, 3, :], -c1, trig[:, 1, :], ALU.mult, ALU.add))
            step(stt(trig[:, 1, :], trig[:, 3, :], c1 - two_pi, trig[:, 1, :], ALU.mult, ALU.add))
            ts(trig[:, 0, :], trig[:, 1, :], -3.1415925, 3.1415925, ALU.max, ALU.min).then_inc(D("angle_ready"), 1)
            dve.wait_ge(S("sines_ready"), 1)
            step(tt(trig[:, 2, :], trig[:, 1, :], trig[:, 1, :], ALU.mult))
            ts(cos_r[:], trig[:, 2, :], -2.0, 1.0, ALU.mult, ALU.add).then_inc(D("dve_step"), 1)
            dve.wait_ge(S("params_loaded"), 16)
            ka = par["k_a"][0]
            ts(one_ka, params[:, ka:ka + 4], -1.0, 1.0, ALU.mult, ALU.add).then_inc(D("dve_step"), 1)

            for kc in range(KC):
                dve.wait_ge(S("a_hi_ready"), kc + 1)
                stt(a_lo[:, kc, :], x_in[:, kc, :], V("norm_mix", kc), a_hi[:, kc, :].bitcast(F32),
                    ALU.mult, ALU.subtract).then_inc(D("a_lo_ready"), 1)
            dve.wait_ge(S("rms_ready"), 1)
            recip(rstd[:], rstd[:]).then_inc(D("rstd_ready"), 1)
            dve.wait_ge(S("rstd_ready"), 1)

            def rope(j):
                dve.wait_ge(S("rot_done"), j + 1)
                if j == 0:
                    dve.wait_ge(S("xn_sq"), KC)
                dve.wait_ge(S("tile_taken"), j + 1)
                step(tt(tmp[:, 0, :], psum[2 + j % 2][:], sin_r[:], ALU.mult))
                step(tt(qk[:, j, :], qk[:, j, :], cos_r[:], ALU.mult))
                tt(qk[:, j, :], qk[:, j, :], tmp[:, 0, :], ALU.add).then_inc(D("rope_done"), 1)

            mixed = [(low, 0), (low, 1), (low, 2)] + [(d, f) for d in (kx, rx, vx) for f in range(NF)]
            for s in range(S_WOUT):
                dve.wait_ge(S("slab_done"), s + 1)
                bank = psum[s % 2]
                if s < S_RV:
                    tt(qk[:, s, :], bank[:], rstd[:], ALU.mult).then_inc(D("tile_taken"), 1)
                    if s > 0:
                        rope(s - 1)
                elif s < S_RG:
                    if s == S_RV:
                        rope(7)
                        dve.wait_ge(S("column_done"), 1)
                        cp(r_tok[:], psum[4][:, 0:8]).then_inc(D("r_tok_ready"), 1)
                        dve.wait_ge(S("r_tok_ready"), 1)
                    tt(v_ret[:, :, (s - S_RV) * P:(s - S_RV + 1) * P], bank[:].rearrange("p (t n) -> p t n", t=TT),
                       r_tok.rearrange("p (t k) -> p t k", k=2)[:, :, 0:1].broadcast_to([P, TT, P]), ALU.mult).then_inc(D("tile_taken"), 1)
                elif s < S_WA:
                    tt(rg[:, s - S_RG, :], bank[:], rstd[:], ALU.mult).then_inc(D("tile_taken"), 1)
                else:
                    j = s - S_WA
                    cur, prev = shift[:, j % 2, 1:T + 1], shift[:, j % 2, 0:T]
                    tt(cur, bank[:], rstd[:], ALU.mult).then_inc(D("tile_taken"), 1)
                    dve.wait_ge(S("tile_taken"), s + 1)
                    step(tt(tmp[:, 0, :], prev, cur, ALU.subtract))
                    dst, f = mixed[j]
                    stt(dst[:, f, :], tmp[:, 0, :], V("mu", j), cur, ALU.mult, ALU.add).then_inc(
                        S("low_ready" if j < 3 else "mix_ready"), 1)

            dve.wait_ge(S("slab_done"), S_WOUT)
            dve.wait_ge(S("mix_ready"), 12)
            for f in range(NF):
                ts(kk[:, f, :], kx[:, f, :], V("k_k", f), None, ALU.mult).then_inc(D("kk0_ready"), 1)
            dve.wait_ge(S("kn_ready"), 1)
            step(ts(rn[0:8, :], rn[0:8, :], 1e-12, None, ALU.max))
            recip(rn[0:8, :], rn[0:8, :]).then_inc(D("krn_ready"), 1)

            def prep(f):
                dve.wait_ge(S("kk_done"), f + 1)
                step(tt(kk[:, f, :], kk[:, f, :], psum[5][:], ALU.mult))
                dve.wait_ge(S("lora_ready"), TT + f + 1)
                step(ts(pt[:, 0, :], ax[:, f, :], V("k_a", f), one_ka[:, f:f + 1], ALU.mult, ALU.add))
                step(tt(ax[:, f, :], ax[:, f, :], kk[:, f, :], ALU.mult))
                step(tt(kx[:, f, :], kx[:, f, :], pt[:, 0, :], ALU.mult))
                stt(pt[:, 1, :], rx[:, f, :], V("r_k", f), kx[:, f, :], ALU.mult, ALU.mult).then_inc(D("rk_ready"), 1)
                dve.wait_ge(S("exps_ready"), f + 1)
                step(recip(sr[:, f, 0:NCH - 1],
                                               e_exc[:, f, :].rearrange("p (c t) -> p c t", c=NCH)[:, 1:NCH, 0]))
                step(tt(ax[:, f, :], ax[:, f, :], e_neg[:, f, :], ALU.mult))
                step(stt(kk[:, f, :], kk[:, f, :], -1.0, e_exc[:, f, :], ALU.mult, ALU.mult))
                step(tt(sc[:, f, 0:NCH - 1], e_inc[:, f, :].rearrange("p (c t) -> p c t", c=NCH)[:, 0:NCH - 1, CH - 1],
                             sr[:, f, 0:NCH - 1], ALU.mult))
                dve.wait_ge(S("rk_ready"), f + 1)
                step(tt(kx[:, f, :], kx[:, f, :], e_neg[:, f, :], ALU.mult))
                step(tt(rx[:, f, :], rx[:, f, :], e_inc[:, f, :], ALU.mult))
                scale = sc[:, f, :].unsqueeze(2).broadcast_to([P, NCH, CH])
                if f == 0:
                    dve.wait_ge(S("lora_ready"), TT + NF + NF)
                step(tt(bh[:, f, :].rearrange("p (c t) -> p c t", c=NCH), ax[:, f, :].rearrange("p (c t) -> p c t", c=NCH),
                        scale, ALU.mult))
                step(tt(kh[:, f, :].rearrange("p (c t) -> p c t", c=NCH), kx[:, f, :].rearrange("p (c t) -> p c t", c=NCH),
                        scale, ALU.mult))
                dve.wait_ge(S("bonus_done"), f + 1)
                tt(bon[:, f, :], psum[5][:], vx[:, f, :], ALU.mult).then_inc(D("prep_ready"), 1)

            dve.wait_ge(S("decay_loaded"), 16)
            for h in range(RH):
                off = 0
                dve.wait_ge(S("s_ret_done"), h + 1)
                if h >= 2:
                    dve.wait_ge(S("y_ret_step"), h - 1)
                for j in range(TT):
                    w = T - P * j
                    src = psum[(2, 3, 4, 3)[j]][:, (384 if j == 3 else 0):(384 if j == 3 else 0) + w]
                    ins_ = tt(s_ret[:, h % 2, off:off + w], src, decay[:, h, 0:w], ALU.mult)
                    if j == TT - 1:
                        ins_.then_inc(D("s_ret_ready"), 1)
                    else:
                        step(ins_)
                    off += w
                if h % 2 == 1:
                    prep(h // 2)
            dve.wait_ge(S("gn_sd"), 1)
            recip(grn[0:8, :], gsd[0:8, :]).then_inc(D("gn_rn"), 1)
            for f in range(NF):
                dve.wait_ge(S("gn_spread_done"), f + 1)
                dve.wait_ge(S("gn_cent"), f + 1)
                step(tt(qk[:, 4 + f, :], qk[:, 4 + f, :], psum[2 + f][:], ALU.mult))
                step(ts(qk[:, 4 + f, :], qk[:, 4 + f, :], V("ret_gn_w", f), V("ret_gn_b", f), ALU.mult, ALU.add))
                dve.wait_ge(S("silu_ready"), f + 1)
                tt(rg[:, f, :], rg[:, f, :], qk[:, 4 + f, :], ALU.mult).then_inc(D("ret_ready"), 1)

            strict = C("mask_strict").unsqueeze(1).broadcast_to([P, TT, P])
            inc = C("mask_inc").unsqueeze(1).broadcast_to([P, TT, P])
            pairm = C("mask_pair").unsqueeze(1).broadcast_to([P, TT, P])
            ident = C("ident").unsqueeze(1).broadcast_to([P, TT, P])

            def t4(a):
                return a.rearrange("p (t c) -> p t c", t=TT)

            for g in range(2):
                for j in range(4):
                    n = 4 * g + j
                    if g == 0 and j == 0:
                        dve.wait_ge(S("tok_done"), 16)
                        dve.wait_ge(S("ret_ready"), NF)
                    if j == 0 and g == 1:
                        dve.wait_ge(S("y_rwkv_done"), 2)
                    dve.wait_ge(S("ab_done"), n + 1)
                    tt(t4(AB[:, j, :]), t4(psum[2 * j][:]), strict, ALU.mult).then_inc(D("ab_ready"), 1)
                    dve.wait_ge(S("ak_done"), n + 1)
                    tt(t4(PX[:, j, :]), t4(psum[2 * j + 1][:]), strict, ALU.mult).then_inc(D("ak_ready"), 1)
                    dve.wait_ge(S("ab_ready"), n + 1)
                    step(tt(t4(XT[:, j, :]), t4(AB[:, j, :]), pairm, ALU.mult))
                    dve.wait_ge(S("rb_done"), n + 1)
                    tt(t4(RB[:, j, :]), t4(psum[2 * j][:]), inc, ALU.mult).then_inc(D("rb_ready"), 1)
                    tt(t4(XT[:, j, :]), t4(XT[:, j, :]), ident, ALU.add).then_inc(D("xt0_ready"), 1)
                    dve.wait_ge(S("rk_mm_done"), n + 1)
                    tt(t4(RK[:, j, :]), t4(psum[2 * j + 1][:]), inc, ALU.mult).then_inc(D("rkm_ready"), 1)
                for lv in range(5):
                    mask = C("mask_level", lv * P, P).unsqueeze(1).broadcast_to([P, TT, P])
                    for j in range(4):
                        n = 4 * (5 * g + lv) + j
                        dve.wait_ge(S("nx_done"), n + 1)
                        if lv == 0:
                            dve.wait_ge(S("u_done"), 4 * g + j + 1)
                        tt(t4(PX[:, j, :]), t4(psum[2 * j][:]), mask, ALU.mult).then_inc(D("px_ready"), 1)
                    for j in range(4):
                        n = 4 * (5 * g + lv) + j
                        dst = XT if lv == 4 else X
                        dve.wait_ge(S("xp_done"), n + 1)
                        if lv == 0:
                            dve.wait_ge(S("x0_ready"), 4 * g + j + 1)
                        else:
                            dve.wait_ge(S("xn_ready"), n - 3)
                        if lv == 4:
                            dve.wait_ge(S("xt_ready"), 4 * (4 * g + 3) + j + 1)
                        tt(dst[:, j, :], dst[:, j, :], psum[2 * j + 1][:], ALU.add).then_inc(D("xn_ready"), 1)
                for i in range(2):
                    f = 2 * g + i
                    step(tt(AT[:, i], C("ident2").unsqueeze(1).broadcast_to([P, NCH, HD]),
                                sc[:, f, :].unsqueeze(2).broadcast_to([P, NCH, HD]), ALU.mult))
                    dve.wait_ge(S("qt_done"), f + 1)
                    tt(QT[:, i, :], psum[1 + 2 * i][:], rx[:, f, :], ALU.add).then_inc(D("qt_ready"), 1)
                    dve.wait_ge(S("at_done"), f + 1)
                    for u, n in ((0, 4), (1, 3)):
                        half = AT[:, i].rearrange("p (t u) e -> p t u e", u=2)[:, 0:n, u, :]
                        tt(half, half, psum[(4, 0)[i] + 2 * u][:, 0:n * HD].rearrange("p (c e) -> p c e", c=n),
                           ALU.add).then_inc(D("at_ready"), 1)
                dve.wait_ge(S("bc_ready"), 4 * g + 4)
                cp(ST[:, 1], BC[:, :, 0, :]).then_inc(D("state_ready"), 1)
                for c in range(1, 7):
                    dve.wait_ge(S("state_done"), 6 * g + c)
                    tt(ST[:, c + 1], psum[0][:, 0:128].rearrange("p (i e) -> p i e", i=2), BC[:, :, c, :],
                       ALU.add).then_inc(D("state_ready"), 1)
            dve.wait_ge(S("gn_sd"), 1 + 1)
            recip(hrn[0:8, :], hsd[0:8, :]).then_inc(D("gn_rn"), 1)
            for f in range(NF):
                dve.wait_ge(S("gn_spread_done"), NF + f + 1)
                dve.wait_ge(S("gn_cent"), NF + f + 1)
                step(tt(kx[:, f, :], kx[:, f, :], psum[4 + f][:], ALU.mult))
                step(ts(kx[:, f, :], kx[:, f, :], V("gn_w", f), V("gn_b", f), ALU.mult, ALU.add))
                dve.wait_ge(S("prep_ready"), NF)
                step(tt(kx[:, f, :], kx[:, f, :], bon[:, f, :], ALU.add))
                tt(kx[:, f, :], kx[:, f, :], gx[:, f, :], ALU.mult).then_inc(D("y_ready"), 1)
            for c in range(KC):
                dve.wait_ge(S("a_hi_ready"), KC + c + 1)
                y = rg[:, c, :] if c < 4 else kx[:, c - 4, :]
                tt(a_lo[:, c, :], y, a_hi[:, c, :].bitcast(F32), ALU.subtract).then_inc(D("a_lo_ready"), 1)
            ts(gain_12, params[:, par["norm_final"][0]:par["norm_final"][1]], 1.0, None, ALU.mult).then_inc(D("dve_step"), 1)
            tt(gain_12, gain_12, params[:, par["norm_gain_2"][0]:par["norm_gain_2"][1]], ALU.mult).then_inc(D("gain_12_ready"), 1)
            dve.wait_ge(S("mem_loaded"), 16)
            for kc in range(KC):
                dve.wait_ge(S("mem_hi_ready"), kc + 1)
                stt(mem_lo[:, kc, :], mem_in[:, kc, :], V("norm_mem", kc), mem_hi[:, kc, :].bitcast(F32),
                    ALU.mult, ALU.subtract).then_inc(D("mem_lo_ready"), 1)

            def residual(s0, gain, k):
                for n in range(KC):
                    dve.wait_ge(S("slab_done"), s0 + n + 1)
                    if k == 0:
                        dve.wait_ge(S(f"x_loaded{n // 2}"), 32)
                    tt(x_res[:, n, :], psum[(s0 + n) % 2][:], x_res[:, n, :], ALU.add).then_inc(D("tile_taken"), 1)
                    dve.wait_ge(S("b_hi_ready"), KC * k + n + 1)
                    stt(b_lo[:, n, :], x_res[:, n, :], V(gain, n), b_hi[:, n, :].bitcast(F32),
                        ALU.mult, ALU.subtract).then_inc(D("b_lo_ready"), 1)

            residual(S_WOUT, "norm_xattn", 0)
            dve.wait_ge(S("rms_ready"), 1 + 1)
            recip(rstd[:], rstd[:]).then_inc(D("rstd_ready"), 1)
            for s in range(S_MK, S_XQ):
                dve.wait_ge(S("slab_done"), s + 1)
                if s == S_MK:
                    dve.wait_ge(S("mem_rms"), 1)
                    recip(mem_rs[:], mem_rs[:]).then_inc(D("mem_rstd"), 1)
                if s < S_MV:
                    tt(mem_k[:, s - S_MK, :], psum[s % 2][:, 0:MEM], mem_rs[:], ALU.mult).then_inc(D("tile_taken"), 1)
                else:
                    if s == S_MV:
                        dve.wait_ge(S("column_done"), 1 + 1)
                        cp(m_tok, psum[5][:, 0:4]).then_inc(D("m_tok_ready"), 1)
                    n = s - S_MV
                    tt(mem_v[:, :, n * P:(n + 1) * P], psum[s % 2][:, 0:MEM].rearrange("p (m n) -> p m n", m=2),
                       m_tok.rearrange("p (m k) -> p m k", k=2)[:, :, 0:1].broadcast_to([P, 2, P]), ALU.mult).then_inc(D("tile_taken"), 1)

            def xattn_dve(h):
                for k in range(2):
                    dve.wait_ge(S("xs_done"), 2 * h + k + 1)
                    hold()
                    nc.vector.tensor_reduce(neg_max[:, 2 * k:2 * k + 2], psum[2 + k][:].rearrange("p (t m) -> p t m", t=2),
                                            axis=AX.X, op=ALU.max, negate=True).then_inc(D("xmax_ready"), 1)
                dve.wait_ge(S("xexp_ready"), TT * (h + 1))
                recip(p_inv, p_sum).then_inc(D("dve_step"), 1)
                tt(prob[:, h % 2], prob[:, h % 2], p_inv.unsqueeze(2).broadcast_to([P, TT, MEM]), ALU.mult).then_inc(D("xprob_ready"), 1)
                for d in range(2):
                    dve.wait_ge(S("a_hi_ready"), 2 * KC + 2 * h + d + 1)
                    tt(a_lo[:, 2 * h + d, :], psum[6 + d][:], a_hi[:, 2 * h + d, :].bitcast(F32), ALU.subtract).then_inc(D("a_lo_ready"), 1)

            for s in range(S_XQ, S_XO):
                dve.wait_ge(S("slab_done"), s + 1)
                stt(xq[:, s - S_XQ, :], psum[s % 2][:], 256.0 ** -0.5, rstd[:], ALU.mult, ALU.mult).then_inc(D("tile_taken"), 1)
                if (s - S_XQ) % 2 == 1 and s > S_XQ + 1:
                    xattn_dve((s - S_XQ) // 2 - 1)
            xattn_dve(XH - 1)
            residual(S_XO, "norm_mlp", 1)
            dve.wait_ge(S("rms_ready"), 1 + 2)
            recip(rstd[:], rstd[:]).then_inc(D("rstd_ready"), 1)

            for q in range(MLP_Q):
                for n in range(KC):
                    s = S_MLP + 16 * q + n
                    m = m_mid[:, n % 2, :]
                    dve.wait_ge(S("slab_done"), s + 1)
                    if KC * q + n >= 2:
                        dve.wait_ge(S("m_hi_ready"), KC * q + n - 1)
                    tt(m, psum[s % 2][:], rstd[:], ALU.mult).then_inc(D("tile_taken"), 1)
                    stt(m, m, 0.0, m, ALU.max, ALU.mult).then_inc(D("m_ready"), 1)
                    dve.wait_ge(S("m_hi_ready"), KC * q + n + 1)
                    tt(m_lo[:, n, :], m, m_hi[:, n, :].bitcast(F32), ALU.subtract).then_inc(D("m_lo_ready"), 1)
                for n in range(KC):
                    s = S_MLP + 16 * q + 8 + n
                    dve.wait_ge(S("slab_done"), s + 1)
                    tt(x_res[:, n, :], psum[s % 2][:], x_res[:, n, :], ALU.add).then_inc(D("tile_taken"), 1)
                    if q == MLP_Q - 1:
                        dve.wait_ge(S("a_hi_ready"), 3 * KC + n + 1)
                        stt(a_lo[:, n, :], x_res[:, n, :], gain_12[:, n:n + 1], a_hi[:, n, :].bitcast(F32),
                            ALU.mult, ALU.subtract).then_inc(D("a_lo_ready"), 1)
            dve.wait_ge(S("rms_ready"), 1 + 3)
            recip(rstd[:], rstd[:]).then_inc(D("rstd_ready"), 1)
            step(tt(rs_tmp[:], rstd[:], rstd[:], ALU.mult))
            dve.wait_ge(S("ssq_done"), 3 + 1)
            tt(rs_tmp[:], psum[6][:], rs_tmp[:], ALU.mult).then_inc(D("mid_var_ready"), 1)
            dve.wait_ge(S("rms3_ready"), 1)
            step(recip(rs_all[:], rs_all[:]))
            tt(rs_all[:], rs_all[:], rstd[:], ALU.mult).then_inc(D("rs_all_ready"), 1)
            dve.wait_ge(S("column_done"), 2 + 1)
            step(cp(r2_tok, psum[5][:, 0:8]))
            by_tok = r2_tok.rearrange("p (t k) -> p t k", k=2)[:, :, 0:1].broadcast_to([P, TT, P])
            for s in range(S_VIN, S_MERGE):
                dve.wait_ge(S("slab_done"), s + 1)
                bank = psum[s % 2]
                if s < S_V2:
                    n = s - S_VIN
                    tt(vv[:, :, n * P:(n + 1) * P], bank[:].rearrange("p (t n) -> p t n", t=TT), by_tok, ALU.mult).then_inc(D("tile_taken"), 1)
                elif s == S_V2:
                    tt(v2[:], bank[:].rearrange("p (t n) -> p t n", t=TT), by_tok, ALU.mult).then_inc(D("tile_taken"), 1)
                    for n in range(KC):
                        step(stt(x_res[:, n, :], x_res[:, n, :], V("norm_final", n), rstd[:], ALU.mult, ALU.mult))
                elif s < S_U:
                    tt(qk2[:, (s - S_K2 + 4) % 5, :], bank[:], rs_all[:], ALU.mult).then_inc(D("tile_taken"), 1)
                    if s == S_K2:
                        for t in range(TT):
                            dve.wait_ge(S("gelu_ready"), t + 1)
                            hold()
                            step(nc.vector.bn_stats(ln_stats[:, 6 * t:6 * t + 6], vv[:, t, :]))
                            hold()
                            nc.vector.bn_aggr(ln_mv[:, 2 * t:2 * t + 2], ln_stats[:, 6 * t:6 * t + 6]).then_inc(D("ln_mv_ready"), 1)
                    if s == S_K2 + 2:
                        dve.wait_ge(S("ln_sd"), 1)
                        step(recip(ln_rs, ln_rs))
                        dve.wait_ge(S("tables_loaded"), 64)
                        for t in range(TT):
                            step(ts(vv[:, t, :], vv[:, t, :], ln_mv[:, 2 * t:2 * t + 1], ln_rs[:, t:t + 1], ALU.subtract, ALU.mult))
                            step(tt(vv[:, t, :], vv[:, t, :], ln[:, 0, :], ALU.mult))
                            tt(vv[:, t, :], vv[:, t, :], ln[:, 1, :], ALU.add).then_inc(D("vv_ready"), 1)
                elif s < S_GA:
                    tt(u2[:, s - S_U, :], bank[:], rs_all[:], ALU.mult).then_inc(D("tile_taken"), 1)
                    if s == S_U + 1:
                        dve.wait_ge(S("sq10_ready"), 5)
                        for f in range(5):
                            ts(qk2[:, f, :], qk2[:, f, :], V("k_gain" if f == 4 else "q_gain"), None, ALU.mult).then_inc(D("qg_ready"), 1)
                    if s == S_U + 3:
                        dve.wait_ge(S("qk_sd"), 1)
                        recip(rn2[0:10, :], rn2[0:10, :]).then_inc(D("qk_rn"), 1)
                elif s < S_GB:
                    tt(ga[:, s - S_GA, :], bank[:], rs_all[:], ALU.mult).then_inc(D("tile_taken"), 1)
                    for f in ((0, 1), (2,), (3,), (4,))[s - S_GA]:
                        dve.wait_ge(S("rot_done"), 8 + f + 1)
                        step(tt(tmp2[:, 0, :], psum[3 + f % 2][:], axial[:, 1, :], ALU.mult))
                        step(tt(qk2[:, f, :], qk2[:, f, :], axial[:, 0, :], ALU.mult))
                        tt(qk2[:, f, :], qk2[:, f, :], tmp2[:, 0, :], ALU.add).then_inc(D("dve_step"), 1)
                        dve.wait_ge(S("spread2_done"), f + 1)
                        tt(qk2[:, f, :], qk2[:, f, :], psum[5 + f % 2][:], ALU.mult).then_inc(D("qk2_ready"), 1)
                else:
                    tt(gb[:, s - S_GB, :], bank[:], rs_all[:], ALU.mult).then_inc(D("tile_taken"), 1)
            for f in range(NF):
                dve.wait_ge(S("gelu_ready"), TT + f + 1)
                dve.wait_ge(S("silu_ready"), 2 * NF + f + 1)
                step(tt(u2[:, f, :], u2[:, f, :], gb[:, f, :], ALU.mult))
                dve.wait_ge(S("vmix_done"), f + 1)
                if f >= 2:
                    dve.wait_ge(S("branch_hi"), f - 1)
                tt(tmp2[:, f % 2, :], psum[2 + f % 2][:], u2[:, f, :], ALU.mult).then_inc(D("gm_ready"), 1)
                dve.wait_ge(S("branch_hi"), f + 1)
                tt(b_lo[:, NF + f, :], tmp2[:, f % 2, :], b_hi[:, NF + f, :].bitcast(F32), ALU.subtract).then_inc(D("branch_lo"), 1)

            def attn_out(f):
                dve.wait_ge(S("o2_done"), 2 * f + 2)
                dve.wait_ge(S("silu_ready"), NF + f + 1)
                tt(ga[:, f, :], psum[6 + f % 2][:], ga[:, f, :], ALU.mult).then_inc(D("oa_ready"), 1)

            for i in range(2 * QH):
                for k in range(2):
                    dve.wait_ge(S("s2_done"), 2 * i + k + 1)
                    hold()
                    nc.vector.tensor_reduce(max2[:, k:k + 1], psum[2 + k][:], axis=AX.X, op=ALU.max, negate=True).then_inc(D("max2_ready"), 1)
                dve.wait_ge(S("exp2_ready"), 2 * i + 2)
                step(recip(inv2, sum2))
                for k in range(2):
                    ts(p2[:, i % 2, k, :], p2[:, i % 2, k, :], inv2[:, k:k + 1], None, ALU.mult).then_inc(D("p2_ready"), 1)
                if i % 4 == 1 and i > 1:
                    attn_out(i // 4 - 1)
            attn_out(NF - 1)
            for f in range(NF):
                dve.wait_ge(S("branch_hi"), NF + f + 1)
                tt(b_lo[:, f, :], ga[:, f, :], b_hi[:, f, :].bitcast(F32), ALU.subtract).then_inc(D("branch_lo"), 1)
            for n in range(KC):
                s = S_MERGE + 3 * n
                for k in range(2):
                    dve.wait_ge(S("slab_done"), s + k + 1)
                    tt(gate[:, 2 * (n % 2) + k, :], psum[(s + k) % 2][:], rs_all[:], ALU.mult).then_inc(D("tile_taken"), 1)
                dve.wait_ge(S("gate_ready"), 2 * n + 2)
                dve.wait_ge(S("slab_done"), s + 3)
                if n >= 1:
                    dve.wait_ge(S("ym_hi"), n)
                step(tt(y_mid[:, 0, :], psum[(s + 2) % 2][:], gate[:, 2 * (n % 2), :], ALU.mult))
                tt(y_mid[:, 1, :], psum[2 + (s + 2) % 2][:], gate[:, 2 * (n % 2) + 1, :], ALU.mult).then_inc(D("tile_taken"), 1)
                tt(y_mid[:, 0, :], y_mid[:, 0, :], y_mid[:, 1, :], ALU.add).then_inc(D("y_mid_ready"), 1)
                dve.wait_ge(S("ym_hi"), n + 1)
                tt(y_lo[:, n, :], y_mid[:, 0, :], y_hi[:, n, :].bitcast(F32), ALU.subtract).then_inc(D("ym_lo"), 1)
            for n in range(KC):
                s = S_OUT2 + n
                dve.wait_ge(S("slab_done"), s + 1)
                tt(x_res[:, n, :], psum[s % 2][:], x_res[:, n, :], ALU.add).then_inc(D("tile_taken"), 1)
            dve.wait_ge(S("rms_ready"), 1 + 4)
            recip(rstd[:], rstd[:]).then_inc(D("rstd_ready"), 1)
            for n in range(KC):
                if n >= 2:
                    dve.wait_ge(S(f"out_stored{n % 2}"), 16 * (n // 2))
                stt(o_fin[:, n % 2, :], x_res[:, n, :], V("final_gain", n), rstd[:], ALU.mult, ALU.mult).then_inc(D("out_ready"), 1)

        @block.tensor
        def _(pe):
            mm = nc.tensor.matmul

            def slab(s, hi, lo, ready=None, k=0):
                pe.wait_ge(S("w_lo_ready"), s + 1)
                if s >= 2:
                    pe.wait_ge(S("tile_taken"), s - 1)
                for kc in range(KC):
                    if ready:
                        pe.wait_ge(S(ready), k + kc + 1)
                    w = slice(kc * P, (kc + 1) * P)
                    o = psum[s % 2][:, 0:hi.shape[2]]
                    mm(o, w_hi[:, s % 2, w], hi[:, kc, :], start=kc == 0, stop=False)
                    mm(o, w_hi[:, s % 2, w], lo[:, kc, :], start=False, stop=False)
                    last = mm(o, w_lo[:, s % 2, w], hi[:, kc, :], start=False, stop=kc == KC - 1)
                last.then_inc(S("slab_done"), 1)

            def slab_tok(s, hi, lo):
                pe.wait_ge(S("w_lo_ready"), s + 1)
                pe.wait_ge(S("tile_taken"), s - 1)
                for t in range(hi.shape[2] // P):
                    o = psum[s % 2][:, t * P:(t + 1) * P]
                    c = slice(t * P, (t + 1) * P)
                    for kc in range(KC):
                        w = slice(kc * P, (kc + 1) * P)
                        mm(o, hi[:, kc, c], w_hi[:, s % 2, w], start=kc == 0, stop=False)
                        mm(o, lo[:, kc, c], w_hi[:, s % 2, w], start=False, stop=False)
                        last = mm(o, hi[:, kc, c], w_lo[:, s % 2, w], start=False, stop=kc == KC - 1)
                last.then_inc(S("slab_done"), 1)

            def rot(j):
                pe.wait_ge(S("tile_taken"), j + 1)
                if j >= 2:
                    pe.wait_ge(S("rope_done"), j - 1)
                mm(psum[2 + j % 2][:], C("swap_ret"), qk[:, j, :], start=True, stop=True).then_inc(S("rot_done"), 1)

            pe.wait_ge(S("consts_loaded"), 16)
            for s in range(S_WOUT):
                if S_RV <= s < S_RG:
                    slab_tok(s, a_hi, a_lo)
                else:
                    slab(s, a_hi, a_lo, "a_lo_ready" if s == 0 else None)
                if s == 0:
                    for kc in range(KC):
                        pe.wait_ge(S("xn_sq"), kc + 1)
                        last = mm(psum[7][:], C("ones"), sq_in[:, kc, :], start=kc == 0, stop=kc == KC - 1)
                    last.then_inc(S("ssq_done"), 1)
                if 1 <= s <= S_RV:
                    rot(s - 1)
                if s == 4:
                    pe.wait_ge(S("rstd_ready"), 1)
                    for t in range(TT):
                        last = mm(psum[4][:, 2 * t:2 * t + 2], rstd[0:1, t * P:(t + 1) * P], C("ones", 0, 2)[0:1, :],
                                  start=True, stop=True)
                    last.then_inc(S("column_done"), 1)
                if s == S_K + 1:
                    pe.wait_ge(S("low_act"), 3)
                    pe.wait_ge(S("lora_loaded"), 48)
                    pe.wait_ge(S("rope_done"), 8)
                    for t in range(TT):
                        if t >= 2:
                            pe.wait_ge(S("lora_ready"), t - 1)
                        mm(psum[2 + t % 2][:], low[0:HD, 0, t * P:(t + 1) * P], lora[0:HD, :], start=True, stop=False)
                        mm(psum[2 + t % 2][:], C("ones")[0:1, :], w0_row[0:1, :], start=False, stop=True).then_inc(S("lora_done"), 1)
                if s == S_K + 2:
                    pe.wait_ge(S("r_tok_ready"), 1)
                    for f in range(NF):
                        if f >= 2:
                            pe.wait_ge(S("lora_ready"), TT + f - 1)
                        mm(psum[4 + f % 2][:], lora[HD:P, f * P:(f + 1) * P], low[HD:P, 0, :], start=True, stop=True).then_inc(S("lora_done"), 1)
                if s == S_K + 3:
                    for f in range(NF):
                        if f >= 2:
                            pe.wait_ge(S("lora_ready"), TT + NF + f - 1)
                        mm(psum[6 + f % 2][:], g_up[:, 0, f * P:(f + 1) * P], low[:, 1, :], start=True, stop=False)
                        mm(psum[6 + f % 2][:], g_up[0:32, 1, f * P:(f + 1) * P], low[0:32, 2, :], start=False, stop=True).then_inc(S("lora_done"), 1)

            pe.wait_ge(S("tile_taken"), S_WOUT)
            pe.wait_ge(S("lora_ready"), TT)

            def cumulate(f):
                if f >= 2:
                    pe.wait_ge(S("exps_ready"), f - 1)
                for t in range(TT):
                    c = slice(t * P, (t + 1) * P)
                    mm(psum[2 * (f % 2)][:, c], lw[:, t, f * P:(f + 1) * P], C("cum_inc"), start=True, stop=True)
                for t in range(TT):
                    c = slice(t * P, (t + 1) * P)
                    last = mm(psum[2 * (f % 2) + 1][:, c], lw[:, t, f * P:(f + 1) * P], C("cum_exc"), start=True, stop=True)
                last.then_inc(S("cum_done"), 1)

            pe.wait_ge(S("lora_ready"), TT + NF)
            for f in range(NF):
                pe.wait_ge(S("sqk_ready"), f + 1)
                last = mm(psum[4][0:10, :], C("sel", 10 * f, 10), sqk[:, f, :], start=f == 0, stop=f == NF - 1)
            last.then_inc(S("kss_done"), 1)
            for f in range(NF):
                cumulate(f)
            pe.wait_ge(S("exps_ready"), NF)
            pe.wait_ge(S("lora_ready"), TT + NF + NF)

            def scores(h):
                f, b = h // 2, HD * (h % 2)
                if h >= 1:
                    pe.wait_ge(S("s_ret_ready"), h)
                for j in range(TT):
                    w = T - P * j
                    o = psum[(2, 3, 4, 3)[j]][:, (384 if j == 3 else 0):(384 if j == 3 else 0) + w]
                    last = mm(o, qk[b:b + HD, 4 + f, j * P:(j + 1) * P], qk[b:b + HD, f, j * P:T], start=True, stop=True)
                last.then_inc(S("s_ret_done"), 1)

            def ret_out(h):
                f, b = h // 2, HD * (h % 2)
                pe.wait_ge(S("s_ret_ready"), h + 1)
                if f >= 2:
                    pe.wait_ge(S("y_ret_out"), f - 1)
                off = 0
                for j in range(TT):
                    w = T - P * j
                    last = mm(psum[6 + f % 2][b:b + HD, j * P:T], v_ret[:, j, h * HD:(h + 1) * HD], s_ret[:, h % 2, off:off + w],
                              start=j == 0, stop=j == TT - 1)
                    off += w
                last.then_inc(S("y_ret_step"), 1)

            pe.wait_ge(S("kn_ready"), 1)
            for h in range(RH):
                scores(h)
                ret_out(h)
                if h % 2 == 1:
                    f = h // 2
                    pe.wait_ge(S("krn_ready"), 1)
                    if f >= 1:
                        pe.wait_ge(S("prep_ready"), f)
                    mm(psum[5][:], C("spread", f * P, P)[0:8, :], rn[0:8, :], start=True, stop=True).then_inc(S("kk_done"), 1)
                    pe.wait_ge(S("rk_ready"), f + 1)
                    mm(psum[5][:], C("blockones"), pt[:, 1, :], start=True, stop=True).then_inc(S("bonus_done"), 1)

            pe.wait_ge(S("prep_ready"), NF)
            for f in range(NF):
                pe.wait_ge(S("y_ret_out"), f + 1)
                mm(psum[2 + f][:], C("center"), qk[:, f, :], start=True, stop=True).then_inc(S("gn_cent_done"), 1)
            for f in range(NF):
                pe.wait_ge(S("gn_sq"), f + 1)
                last = mm(psum[6][0:10, :], C("sel", 10 * f, 10), qk[:, f, :], start=f == 0, stop=f == NF - 1)
            last.then_inc(S("gn_var_done"), 1)
            pe.wait_ge(S("gn_rn"), 1)
            for f in range(NF):
                mm(psum[2 + f][:], C("spread", f * P, P)[0:8, :], grn[0:8, :], start=True, stop=True).then_inc(S("gn_spread_done"), 1)

            pe.wait_ge(S("ret_ready"), NF)
            n = 0
            for src in (kk, bh, kh, vx):
                for t in range(TT):
                    n += 1
                    if n > 8:
                        pe.wait_ge(S("tok_ready"), n - 8)
                    for f in range(NF):
                        last = nc.tensor.transpose(psum[(n - 1) % 8][:, f * P:(f + 1) * P], src[:, f, t * P:(t + 1) * P], C("ident"))
                    last.then_inc(S("tok_done"), 1)
            pe.wait_ge(S("tok_ready"), 16)

            def blocks(o, lhsT, rhs):
                for t in range(TT):
                    c = slice(t * P, (t + 1) * P)
                    last = mm(o[:, c], lhsT[:, c], rhs[:, c], start=True, stop=True)
                return last

            for g in range(2):
                heads = [(j, (4 * g + j) // 2, HD * (j % 2), (4 * g + j) * HD) for j in range(4)]
                if g == 1:
                    pe.wait_ge(S("y_rwkv_out"), 2)
                for j, f, b, _ in heads:
                    blocks(psum[2 * j], ax[b:b + HD, f, :], kk[b:b + HD, f, :]).then_inc(S("ab_done"), 1)
                    blocks(psum[2 * j + 1], kx[b:b + HD, f, :], kk[b:b + HD, f, :]).then_inc(S("ak_done"), 1)
                for j, f, b, _ in heads:
                    pe.wait_ge(S("ab_ready"), 4 * g + j + 1)
                    blocks(psum[2 * j], ax[b:b + HD, f, :], rx[b:b + HD, f, :]).then_inc(S("rb_done"), 1)
                    pe.wait_ge(S("ak_ready"), 4 * g + j + 1)
                    blocks(psum[2 * j + 1], kx[b:b + HD, f, :], rx[b:b + HD, f, :]).then_inc(S("rk_mm_done"), 1)
                for j, f, b, e in heads:
                    pe.wait_ge(S("rb_ready"), 4 * g + j + 1)
                    for t in range(TT):
                        last = mm(psum[2 * j][:, t * HD:(t + 1) * HD], PX[:, j, t * P:(t + 1) * P], v_tok[:, t, e:e + HD],
                                  start=True, stop=True)
                    last.then_inc(S("u_done"), 1)
                    pe.wait_ge(S("xt0_ready"), 4 * g + j + 1)
                    pe.wait_ge(S("rkm_ready"), 4 * g + j + 1)
                    for t in range(TT):
                        c = slice(t * P, (t + 1) * P)
                        last = nc.tensor.transpose(psum[2 * j + 1][:, c], XT[:, j, c], C("ident"))
                    last.then_inc(S("x0_done"), 1)
                for lv in range(5):
                    k = 4 * (5 * g + lv)
                    for j in range(4):
                        if lv == 0:
                            pe.wait_ge(S("u_ready"), 4 * g + j + 1)
                            pe.wait_ge(S("x0_ready"), 4 * g + j + 1)
                        else:
                            pe.wait_ge(S("xt_ready"), 4 * (4 * g + lv - 1) + j + 1)
                        blocks(psum[2 * j], AB[:, j, :], X[:, j, :]).then_inc(S("nx_done"), 1)
                    for j in range(4):
                        pe.wait_ge(S("px_ready"), k + j + 1)
                        if lv < 4:
                            blocks(psum[2 * j + 1], XT[:, j, :], PX[:, j, :]).then_inc(S("xp_done"), 1)
                        else:
                            blocks(psum[2 * j + 1], PX[:, j, :], XT[:, j, :]).then_inc(S("xp_done"), 1)
                    if lv < 4:
                        for j in range(4):
                            pe.wait_ge(S("xn_ready"), k + j + 1)
                            for t in range(TT):
                                c = slice(t * P, (t + 1) * P)
                                last = nc.tensor.transpose(psum[2 * j][:, c], X[:, j, c], C("ident"))
                            last.then_inc(S("xt_done"), 1)
                for j, f, b, e in heads:
                    pe.wait_ge(S("xn_ready"), 4 * (5 * g + 4) + j + 1)
                    o = psum[2 * j][:].rearrange("p (t k e) -> p t k e", t=TT, k=2)
                    for t in range(TT):
                        c = slice(t * P, (t + 1) * P)
                        mm(o[:, t, 0, :], XT[:, j, c], a_tok[:, t, e:e + HD], start=True, stop=True)
                        last = mm(o[:, t, 1, :], XT[:, j, c], GH[:, j, t, 1, :], start=True, stop=True)
                    last.then_inc(S("gh_done"), 1)
                pe.wait_ge(S("gh_ready"), 4 * g + 4)
                for i in range(2):
                    pair = heads[2 * i:2 * i + 2]
                    for j, f, b, e in pair:
                        for t in range(TT):
                            c = slice(t * P, (t + 1) * P)
                            last = mm(psum[1 + 2 * i][b:b + HD, c], GH[:, j, t, 0, :], RB[:, j, c], start=True, stop=True)
                    last.then_inc(S("qt_done"), 1)
                for i in range(2):
                    pair = heads[2 * i:2 * i + 2]
                    for j, f, b, e in pair:
                        for c in range(NCH - 1):
                            t, r = c // 2, slice(CH * (c % 2), CH * (c % 2) + CH)
                            last = mm(psum[(4, 0)[i] + 2 * (c % 2)][b:b + HD, t * HD:(t + 1) * HD], GH[r, j, t, 0, :], b_tok[r, t, e:e + HD],
                                      start=True, stop=True)
                    last.then_inc(S("at_done"), 1)
                    if i == 1:
                        pe.wait_ge(S("qt_ready"), 2 * g + 2)
                    for j, f, b, e in pair:
                        for c in range(NCH - 1):
                            t, r = c // 2, slice(CH * (c % 2), CH * (c % 2) + CH)
                            o = psum[(5, 1)[i] + 2 * (c % 2)][b:b + HD, t * HD:(t + 1) * HD]
                            mm(o, b_tok[r, t, e:e + HD], GH[r, j, t, 1, :], start=True, stop=False)
                            last = mm(o, k_tok[r, t, e:e + HD], v_tok[r, t, e:e + HD], start=False, stop=True)
                    last.then_inc(S("bc_done"), 1)
                pe.wait_ge(S("at_ready"), 4 * g + 4)
                for c in range(1, NCH - 1):
                    pe.wait_ge(S("state_ready"), 7 * g + c)
                    for j, f, b, e in heads:
                        i = j // 2
                        last = mm(psum[0][b:b + HD, i * HD:(i + 1) * HD], AT[b:b + HD, i, c, :], ST[b:b + HD, c, i, :],
                                  start=True, stop=True)
                    last.then_inc(S("state_done"), 1)
                pe.wait_ge(S("state_ready"), 7 * g + 7)
                pe.wait_ge(S("qt_ready"), 2 * g + 2)
                for i in range(2):
                    for j, f, b, e in heads[2 * i:2 * i + 2]:
                        o = psum[2 + 4 * i][b:b + HD, :]
                        for t in range(TT):
                            c = slice(t * P, (t + 1) * P)
                            mm(o[:, c], GH[:, j, t, 1, :], RB[:, j, c], start=True, stop=False)
                            mm(o[:, c], v_tok[:, t, e:e + HD], RK[:, j, c], start=False, stop=False)
                            for u in range(2):
                                k = 2 * t + u
                                if k > 0:
                                    cc = slice(k * CH, (k + 1) * CH)
                                    last = mm(o[:, cc], ST[b:b + HD, k, i, :], QT[b:b + HD, i, cc], start=False, stop=u == 1)
                    last.then_inc(S("y_rwkv_done"), 1)
            pe.wait_ge(S("at_ready"), 2 * NF)
            for f in range(NF):
                pe.wait_ge(S("y_rwkv_out"), NF if f == 2 else f + 1)
                mm(psum[4 + f][:], C("center"), rx[:, f, :], start=True, stop=True).then_inc(S("gn_cent_done"), 1)
            for f in range(NF):
                pe.wait_ge(S("gn_sq"), NF + f + 1)
                last = mm(psum[0][0:10, :], C("sel", 10 * f, 10), ax[:, f, :], start=f == 0, stop=f == NF - 1)
            last.then_inc(S("gn_var_done"), 1)
            pe.wait_ge(S("gn_rn"), 1 + 1)
            for f in range(NF):
                mm(psum[4 + f][:], C("spread", f * P, P)[0:8, :], hrn[0:8, :], start=True, stop=True).then_inc(S("gn_spread_done"), 1)

            def ssq(n, k, ready="sq_ready", src=0, o=7):
                pe.wait_ge(S(ready), k)
                return mm(psum[o][:], C("ones"), sqb[:, src, :], start=n == 0, stop=n == KC - 1)

            pe.wait_ge(S("y_ready"), NF)
            for n in range(KC):
                slab(S_WOUT + n, a_hi, a_lo, "a_lo_ready" if n == 0 else None, KC)
                if n > 0:
                    ssq(n - 1, n, src=(n - 1) % 2).then_inc(S("sq_used"), 1)
            for kc in range(KC):
                pe.wait_ge(S("mem_sq_ready"), kc + 1)
                last = mm(psum[6][:, 0:MEM], C("ones"), mem_sq[:, kc, :], start=kc == 0, stop=kc == KC - 1)
            last.then_inc(S("mem_ssq_done"), 1)
            ssq(7, 8, src=1).then_inc(S("ssq_done"), 1)
            for s in range(S_MK, S_MV):
                slab(s, mem_hi, mem_lo, "mem_lo_ready" if s == S_MK else None)
            pe.wait_ge(S("mem_rstd"), 1)
            for m in range(MEM // P):
                last = mm(psum[5][:, 2 * m:2 * m + 2], mem_rs[0:1, m * P:(m + 1) * P], C("ones", 0, 2)[0:1, :], start=True, stop=True)
            last.then_inc(S("column_done"), 1)
            for s in range(S_MV, S_XQ):
                slab_tok(s, mem_hi, mem_lo)

            def xscores(h):
                for k in range(2):
                    for t in (2 * k, 2 * k + 1):
                        o = psum[2 + k][:, (t % 2) * MEM:(t % 2 + 1) * MEM]
                        for d in range(2):
                            last = mm(o, xq[:, 2 * h + d, t * P:(t + 1) * P], mem_k[:, 2 * h + d, :], start=d == 0, stop=d == 1)
                    last.then_inc(S("xs_done"), 1)

            def xout(h):
                pe.wait_ge(S("xprob_ready"), h + 1)
                for m in range(MEM // P):
                    for t in range(TT):
                        last = nc.tensor.transpose(psum[4 + m][:, t * P:(t + 1) * P], prob[:, h % 2, t, m * P:(m + 1) * P], C("ident"))
                    last.then_inc(S("xprob_t_done"), 1)
                pe.wait_ge(S("xprob_t_ready"), 2 * h + 2)
                if h >= 1:
                    pe.wait_ge(S("a_lo_ready"), 2 * KC + 2 * h)
                for d in range(2):
                    for m in range(MEM // P):
                        last = mm(psum[6 + d][:], mem_v[:, m, h * MEM + d * P:h * MEM + (d + 1) * P], prob_t[:, h % 2, m, :],
                                  start=m == 0, stop=m == 1)
                    last.then_inc(S("xo_done"), 1)

            pe.wait_ge(S("rstd_ready"), 1 + 1)
            for s in range(S_XQ, S_XO):
                slab(s, b_hi, b_lo, "b_lo_ready" if s == S_XQ else None)
                if (s - S_XQ) % 2 == 1:
                    h = (s - S_XQ) // 2
                    if h >= 1:
                        xout(h - 1)
                    pe.wait_ge(S("tile_taken"), s + 1)
                    pe.wait_ge(S("m_tok_ready"), 1)
                    xscores(h)
            xout(XH - 1)
            pe.wait_ge(S("a_lo_ready"), 2 * KC + KC)
            for n in range(KC):
                slab(S_XO + n, a_hi, a_lo)
                if n > 0:
                    ssq(n - 1, KC + n, src=(n - 1) % 2).then_inc(S("sq_used"), 1)
            ssq(7, 2 * KC, src=1).then_inc(S("ssq_done"), 1)

            pe.wait_ge(S("b_lo_ready"), 2 * KC)
            for q in range(MLP_Q):
                for n in range(KC):
                    slab(S_MLP + 16 * q + n, b_hi, b_lo)
                for n in range(KC):
                    if n == 0:
                        pe.wait_ge(S("m_lo_ready"), KC * (q + 1))
                    slab(S_MLP + 16 * q + 8 + n, m_hi, m_lo)
                    if q == MLP_Q - 1 and n > 0:
                        ssq(n - 1, 2 * KC + n)
                        ssq(n - 1, n, "sq3_ready", 1, 6).then_inc(S("sq_used"), 1)
            ssq(7, 3 * KC)
            ssq(7, KC, "sq3_ready", 1, 6).then_inc(S("ssq_done"), 1)

            pe.wait_ge(S("a_lo_ready"), 3 * KC + KC)
            for s in range(S_VIN, S_MERGE):
                if s < S_K2:
                    slab_tok(s, a_hi, a_lo)
                else:
                    slab(s, a_hi, a_lo)
                if s == S_VIN:
                    pe.wait_ge(S("rs_all_ready"), 1)
                    for t in range(TT):
                        last = mm(psum[5][:, 2 * t:2 * t + 2], rs_all[0:1, t * P:(t + 1) * P], C("ones", 0, 2)[0:1, :],
                                  start=True, stop=True)
                    last.then_inc(S("column_done"), 1)
                if s == S_U:
                    for f in range(5):
                        pe.wait_ge(S("sq10_ready"), 5)
                        last = mm(psum[2][0:10, :], C("sel", 10 * f, 10), sq10[:, f, :], start=f == 0, stop=f == 4)
                    last.then_inc(S("qk_ss_done"), 1)
                if S_GA - 1 <= s < S_GB:
                    for f in ((0, 1), (2,), (3,), (4,), ())[s - S_GA + 1]:
                        pe.wait_ge(S("qg_ready"), 5)
                        pe.wait_ge(S("qk_rn"), 1)
                        if f >= 2:
                            pe.wait_ge(S("qk2_ready"), f - 1)
                        mm(psum[3 + f % 2][:], C("swap_ax"), qk2[:, f, :], start=True, stop=True).then_inc(S("rot_done"), 1)
                        mm(psum[5 + f % 2][:], C("spread_q", f * P, P)[0:10, :], rn2[0:10, :], start=True, stop=True).then_inc(S("spread2_done"), 1)
            pe.wait_ge(S("vv_ready"), TT)
            pe.wait_ge(S("qk2_ready"), 5)
            for f in range(NF):
                if f >= 2:
                    pe.wait_ge(S("gm_ready"), f - 1)
                for k in range(2):
                    g, b = 2 * f + k, HD * k
                    for t in range(TT):
                        o = psum[2 + f % 2][b:b + HD, t * P:(t + 1) * P]
                        mm(o, vv[:, t, g * HD:(g + 1) * HD], spatial[:, g, :], start=True, stop=False)
                        last = mm(o, C("ones", 0, HD)[0:1, :], b_row[0:1, g * P:(g + 1) * P], start=False, stop=True)
                last.then_inc(S("vmix_done"), 1)
            pe.wait_ge(S("gm_ready"), NF)

            def scores2(i):
                f, b, t0 = i // 4, HD * ((i // 2) % 2), 2 * (i % 2)
                for k in range(2):
                    if i >= 1:
                        pe.wait_ge(S("exp2_ready"), 2 * (i - 1) + k + 1)
                    c = slice((t0 + k) * P, (t0 + k + 1) * P)
                    mm(psum[2 + k][:], qk2[b:b + HD, f, c], qk2[b:b + HD, 4, :], start=True, stop=True).then_inc(S("s2_done"), 1)

            def transposes2(i):
                pe.wait_ge(S("p2_ready"), 2 * i + 2)
                if i >= 1:
                    pe.wait_ge(S("p2_t_ready"), 2 * i)
                for c in range(TT):
                    for k in range(2):
                        last = nc.tensor.transpose(psum[4 + c // 2][:, (c % 2) * 256 + k * P:(c % 2) * 256 + (k + 1) * P],
                                                   p2[:, i % 2, k, c * P:(c + 1) * P], C("ident"))
                last.then_inc(S("p2_t_done"), 1)

            def out2(h):
                f, b = h // 2, HD * (h % 2)
                pe.wait_ge(S("p2_t_ready"), 4 * h + 4)
                if f >= 2:
                    pe.wait_ge(S("oa_ready"), f - 1)
                for c in range(TT):
                    last = mm(psum[6 + f % 2][b:b + HD, :], v2[:, c, b:b + HD], p2_t[:, c, :], start=c == 0, stop=c == TT - 1)
                last.then_inc(S("o2_done"), 1)

            for i in range(2 * QH + 2):
                if i < 2 * QH:
                    scores2(i)
                if 1 <= i <= 2 * QH:
                    transposes2(i - 1)
                if i >= 2 and i % 2 == 0:
                    out2(i // 2 - 1)
            pe.wait_ge(S("branch_lo"), NF + NF)
            pe.wait_ge(S("branch_lo"), NF)
            for n in range(KC):
                s = S_MERGE + 3 * n
                slab(s, a_hi, a_lo)
                slab(s + 1, a_hi, a_lo)
                s += 2
                pe.wait_ge(S("w_lo_ready"), s + 1)
                pe.wait_ge(S("tile_taken"), s - 1)
                if n >= 2:
                    pe.wait_ge(S("y_mid_ready"), n - 1)
                for kc in range(KC):
                    w = slice(kc * P, (kc + 1) * P)
                    o = psum[s % 2 + 2 * (kc // 4)][:]
                    mm(o, w_hi[:, s % 2, w], b_hi[:, kc, :], start=kc % 4 == 0, stop=False)
                    mm(o, w_hi[:, s % 2, w], b_lo[:, kc, :], start=False, stop=False)
                    last = mm(o, w_lo[:, s % 2, w], b_hi[:, kc, :], start=False, stop=kc % 4 == 3)
                last.then_inc(S("slab_done"), 1)
            for n in range(KC):
                slab(S_OUT2 + n, y_hi, y_lo, "ym_lo" if n == 0 else None)
                if n > 0:
                    ssq(n - 1, 3 * KC + n, src=(n - 1) % 2).then_inc(S("sq_used"), 1)
            ssq(7, 4 * KC, src=1).then_inc(S("ssq_done"), 1)


def shape_constants():
    import numpy as np
    i = np.arange(P)
    row, col = i[:, None], i[None, :]
    chunk = (row // CH) == (col // CH)
    mid = (col // CH) * CH + CH // 2 - 1
    before_mid = chunk & (row <= mid)
    t = {}
    t["ident"] = row == col
    t["ones"] = np.ones((P, P))
    t["blockones"] = (row // HD) == (col // HD)
    t["center"] = (row == col) - ((row // HD) == (col // HD)) / HD
    half = HD // 2
    t["swap_ret"] = (1.0 * ((row // HD == col // HD) & (col % HD >= half) & (row == col - half))
                     - 1.0 * ((row // HD == col // HD) & (col % HD < half) & (row == col + half)))
    quart = HD // 4
    t["swap_ax"] = (1.0 * ((row // half == col // half) & (col % half >= quart) & (row == col - quart))
                    - 1.0 * ((row // half == col // half) & (col % half < quart) & (row == col + quart)))
    t["cum_inc"] = -EXP_HALF * (1.0 * (chunk & (row <= col)) - 1.0 * before_mid)
    t["cum_exc"] = -EXP_HALF * (1.0 * (chunk & (row < col)) - 1.0 * before_mid)
    t["mask_strict"] = chunk & (row < col)
    t["mask_inc"] = chunk & (row <= col)
    t["mask_pair"] = (row // 2 == col // 2) & (row < col)
    t["mask_level"] = np.concatenate([(row // (2 * b) == col // (2 * b)) & (row // b > col // b)
                                      for b in (2, 4, 8, 16, 32)], axis=1)
    t["sel"] = np.concatenate([np.arange(10)[None, :] == 2 * f + row // HD for f in range(5)], axis=1)
    spread = np.concatenate([row == 2 * f + col // HD for f in range(5)], axis=1)
    t["spread"] = spread
    t["spread_q"] = spread * np.where(np.arange(5 * P) < 4 * P, HD ** -0.5, 1.0)
    t["ident2"] = (row % HD) == np.arange(HD)[None, :]
    for name, e in (("eps6", 1e-6), ("eps5", 1e-5), ("eps64", 64e-5)):
        t[name] = np.full((P, 1), e)
    f32 = np.float32
    t["inv_freq"] = (f32(10000.0) ** (-(i % half).astype(f32) / f32(half)))[:, None]
    consts = np.concatenate([np.asarray(t[name], f32) for name, _ in CONSTS], axis=1)

    heads = np.arange(RH, dtype=np.float64)
    log_g = np.log(1.0 - 2.0 ** (-5.0 - heads))
    diff = np.arange(T)[None, :] - i[:, None]
    decay = np.where(diff >= 0, np.exp(log_g[:, None, None] * np.maximum(diff, 0)), 0.0) * HD ** -0.5
    decay = np.ascontiguousarray(decay.transpose(1, 0, 2)).astype(f32)

    tok = np.arange(T)
    freq = f32(10000.0) ** (-np.arange(0, half, 2, dtype=f32) / f32(half))
    place = np.where((i % HD < half)[:, None], (tok // 64)[None, :], (tok % 64)[None, :]).astype(f32)
    ang = (place * freq[i % quart][:, None]).astype(f32)
    axial = np.stack([np.cos(ang), np.sin(ang)], axis=1).astype(f32)
    return consts, decay, axial


def lay_out(a):
    import numpy as np

    def slabs(w):
        k, n = w.shape
        return [w[r:r + DM, c:c + P].reshape(-1, P, P).transpose(1, 0, 2).reshape(P, -1)
                for r in range(0, k, DM) for c in range(0, n, P)]

    w_in, w2 = a["w_in"][0], a["w_in_2"][0]
    up, down = a["mlp_w_up"][0], a["mlp_w_down"][0]
    pad = np.zeros((DM, 96), np.float32)
    rw = 2048
    s = slabs(w_in[:, 0:rw])
    s += slabs(w_in[:, rw + 1536:rw + 1792]) + slabs(np.concatenate([w_in[:, rw + 1792:], pad], axis=1))
    s += slabs(w_in[:, rw + 512:rw + 1024]) + slabs(w_in[:, rw:rw + 512]) + slabs(w_in[:, rw + 1024:rw + 1536])
    s += slabs(a["w_out"][0])
    s += slabs(a["xattn_w_kv"][0]) + slabs(a["xattn_w_q"][0]) + slabs(a["xattn_w_o"][0])
    for q in range(MLP_Q):
        s += slabs(up[:, q * DM:(q + 1) * DM]) + slabs(down[q * DM:(q + 1) * DM, :])
    head = np.concatenate([np.arange(HD) + HD * (f + 4 * k) for f in range(NF) for k in range(2)])
    s += slabs(w2[:, 1792:2304]) + slabs(w2[:, 640:768]) + slabs(w2[:, 512:640]) + slabs(w2[:, 0:512][:, head])
    s += slabs(w2[:, 1280:1792]) + slabs(w2[:, 768:1280][:, head]) + slabs(w2[:, 2304:2816])
    merge = slabs(w2[:, 2816:4864])
    proj = slabs(np.concatenate([a["w_proj_attn_2"][0][head], a["w_proj_gmlp_2"][0]], axis=0))
    s += [w for n in range(KC) for w in (merge[n], merge[KC + n], proj[n])]
    s += slabs(a["w_out_2"][0])
    assert len(s) == NSLAB

    def cols(v):
        return np.asarray(v, np.float32).reshape(-1, P).T

    mu = a["rwkv_mu"][0]
    mu_pad = np.concatenate([mu[1536:1824], np.zeros(96, np.float32), mu[512:1024], mu[0:512], mu[1024:1536]])
    vec = {"norm_mix": a["norm_mix"], "ret_gn_w": a["ret_gn_w"], "ret_gn_b": a["ret_gn_b"], "mu": mu_pad,
           "a0": a["rwkv_a0"], "k_k": a["rwkv_k_k"], "k_a": a["rwkv_k_a"], "r_k": a["rwkv_r_k"],
           "gn_w": a["rwkv_gn_w"], "gn_b": a["rwkv_gn_b"], "norm_xattn": a["norm_xattn"], "norm_mem": a["norm_mem"],
           "norm_mlp": a["norm_mlp"], "norm_final": a["norm_final"], "norm_gain_2": a["norm_gain_2"],
           "q_gain": np.concatenate([a["q_gain_2"][0]] * 2), "k_gain": np.concatenate([a["k_gain_2"][0]] * 2),
           "b_merge": a["b_merge_2"], "final_gain": a["final_gain_2"]}
    params = np.concatenate([cols(vec[name]) for name, _ in PARAMS], axis=1)
    consts, decay, axial = shape_constants()

    def feature_major(x):
        return x[0].T.reshape(KC, P, -1).transpose(1, 0, 2)

    g_up = np.concatenate([a["rwkv_g_up"][0], np.zeros((96, 512), np.float32)])
    rows = np.concatenate([a["rwkv_w0"][0], a["b_spatial_2"][0].reshape(-1)])[None, :]
    ln = np.stack([np.broadcast_to(a["ln_v_gain_2"][0], (P, 512)), np.broadcast_to(a["ln_v_bias_2"][0], (P, 512))], axis=1)
    arrays = {"weights": np.stack(s), "x": feature_major(a["x"]), "mem": feature_major(a["mem"]),
              "pos": np.broadcast_to(a["positions"], (P, T)), "params": params, "consts": consts, "decay": decay,
              "axial": axial, "lora": np.concatenate([a["rwkv_w_up"][0], a["rwkv_a_up"][0]]),
              "g_up": g_up.reshape(2, P, 512).transpose(1, 0, 2), "rows": rows,
              "spatial": a["w_spatial_2"][0].transpose(2, 0, 1), "ln": ln}
    return {name: np.ascontiguousarray(v) for name, v in arrays.items()}


def kernel(**inputs):
    import numpy as np
    import concourse.bacc as bacc
    from concourse.bass_utils import run_bass_kernel_spmd

    arrays = lay_out({name: np.asarray(v) for name, v in inputs.items()})
    nc = bacc.Bacc("TRN2", target_bir_lowering=False, num_devices=1)
    ins = {name: nc.dram_tensor(f"in_{name}", v.shape, mybir.dt.from_np(v.dtype), kind="ExternalInput").ap()
           for name, v in arrays.items()}
    out = nc.dram_tensor("out_fm", (P, KC, T), mybir.dt.float32, kind="ExternalOutput").ap()
    hybrid_blocks(nc, ins, out)
    r = run_bass_kernel_spmd(nc, [{f"in_{name}": v for name, v in arrays.items()}], core_ids=[0])
    return np.ascontiguousarray(r.results[0]["out_fm"].transpose(2, 1, 0).reshape(1, T, DM))
```

```python
import concourse.bass as bass
from concourse import mybir
from concourse.alu_op_type import AluOpType as ALU
from contextlib import ExitStack

P = 128
T = 512
DM = 1024
KC = DM // P
TT = T // P
HD = 64
MEM = 256
XH = 4
CH = 64
NCH = T // CH
RH = 8
NF = 4
EXP_HALF = 0.6065306597126334
QH = 8
NGRP = 8
N_DVE_OUT = 5
MLP_Q = 4

S_RQ, S_RK, S_RV, S_RG = 0, 4, 8, 12
S_WA, S_G0, S_G1 = 16, 17, 18
S_K, S_R, S_V = 19, 23, 27
S_MK, S_MV = 31, 39
S_WOUT = 47
S_XQ, S_XO = 55, 63
S_MLP = 71
S_VIN = S_MLP + MLP_Q * 16
S_V2, S_K2, S_Q2 = S_VIN + 4, S_VIN + 5, S_VIN + 6
S_U, S_GA, S_GB, S_MERGE = S_Q2 + 4, S_Q2 + 8, S_Q2 + 12, S_Q2 + 16
S_ATTN = S_GB + 1
S_PROJ = S_MERGE + 16
S_OUT2 = S_PROJ + 8
NSLAB = S_OUT2 + 8

PARAMS = [("norm_mix", 8), ("ret_gn_w", 4), ("ret_gn_b", 4), ("mu", 15), ("a0", 4), ("k_k", 4), ("k_a", 4),
          ("r_k", 4), ("gn_w", 4), ("gn_b", 4), ("norm_xattn", 8), ("norm_mem", 8), ("norm_mlp", 8),
          ("norm_final", 8), ("norm_gain_2", 8), ("q_gain", 1), ("k_gain", 1), ("b_merge", 16), ("final_gain", 8)]
CONSTS = [("eps6", 1), ("eps64", 1), ("inv_freq", 1), ("kg_scale", 1), ("kg_eps", 1), ("kg_min", 1),
          ("ident", 128), ("ones", 128), ("blockones", 128), ("center", 128), ("swap_ret", 128), ("swap_ax", 128),
          ("cum_inc", 128), ("cum_exc", 128), ("mask_strict", 128), ("mask_inc", 128), ("mask_pair", 128),
          ("mask_level", 5 * 128), ("sel", 50), ("sel_k", 4 * 16), ("sel_g", 4 * 16), ("spread", 8 * 128),
          ("ident2", 64)]


def columns(table):
    at, out = 0, {}
    for name, n in table:
        out[name] = (at, at + n)
        at += n
    return out, at


def hybrid_blocks(nc, ins, out):
    F32, F32R = mybir.dt.float32, mybir.dt.float32r
    ACT = mybir.ActivationFunctionType
    AX = mybir.AxisListType
    cst, n_cst = columns(CONSTS)
    par, n_par = columns(PARAMS)

    ctx = ExitStack()
    with ctx:
        sems = {}

        def S(name):
            if name not in sems:
                sems[name] = ctx.enter_context(nc.semaphore(name))
            return sems[name]

        base = -(-nc.sbuf_base // 1024) * 1024

        def at(name, kib, shape, dtype=F32):
            return nc.alloc_sbuf_tensor_at(name, shape, dtype, offset=base + int(kib * 1024))

        fence = ctx.enter_context(nc.sbuf_tensor("fence", [P, (206 * 1024) // 4], F32))
        del fence
        psum = [ctx.enter_context(nc.psum_tensor(f"bank{i}", [P, 512], F32)) for i in range(8)]

        consts = at("consts", 0, [P, n_cst])
        params = at("params", 13.5, [P, n_par])
        small = at("small", 14, [P, 512])

        def C(name, a=0, n=None):
            lo, hi = cst[name]
            return consts[:, lo + a:(hi if n is None else lo + a + n)]

        def V(name, j=0):
            return params[:, par[name][0] + j:par[name][0] + j + 1]

        w_raw = at("w_raw", 16, [P, 2, KC * P])
        w_hi = at("w_hi", 24, [P, 2, KC * P], F32R)
        w_lo = at("w_lo", 32, [P, 2, KC * P], F32R)
        rstd = at("rstd", 40, [P, T])
        a_hi = at("a_hi", 62, [P, KC, T], F32R)
        a_lo = at("a_lo", 78, [P, KC, T], F32R)

        cos_r = at("cos_r", 42, [P, T])
        sin_r = at("sin_r", 44, [P, T])
        lora = at("lora", 46, [P, 512])
        g_up = at("g_up", 48, [P, 2, 512])
        w0_row = at("w0_row", 150, [1, 512])
        decay = at("decay", 94, [P, RH, T])
        x_in = at("x_in", 110, [P, KC, T])
        qk = at("qk", 110, [P, 8, T])
        v_ret = at("v_ret", 126, [P, TT, 512])
        trig = at("trig", 126, [P, 4, T])
        pos = at("pos", 134, [P, T], mybir.dt.int32)
        rg = at("rg", 134, [P, NF, T])
        sq_in = at("sq_in", 142, [P, KC, T])
        low = at("low", 142, [P, 3, T])
        tmp = at("tmp", 148, [P, 1, T])
        s_ret = at("s_ret", 52, [P, 2, 1280])
        kx = at("kx", 152, [P, NF, T])
        rx = at("rx", 160, [P, NF, T])
        vx = at("vx", 168, [P, NF, T])
        ax = at("ax", 176, [P, NF, T])
        gx = at("gx", 184, [P, NF, T])
        lw = at("lw", 192, [P, TT, 512])
        shift = at("shift", 200, [P, 2, T + 1])
        kk = at("kk", 54, [P, NF, T])
        sqk = at("sqk", 94, [P, NF, T])
        e_inc = at("e_inc", 94, [P, NF, T])
        e_exc = at("e_exc", 102, [P, NF, T])
        e_neg = at("e_neg", 126, [P, NF, T])
        kg_sd = at("kg_sd", 42, [P, T])
        kg_rn = at("kg_rn", 44, [P, T])
        pt = at("pt", 46, [P, 2, T])
        bon = at("bon", 192, [P, NF, T])
        sc = small[:, 0:NF * NCH].rearrange("p (f c) -> p f c", f=NF)
        sr = small[:, 32:64].rearrange("p (f c) -> p f c", f=NF)
        one_ka = small[:, 64:68]
        r_tok = small[:, 68:76]
        GH = at("GH", 62, [P, 4, TT, 2, HD])
        QT = at("QT", 50, [P, 2, T])
        b_tok = at("b_tok", 70, [P, TT, 512])
        k_tok = at("k_tok", 78, [P, TT, 512])
        v_tok = at("v_tok", 86, [P, TT, 512])
        AB = at("AB", 94, [P, 4, T])
        X = at("X", 102, [P, 4, T])
        RB = at("RB", 110, [P, 4, T])
        RK = at("RK", 118, [P, 4, T])
        AK = at("AK", 126, [P, 4, T])
        PX = AK
        AT = at("AT", 126, [P, 2, NCH, HD])
        BC = at("BC", 130, [P, 2, NCH, HD])
        XT = at("XT", 142, [P, 4, T])
        ST = at("ST", 200, [P, NCH, 2, HD])
        gsq = at("gsq", 142, [P, NF, T])
        hsd = at("hsd", 150, [P, T])
        hrn = at("hrn", 52, [P, T])

        x_res = at("x_res", 110, [P, KC, T])
        b_hi = at("b_hi", 126, [P, KC, T], F32R)
        b_lo = at("b_lo", 142, [P, KC, T], F32R)
        sqb = at("sqb", 42, [P, 2, T])
        sq_sum = at("sq_sum", 202, [P, 2, T])
        sqg = at("sqg", 194, [P, 2, T])
        mem_in = at("mem_in", 168, [P, KC, MEM])
        mem_hi = at("mem_hi", 54, [P, KC, MEM], F32R)
        mem_lo = at("mem_lo", 176, [P, KC, MEM], F32R)
        mem_k = at("mem_k", 94, [P, KC, MEM])
        mem_v = at("mem_v", 102, [P, MEM // P, DM])
        mem_rs = at("mem_rs", 204, [P, MEM])
        xq = at("xq", 158, [P, KC, T])
        prob = at("prob", 190, [P, 2, TT, MEM])
        prob_t = at("prob_t", 198, [P, 2, MEM // P, T])
        m_hi = at("m_hi", 158, [P, KC, T], F32R)
        m_lo = at("m_lo", 174, [P, KC, T], F32R)
        m_mid = at("m_mid", 190, [P, 2, T])
        m_tok = small[:, 76:80]
        neg_max = small[:, 80:84]
        p_sum = small[:, 84:88]
        p_inv = small[:, 88:92]
        gain_12 = small[:, 92:100]
        rs_all = at("rs_all", 46, [P, T])
        rs_tmp = at("rs_tmp", 48, [P, T])
        rn2 = at("rn2", 48, [P, T])
        v2 = at("v2", 50, [P, TT, P])
        qk2 = at("qk2", 52, [P, 5, T])
        tmp2 = at("tmp2", 42, [P, 2, T])
        vv = at("vv", 94, [P, TT, 512])
        u2 = at("u2", 102, [P, NF, T])
        ga = at("ga", 158, [P, NF, T])
        gb = at("gb", 166, [P, NF, T])
        ln = at("ln", 174, [P, 2, 512])
        spatial = at("spatial", 178, [P, NGRP, P])
        axial = at("axial", 182, [P, 2, T])
        b_sp = at("b_sp", 186, [P, NF, P])
        v2f = at("v2f", 188, [P, T])
        sq10 = at("sq10", 190, [P, 5, T])
        p2 = at("p2", 190, [P, 2, 2, T])
        p2_t = at("p2_t", 198, [P, TT, T])
        r2_tok = small[:, 100:108]
        ln_stats = small[:, 108:132]
        ln_mv = small[:, 132:140]
        ln_rs = small[:, 140:144]
        max2 = small[:, 144:146]
        sum2 = small[:, 146:148]
        inv2 = small[:, 148:150]
        gate = [at("gate_attn", 94, [P, KC, T]), at("gate_gmlp", 174, [P, KC, T])]
        y_mid = at("y_mid", 166, [P, 2, T])
        y_hi = at("y_hi", 62, [P, KC, T], F32R)
        y_lo = at("y_lo", 78, [P, KC, T], F32R)

        def t4(a):
            return a.rearrange("p (t c) -> p t c", t=TT)

        pair_mask = C("mask_pair").unsqueeze(1).broadcast_to([P, TT, P])
        ident4 = C("ident").unsqueeze(1).broadcast_to([P, TT, P])
        n_first = cst["ones"][1]

        block = ctx.enter_context(nc.Block())
        W = ins["weights"]

        @block.sync
        def _(sp):
            def load_x(i):
                sp.dma_start(x_in[:, 2 * i:2 * i + 2, :], ins["x"][:, 2 * i:2 * i + 2, :]).then_inc(S(f"x_loaded{i}"), 16)

            load_x(0)
            for s in range(NSLAB):
                if s >= 2:
                    sp.wait_ge(S("w_lo_ready"), s - 1)
                sp.dma_start(w_raw[:, s % 2, :], W[s]).then_inc(S(f"w_loaded{s % 2}"), 16)
                if s == 0:
                    load_x(1)
                    load_x(2)
                if s == 1:
                    load_x(3)
                    sp.dma_start(consts[:, n_first:], ins["consts"][:, n_first:]).then_inc(S("masks_loaded"), 16)
                    sp.dma_start(lora[:], ins["lora"]).then_inc(S("masks_loaded"), 16)
                    sp.dma_start(g_up[:], ins["g_up"]).then_inc(S("masks_loaded"), 16)
            for n, name in [(n, "out_ready") for n in range(N_DVE_OUT)] + [(n, "out_ready2") for n in range(N_DVE_OUT, KC)]:
                sp.wait_ge(S(name), n + 1 if n < N_DVE_OUT else n + 1 - N_DVE_OUT)
                sp.dma_start(out[:, n, :], x_res[:, n, :]).then_inc(S("out_stored"), 16)
            sp.wait_ge(S("out_stored"), 16 * KC)

        @block.gpsimd
        def _(pool):
            def mul(o, a, b, name, op=ALU.mult):
                nc.gpsimd.tensor_tensor(o, a, b, op).then_inc(S(name), 1)

            for s in range(NSLAB + 2):
                if s < NSLAB:
                    pool.wait_ge(S("w_hi_ready"), s + 1)
                    mul(w_lo[:, s % 2, :], w_raw[:, s % 2, :], w_hi[:, s % 2, :].bitcast(F32), "w_lo_ready", ALU.subtract)
                if s == S_MK - 1:
                    for f in range(NF):
                        pool.wait_ge(S("rk_ready"), f + 1)
                        pool.wait_ge(S("exps_ready"), f + 1)
                        mul(ax[:, f, :], ax[:, f, :], e_neg[:, f, :], "decayed")
                        mul(kx[:, f, :], kx[:, f, :], e_neg[:, f, :], "decayed")
                        mul(rx[:, f, :], rx[:, f, :], e_inc[:, f, :], "decayed")
                if s == S_MK + 1:
                    for n in range(8):
                        j = n % 4
                        pool.wait_ge(S("ab_ready"), n + 1)
                        if n >= 4:
                            pool.wait_ge(S("gh_done"), 4)
                        mul(t4(XT[:, j, :]), t4(AB[:, j, :]), pair_mask, "pair_ready")
                        pool.wait_ge(S("pair_ready"), n + 1)
                        mul(t4(XT[:, j, :]), t4(XT[:, j, :]), ident4, "xt0_ready", ALU.add)
                for k, s0 in enumerate((S_WOUT, S_XO, S_MLP + 16 * MLP_Q - KC, S_OUT2)):
                    n = s - 2 - s0
                    if 1 <= n <= KC - 2:
                        pool.wait_ge(S("sq_ready"), KC * k + n + 1)
                        if n > 1:
                            pool.wait_ge(S("sq_used"), (KC - 2) * k + n - 1)
                        elif k > 0:
                            pool.wait_ge(S("ssq_done"), k + 1)
                        mul(sq_sum[:, 0, :], sqb[:, 0, :] if n == 1 else sq_sum[:, 0, :], sqb[:, n % 2, :], "sq_used", ALU.add)
            pool.wait_ge(S("rstd_ready"), 5)
            for n in range(N_DVE_OUT, KC):
                pool.wait_ge(S("x_gained"), n + 1)
                mul(x_res[:, n, :], x_res[:, n, :], rstd[:], "out_ready2")

        @block.scalar
        def _(act):
            copy, exp, sigmoid, square, sqrt = ACT.Copy, ACT.Exp, ACT.Sigmoid, ACT.Square, ACT.Sqrt
            marks, last = {}, []

            def A(name):
                marks[name] = marks.get(name, 0) + 1
                last[:] = [name, marks[name]]
                return S(name)

            def actv(o, a, f, **kw):
                if last:
                    act.wait_ge(S(last[0]), last[1])
                return nc.scalar.activation(o, a, f, **kw)

            def split_hi(s):
                if s >= NSLAB:
                    return
                act.wait_ge(S(f"w_loaded{s % 2}"), 16 * (s // 2 + 1))
                if s >= 2:
                    act.wait_ge(S("slab_done"), s - 1)
                actv(w_hi[:, s % 2, :], w_raw[:, s % 2, :], copy).then_inc(A("w_hi_ready"), 1)

            act.dma_start(pos[:], ins["pos"]).then_inc(S("first_loaded"), 16)
            act.dma_start(params[:], ins["params"]).then_inc(S("first_loaded"), 16)
            act.dma_start(consts[:, 0:n_first], ins["consts"][:, 0:n_first]).then_inc(S("first_loaded"), 16)
            act.wait_ge(S("first_loaded"), 48)
            split_hi(0)
            for kc in range(KC):
                act.wait_ge(S(f"x_loaded{kc // 2}"), 16)
                actv(a_hi[:, kc, :], x_in[:, kc, :], copy, scale=V("norm_mix", kc)).then_inc(A("a_hi_ready"), 1)
                actv(sq_in[:, kc, :], x_in[:, kc, :], square).then_inc(A("xn_sq"), 1)
                if kc == 3:
                    split_hi(1)
            act.wait_ge(S("ssq_done"), 1)
            actv(rstd[:], psum[7][:], sqrt, bias=C("eps6"), scale=1.0 / DM).then_inc(A("rms_ready"), 1)
            act.wait_ge(S("angle_ready"), 1)
            actv(sin_r[:], trig[:, 0, :], ACT.Sin).then_inc(A("act_step"), 1)
            actv(trig[:, 1, :], trig[:, 0, :], ACT.Sin, scale=0.5).then_inc(A("sines_ready"), 1)

            def exps(f):
                act.wait_ge(S("cum_done"), f + 1)
                bi, be = psum[2 + 2 * (f % 2)], psum[3 + 2 * (f % 2)]
                actv(e_inc[:, f, :], bi[:], exp).then_inc(A("act_step"), 1)
                actv(e_neg[:, f, :], bi[:], exp, scale=-1.0).then_inc(A("act_step"), 1)
                actv(e_exc[:, f, :], be[:], exp).then_inc(A("exps_ready"), 1)

            for s in range(S_MK):
                split_hi(s + 2)
                if s == 1:
                    act.dma_start(w0_row[:], ins["w0"]).then_inc(S("decay_loaded"), 16)
                    act.dma_start(decay[:], ins["decay"]).then_inc(S("decay_loaded"), 16)
                if S_RG + 2 <= s < S_RG + 2 + NF:
                    f = s - S_RG - 2
                    act.wait_ge(S("tile_taken"), S_RG + f + 1)
                    actv(rg[:, f, :], rg[:, f, :], ACT.Silu).then_inc(A("silu_ready"), 1)
                if s in (14, 16, 18, 20):
                    f = (s - 14) // 2
                    act.wait_ge(S("y_ret_step"), 2 * f + 2)
                    actv(qk[:, f, :], psum[6 + f % 2][:], copy).then_inc(A("y_ret_out"), 1)
                if s == S_G1:
                    act.wait_ge(S("low_ready"), 1)
                    actv(low[0:HD, 0, :], low[0:HD, 0, :], ACT.Tanh).then_inc(A("low_act"), 1)
                    act.wait_ge(S("low_ready"), 2)
                    actv(low[:, 1, :], low[:, 1, :], sigmoid).then_inc(A("low_act"), 1)
                if s == S_K:
                    act.wait_ge(S("low_ready"), 3)
                    actv(low[:, 2, :], low[:, 2, :], sigmoid).then_inc(A("low_act"), 1)
                if s in (S_K + 1, S_K + 2):
                    for i in (2 * (s - S_K) - 2, 2 * (s - S_K) - 1):
                        act.wait_ge(S("lora_done"), 2 * i + 1)
                        actv(lw[:, i, :], psum[2 + i % 2][:], sigmoid).then_inc(A("lora_ready"), 1)
                        act.wait_ge(S("lora_done"), 2 * i + 2)
                        actv(ax[:, i, :], psum[4 + i % 2][:], sigmoid, bias=V("a0", i)).then_inc(A("lora_ready"), 1)
                if s in (S_K + 3, S_K + 4):
                    for f in (2 * (s - S_K) - 6, 2 * (s - S_K) - 5):
                        act.wait_ge(S("lora_done"), 2 * NF + f + 1)
                        actv(gx[:, f, :], psum[6 + f % 2][:], copy).then_inc(A("lora_ready"), 1)
                if s == S_K + 3:
                    for f in range(NF):
                        act.wait_ge(S("gn_cent_done"), f + 1)
                        actv(qk[:, 4 + f, :], psum[2 + f][:], copy).then_inc(A("gn_cent"), 1)
                        actv(qk[:, f, :], psum[2 + f][:], square).then_inc(A("gn_sq"), 1)
                if s == S_K + 4:
                    for f in range(NF):
                        act.wait_ge(S("kk0_ready"), f + 1)
                        actv(sqk[:, f, :], kk[:, f, :], square).then_inc(A("sqk_ready"), 1)
                if s == S_K + 5:
                    act.wait_ge(S("var_done"), 1)
                    actv(kg_sd[0:16, :], psum[6][0:16, :], sqrt, bias=C("kg_eps")[0:16], scale=C("kg_scale")[0:16]).then_inc(A("sd_ready"), 1)
                if s == S_K + 6:
                    exps(0)
                    exps(1)
                if s in (S_K + 8, S_K + 9):
                    exps(s - S_K - 6)

            def tok(g):
                n = 8 * g
                for dst in (v_tok, GH, b_tok, k_tok):
                    for h in range(2):
                        n += 1
                        act.wait_ge(S("tok_done"), n)
                        src = psum[(n - 1) % 4 + (2, 4)[g]][:]
                        if dst is GH:
                            actv(GH[:, :, 2 * h:2 * h + 2, 0, :].rearrange("p j t e -> p t j e"),
                                 src.rearrange("p (t j e) -> p t j e", t=2, j=4), copy).then_inc(A("tok_ready"), 1)
                        else:
                            actv(dst[:, 2 * h:2 * h + 2, 256 * g:256 * g + 256],
                                 src.rearrange("p (t e) -> p t e", t=2), copy).then_inc(A("tok_ready"), 1)

            def memory_hi(kc):
                if kc == 0:
                    act.wait_ge(S("mem_loaded"), 16)
                    act.wait_ge(S("rk_mm_done"), 8)
                actv(mem_hi[:, kc, :], mem_in[:, kc, :], copy, scale=V("norm_mem", kc)).then_inc(A("mem_hi_ready"), 1)

            tok(0)
            for g in range(2):
                for j in range(4):
                    act.wait_ge(S("u_done"), 4 * g + j + 1)
                    actv(GH[:, j, :, 1, :], psum[2 * j][:, 0:256].rearrange("p (t e) -> p t e", t=TT),
                         copy).then_inc(A("u_ready"), 1)
                    act.wait_ge(S("x0_done"), 4 * g + j + 1)
                    actv(X[:, j, :], psum[2 * j + 1][:], copy).then_inc(A("x0_ready"), 1)
                for lv in range(4):
                    for j in range(4):
                        act.wait_ge(S("xt_done"), 4 * (4 * g + lv) + j + 1)
                        actv(XT[:, j, :], psum[2 * j][:], copy).then_inc(A("xt_ready"), 1)
                    if g == 1:
                        memory_hi(2 * lv)
                        memory_hi(2 * lv + 1)
                for j in range(4):
                    act.wait_ge(S("gh_done"), 4 * g + j + 1)
                    actv(GH[:, j].rearrange("p t k e -> p (t k e)"), psum[2 * j][:], copy).then_inc(A("gh_ready"), 1)
                if g == 0:
                    tok(1)
                    act.wait_ge(S("tok_done"), 16)
                    act.wait_ge(S("prep_ready"), NF)
                    act.dma_start(mem_in[:], ins["mem"]).then_inc(S("mem_loaded"), 16)
                else:
                    for kc in range(KC):
                        act.wait_ge(S("mem_lo_ready"), kc + 1)
                        actv(mem_in[:, kc, :], mem_in[:, kc, :], square).then_inc(A("mem_sq_ready"), 1)
                for i in range(2):
                    act.wait_ge(S("y_rwkv_done"), 2 * g + i + 1)
                    actv(rx[:, 2 * g + i, :], psum[2 + 4 * i][:], copy).then_inc(A("y_rwkv_out"), 1)
            for i in range(4):
                act.dma_start(x_res[:, 2 * i:2 * i + 2, :], ins["x"][:, 2 * i:2 * i + 2, :]).then_inc(S(f"x_loaded{i}"), 16)
            act.wait_ge(S("mem_ssq_done"), 1)
            actv(mem_rs[:], psum[3][:, 0:MEM], sqrt, bias=C("eps6"), scale=1.0 / DM).then_inc(A("mem_rms"), 1)
            for f in range(NF):
                act.wait_ge(S("gn_cent_done"), NF + f + 1)
                actv(kx[:, f, :], psum[4 + f][:], copy).then_inc(A("gn_cent"), 1)
                actv(gsq[:, f, :], psum[4 + f][:], square).then_inc(A("gn_sq"), 1)
            split_hi(S_MK + 2)
            split_hi(S_MK + 3)
            act.wait_ge(S("var_done"), 2)
            actv(hsd[0:8, :], psum[2][0:8, :], sqrt, bias=C("eps64")[0:8], scale=1.0 / HD).then_inc(A("sd_ready"), 1)
            for s in range(S_MK + 2, S_WOUT):
                split_hi(s + 2)
                c = s - S_MK - 2
                if c < 4:
                    actv(a_hi[:, c, :], rg[:, c, :], copy).then_inc(A("a_hi_ready"), 1)
                elif c < KC:
                    act.wait_ge(S("y_ready"), c - 3)
                    actv(a_hi[:, c, :], kx[:, c - 4, :], copy).then_inc(A("a_hi_ready"), 1)

            def squares(n, k):
                if n >= 2:
                    act.wait_ge(S("sq_used"), (KC - 2) * k + max(1, n - 2))
                actv(sqb[:, n % 2, :], x_res[:, n, :], square).then_inc(A("sq_ready"), 1)

            def residual(s0, gain, k):
                for n in range(KC):
                    split_hi(s0 + n + 2)
                    act.wait_ge(S("tile_taken"), s0 + n + 1)
                    actv(b_hi[:, n, :], x_res[:, n, :], copy, scale=V(gain, n)).then_inc(A("b_hi_ready"), 1)
                    squares(n, k)

            residual(S_WOUT, "norm_xattn", 0)
            act.wait_ge(S("ssq_done"), 1 + 1)
            actv(rstd[:], psum[7][:], sqrt, bias=C("eps6"), scale=1.0 / DM).then_inc(A("rms_ready"), 1)

            def xattn_exp(h):
                for t in range(TT):
                    act.wait_ge(S("xmax_ready"), 2 * h + t // 2 + 1)
                    actv(prob[:, h % 2, t, :], psum[2 + t // 2][:, (t % 2) * MEM:(t % 2 + 1) * MEM], exp,
                         bias=neg_max[:, t:t + 1], accum_out=p_sum[:, t:t + 1]).then_inc(A("xexp_ready"), 1)

            def xattn_transposed(h):
                for m in range(MEM // P):
                    act.wait_ge(S("xprob_t_done"), 2 * h + m + 1)
                    actv(prob_t[:, h % 2, m, :], psum[4 + m][:], copy).then_inc(A("xprob_t_ready"), 1)

            def xattn_out(h):
                for d in range(2):
                    act.wait_ge(S("xo_done"), 2 * h + d + 1)
                    actv(a_hi[:, 2 * h + d, :], psum[6 + d][:], copy).then_inc(A("a_hi_ready"), 1)

            for s in range(S_XQ, S_XO):
                split_hi(s + 2)
                if (s - S_XQ) % 2 == 1:
                    h = (s - S_XQ) // 2
                    if h >= 1:
                        xattn_transposed(h - 1)
                    xattn_exp(h)
                    if h >= 1:
                        xattn_out(h - 1)
            xattn_transposed(XH - 1)
            xattn_out(XH - 1)
            residual(S_XO, "norm_mlp", 1)
            act.wait_ge(S("ssq_done"), 1 + 2)
            actv(rstd[:], psum[7][:], sqrt, bias=C("eps6"), scale=1.0 / DM).then_inc(A("rms_ready"), 1)
            for q in range(MLP_Q):
                for n in range(KC):
                    split_hi(S_MLP + 16 * q + n + 2)
                    act.wait_ge(S("m_ready"), KC * q + n + 1)
                    actv(m_hi[:, n, :], m_mid[:, n % 2, :], copy).then_inc(A("m_hi_ready"), 1)
                for n in range(KC):
                    split_hi(S_MLP + 16 * q + 8 + n + 2)
                    if q == MLP_Q - 1:
                        act.wait_ge(S("tile_taken"), S_MLP + 16 * q + 8 + n + 1)
                        if n == 0:
                            act.wait_ge(S("gain_12_ready"), 1)
                        actv(a_hi[:, n, :], x_res[:, n, :], copy, scale=gain_12[:, n:n + 1]).then_inc(A("a_hi_ready"), 1)
                        squares(n, 2)
                        if n >= 2:
                            act.wait_ge(S("sqg_used"), max(1, n - 2))
                        actv(sqg[:, n % 2, :], x_res[:, n, :], square, scale=V("norm_final", n)).then_inc(A("sqg_ready"), 1)
            act.dma_start(ln[:], ins["ln"]).then_inc(S("tables_loaded"), 16)
            act.dma_start(spatial[:], ins["spatial"]).then_inc(S("tables_loaded"), 16)
            act.dma_start(axial[:], ins["axial"]).then_inc(S("tables_loaded"), 16)
            act.dma_start(b_sp[:], ins["b_sp"]).then_inc(S("tables_loaded"), 16)
            act.wait_ge(S("ssq_done"), 3 + 1)
            actv(rstd[:], psum[7][:], sqrt, bias=C("eps6"), scale=1.0 / DM).then_inc(A("rms_ready"), 1)
            act.wait_ge(S("mid_var_ready"), 1)
            actv(rs_all[:], rs_tmp[:], sqrt, bias=C("eps6"), scale=1.0 / DM).then_inc(A("rms3_ready"), 1)

            def attn_exp(i):
                for k in range(2):
                    act.wait_ge(S("max2_ready"), 2 * i + k + 1)
                    if i >= 2 and k == 0:
                        act.wait_ge(S("p2_t_done"), i - 1)
                    actv(p2[:, i % 2, k, :], psum[2 + k][:], exp, bias=max2[:, k:k + 1],
                         accum_out=sum2[:, k:k + 1]).then_inc(A("exp2_ready"), 1)

            def attn_t(i):
                for k in range(2):
                    act.wait_ge(S("p2_t_done"), i + 1)
                    if i % 2 == 0 and i >= 2 and k == 0:
                        act.wait_ge(S("o2_done"), i // 2)
                    actv(p2_t[:, 2 * k:2 * k + 2, (i % 2) * 256:(i % 2) * 256 + 256],
                         psum[4 + k][:].rearrange("p (c t) -> p c t", c=2), copy).then_inc(A("p2_t_ready"), 1)

            for s in range(S_VIN, S_PROJ):
                split_hi(s + 2)
                if s == S_V2:
                    act.wait_ge(S("tile_taken"), S_V2)
                    for t in range(TT):
                        actv(vv[:, t, :], vv[:, t, :], ACT.Gelu_apprx_tanh).then_inc(A("gelu_ready"), 1)
                if s == S_K2 + 1:
                    act.wait_ge(S("ln_mv_ready"), TT)
                    actv(ln_rs, ln_mv.rearrange("p (t k) -> p t k", k=2)[:, :, 1], sqrt, bias=C("eps6")).then_inc(A("sd_ready"), 1)
                if S_K2 <= s < S_U:
                    f = (s - S_K2 + 4) % 5
                    act.wait_ge(S("tile_taken"), s + 1)
                    actv(sq10[:, f, :], qk2[:, f, :], square).then_inc(A("sq10_ready"), 1)
                if s == S_U:
                    act.wait_ge(S("var_done"), 3)
                    actv(rn2[0:10, :], psum[6][0:10, :], sqrt, bias=C("eps6")[0:10], scale=1.0 / HD).then_inc(A("sd_ready"), 1)
                if S_U < s <= S_GA:
                    f = s - S_U - 1
                    act.wait_ge(S("tile_taken"), S_U + f + 1)
                    actv(u2[:, f, :], u2[:, f, :], ACT.Gelu_apprx_tanh).then_inc(A("gelu_ready"), 1)
                if S_GA < s <= S_GB:
                    f = s - S_GA - 1
                    act.wait_ge(S("tile_taken"), S_GA + f + 1)
                    actv(ga[:, f, :], ga[:, f, :], ACT.Silu).then_inc(A("silu_ready"), 1)
                if S_GB < s <= S_MERGE:
                    f = s - S_GB - 1
                    act.wait_ge(S("tile_taken"), S_GB + f + 1)
                    actv(gb[:, f, :], gb[:, f, :], ACT.Silu).then_inc(A("silu_ready"), 1)
                i = s - S_ATTN
                if 1 <= i <= 2 * QH:
                    attn_t(i - 1)
                if 0 <= i < 2 * QH:
                    attn_exp(i)
                if s >= S_MERGE:
                    m = s - S_MERGE
                    act.wait_ge(S("tile_taken"), s + 1)
                    actv(gate[m // KC][:, m % KC, :], gate[m // KC][:, m % KC, :], sigmoid, bias=V("b_merge", m)).then_inc(A("gate_ready"), 1)
                if S_GB < s <= S_MERGE:
                    f = s - S_GB - 1
                    act.wait_ge(S("gm_ready"), f + 1)
                    actv(b_hi[:, NF + f, :], tmp2[:, f % 2, :], copy).then_inc(A("branch_hi"), 1)
                if i >= 5 and i % 4 == 1:
                    f = i // 4 - 1
                    act.wait_ge(S("oa_ready"), f + 1)
                    actv(b_hi[:, f, :], ga[:, f, :], copy).then_inc(A("branch_hi"), 1)
            for n in range(KC):
                split_hi(S_PROJ + n + 2)
                act.wait_ge(S("y_mid_ready"), n + 1)
                actv(y_hi[:, n, :], y_mid[:, 0, :], copy).then_inc(A("ym_hi"), 1)
            for n in range(KC):
                split_hi(S_OUT2 + n + 2)
                act.wait_ge(S("tile_taken"), S_OUT2 + n + 1)
                squares(n, 3)
                actv(x_res[:, n, :], x_res[:, n, :], copy, scale=V("final_gain", n)).then_inc(A("x_gained"), 1)
            act.wait_ge(S("ssq_done"), 4 + 1)
            actv(rstd[:], psum[7][:], sqrt, bias=C("eps6"), scale=1.0 / DM).then_inc(A("rms_ready"), 1)

        @block.vector
        def _(dve):
            marks, last = {}, []

            def D(name, n=1):
                marks[name] = marks.get(name, 0) + n
                last[:] = [name, marks[name]]
                return S(name)

            def hold():
                if last:
                    dve.wait_ge(S(last[0]), last[1])

            def step(ins):
                return ins.then_inc(D("dve_step"), 1)

            def tt(o, a, b, op):
                hold()
                return nc.vector.tensor_tensor(o, a, b, op)

            def ts(o, a, s1, s2, op0, op1=ALU.bypass):
                hold()
                return nc.vector.tensor_scalar(o, a, s1, s2, op0, op1)

            def stt(o, a, s1, b, op0, op1):
                hold()
                return nc.vector.scalar_tensor_tensor(out=o, in0=a, scalar=s1, in1=b, op0=op0, op1=op1)

            def cp(o, a):
                hold()
                return nc.vector.tensor_copy(o, a)

            def recip(o, a):
                hold()
                return nc.vector.reciprocal(o, a)

            c1, two_pi = 6.28125, 6.283185307179586
            magic = 1.5 * 2.0 ** 23
            step(nc.vector.memset(sc[:, :, NCH - 1:NCH], 1.0))
            dve.wait_ge(S("first_loaded"), 48)
            dve.wait_ge(S("first_loaded"), 48)
            step(cp(trig[:, 0, :], pos[:]))
            step(ts(trig[:, 1, :], trig[:, 0, :], C("inv_freq"), None, ALU.mult))
            step(ts(trig[:, 2, :], trig[:, 1, :], 1.0 / two_pi, magic, ALU.mult, ALU.add))
            step(ts(trig[:, 3, :], trig[:, 2, :], -magic, None, ALU.add))
            step(stt(trig[:, 1, :], trig[:, 3, :], -c1, trig[:, 1, :], ALU.mult, ALU.add))
            step(stt(trig[:, 1, :], trig[:, 3, :], c1 - two_pi, trig[:, 1, :], ALU.mult, ALU.add))
            ts(trig[:, 0, :], trig[:, 1, :], -3.1415925, 3.1415925, ALU.max, ALU.min).then_inc(D("angle_ready"), 1)

            dve.wait_ge(S("first_loaded"), 48)
            for kc in range(KC):
                dve.wait_ge(S("a_hi_ready"), kc + 1)
                stt(a_lo[:, kc, :], x_in[:, kc, :], V("norm_mix", kc), a_hi[:, kc, :].bitcast(F32),
                    ALU.mult, ALU.subtract).then_inc(D("a_lo_ready"), 1)
                if kc > 0:
                    dve.wait_ge(S("xn_sq"), kc + 1)
                    tt(sq_in[:, 0, :], sq_in[:, 0, :], sq_in[:, kc, :], ALU.add).then_inc(D("x_sq_sum"), 1)
            step(nc.vector.memset(shift[:, :, 0:1], 0.0))
            ka = par["k_a"][0]
            step(ts(one_ka, params[:, ka:ka + 4], -1.0, 1.0, ALU.mult, ALU.add))
            dve.wait_ge(S("rms_ready"), 1)
            recip(rstd[:], rstd[:]).then_inc(D("rstd_ready"), 1)

            def rope(j):
                dve.wait_ge(S("rot_done"), j + 1)
                step(tt(tmp[:, 0, :], psum[2 + j % 2][:], sin_r[:], ALU.mult))
                step(tt(qk[:, j, :], qk[:, j, :], cos_r[:], ALU.mult))
                tt(qk[:, j, :], qk[:, j, :], tmp[:, 0, :], ALU.add).then_inc(D("rope_done"), 1)

            def masked_scores(h):
                off = 0
                dve.wait_ge(S("s_ret_done"), h + 1)
                if h >= 2:
                    dve.wait_ge(S("y_ret_step"), h - 1)
                for j in range(TT):
                    w = T - P * j
                    src = psum[(2, 3, 4, 3)[j]][:, (384 if j == 3 else 0):(384 if j == 3 else 0) + w]
                    tt(s_ret[:, h % 2, off:off + w], src, decay[:, h, 0:w], ALU.mult).then_inc(D("s_ret_ready"), 1)
                    off += w

            def head_norm(f):
                dve.wait_ge(S("gn_spread_done"), f + 1)
                step(tt(qk[:, 4 + f, :], qk[:, 4 + f, :], psum[6 + f % 2][:], ALU.mult))
                step(ts(qk[:, 4 + f, :], qk[:, 4 + f, :], V("ret_gn_w", f), V("ret_gn_b", f), ALU.mult, ALU.add))
                dve.wait_ge(S("silu_ready"), f + 1)
                tt(rg[:, f, :], rg[:, f, :], qk[:, 4 + f, :], ALU.mult).then_inc(D("ret_ready"), 1)

            def prep(f):
                dve.wait_ge(S("kk_done"), f + 1)
                tt(kk[:, f, :], kk[:, f, :], psum[6 + f % 2][:], ALU.mult).then_inc(D("kk_ready"), 1)
                step(ts(pt[:, 0, :], ax[:, f, :], V("k_a", f), one_ka[:, f:f + 1], ALU.mult, ALU.add))
                step(tt(ax[:, f, :], ax[:, f, :], kk[:, f, :], ALU.mult))
                step(tt(kx[:, f, :], kx[:, f, :], pt[:, 0, :], ALU.mult))
                if f > 0:
                    dve.wait_ge(S("bonus_done"), f)
                stt(pt[:, 1, :], rx[:, f, :], V("r_k", f), kx[:, f, :], ALU.mult, ALU.mult).then_inc(D("rk_ready"), 1)
                dve.wait_ge(S("exps_ready"), f + 1)
                stt(kk[:, f, :], kk[:, f, :], -1.0, e_exc[:, f, :], ALU.mult, ALU.mult).then_inc(D("a_ready"), 1)
                step(recip(sr[:, f, 0:NCH - 1], e_exc[:, f, :].rearrange("p (c t) -> p c t", c=NCH)[:, 1:NCH, 0]))
                step(tt(sc[:, f, 0:NCH - 1], e_inc[:, f, :].rearrange("p (c t) -> p c t", c=NCH)[:, 0:NCH - 1, CH - 1],
                        sr[:, f, 0:NCH - 1], ALU.mult))

            def bonus(f):
                dve.wait_ge(S("bonus_done"), f + 1)
                tt(bon[:, f, :], psum[6 + f % 2][:], vx[:, f, :], ALU.mult).then_inc(D("prep_ready"), 1)

            mixed = [(low, 0), (low, 1), (low, 2)] + [(d, f) for d in (kx, rx, vx) for f in range(NF)]
            for s in range(S_MK):
                if S_RV <= s < S_RG - 1:
                    if s == S_RV:
                        rope(7)
                    continue
                dve.wait_ge(S("slab_done"), s + 1)
                bank = psum[s % 2]
                if s < S_RV:
                    tt(qk[:, s, :], bank[:], rstd[:], ALU.mult).then_inc(D("tile_taken"), 1)
                    if s == 0:
                        dve.wait_ge(S("sines_ready"), 1)
                        step(tt(trig[:, 2, :], trig[:, 1, :], trig[:, 1, :], ALU.mult))
                        step(ts(cos_r[:], trig[:, 2, :], -2.0, 1.0, ALU.mult, ALU.add))
                    else:
                        rope(s - 1)
                    if s == 5:
                        dve.wait_ge(S("column_done"), 1)
                        cp(r_tok[:], psum[5][:, 0:8]).then_inc(D("column_ready"), 1)
                elif s < S_RG:
                    for t in range(TT):
                        ts(v_ret[:, t, :], psum[4 + t][:], r_tok[:, 2 * t:2 * t + 1], None, ALU.mult).then_inc(D("tile_taken"), 1)
                elif s < S_WA:
                    tt(rg[:, s - S_RG, :], bank[:], rstd[:], ALU.mult).then_inc(D("tile_taken"), 1)
                    if s == S_RG:
                        dve.wait_ge(S("decay_loaded"), 32)
                else:
                    j = s - S_WA
                    cur, prev = shift[:, j % 2, 1:T + 1], shift[:, j % 2, 0:T]
                    tt(cur, bank[:], rstd[:], ALU.mult).then_inc(D("tile_taken"), 1)
                    step(tt(tmp[:, 0, :], prev, cur, ALU.subtract))
                    dst, f = mixed[j]
                    stt(dst[:, f, :], tmp[:, 0, :], V("mu", j), cur, ALU.mult, ALU.add).then_inc(
                        D("low_ready" if j < 3 else "mix_ready"), 1)
                if S_RG <= s < S_RG + RH:
                    masked_scores(s - S_RG)
                if s == S_K + 2:
                    dve.wait_ge(S("y_ret_step"), RH)
                for f in ((0, 1, 2) if s == S_K + 2 else (3,) if s == S_K + 3 else ()):
                    ts(kk[:, f, :], kx[:, f, :], V("k_k", f), None, ALU.mult).then_inc(D("kk0_ready"), 1)
                if s == S_K + 6:
                    dve.wait_ge(S("sd_ready"), 1)
                    step(ts(kg_rn[0:16, :], kg_sd[0:16, :], C("kg_min")[0:16], None, ALU.max))
                    recip(kg_rn[0:16, :], kg_rn[0:16, :]).then_inc(D("rn_ready"), 1)
                if s in (S_K + 7, S_K + 8):
                    head_norm(2 * (s - S_K) - 14)
                    head_norm(2 * (s - S_K) - 13)
                if s == S_K + 9:
                    prep(0)
                if s == S_K + 10:
                    bonus(0)
                    prep(1)
                if s == S_K + 11:
                    bonus(1)
                    prep(2)
                    bonus(2)
                    prep(3)
                    bonus(3)

            strict = C("mask_strict").unsqueeze(1).broadcast_to([P, TT, P])
            inc = C("mask_inc").unsqueeze(1).broadcast_to([P, TT, P])

            for g in range(2):
                if g == 0:
                    dve.wait_ge(S("decayed"), 3 * NF)
                else:
                    dve.wait_ge(S("y_rwkv_done"), 2)
                for j in range(4):
                    n = 4 * g + j
                    dve.wait_ge(S("ab_done"), n + 1)
                    tt(t4(AB[:, j, :]), t4(psum[2 * j][:]), strict, ALU.mult).then_inc(D("ab_ready"), 1)
                    dve.wait_ge(S("ak_done"), n + 1)
                    tt(t4(AK[:, j, :]), t4(psum[2 * j + 1][:]), strict, ALU.mult).then_inc(D("ak_ready"), 1)
                for j in range(4):
                    n = 4 * g + j
                    dve.wait_ge(S("rb_done"), n + 1)
                    tt(t4(RB[:, j, :]), t4(psum[2 * j][:]), inc, ALU.mult).then_inc(D("rb_ready"), 1)
                    dve.wait_ge(S("rk_mm_done"), n + 1)
                    tt(t4(RK[:, j, :]), t4(psum[2 * j + 1][:]), inc, ALU.mult).then_inc(D("rkm_ready"), 1)
                for lv in range(5):
                    mask = C("mask_level", lv * P, P).unsqueeze(1).broadcast_to([P, TT, P])
                    for j in range(4):
                        n = 4 * (5 * g + lv) + j
                        dve.wait_ge(S("nx_done"), n + 1)
                        tt(t4(PX[:, j, :]), t4(psum[2 * j][:]), mask, ALU.mult).then_inc(D("px_ready"), 1)
                    for j in range(4):
                        n = 4 * (5 * g + lv) + j
                        dve.wait_ge(S("xp_done"), n + 1)
                        dst = XT if lv == 4 else X
                        if lv == 4:
                            dve.wait_ge(S("xt_ready"), 4 * (4 * g + 3) + j + 1)
                        tt(dst[:, j, :], dst[:, j, :], psum[2 * j + 1][:], ALU.add).then_inc(D("xn_ready"), 1)
                    if g == 1 and lv >= 1:
                        for kc in (2 * lv - 2, 2 * lv - 1):
                            dve.wait_ge(S("mem_hi_ready"), kc + 1)
                            stt(mem_lo[:, kc, :], mem_in[:, kc, :], V("norm_mem", kc), mem_hi[:, kc, :].bitcast(F32),
                                ALU.mult, ALU.subtract).then_inc(D("mem_lo_ready"), 1)
                def halves(a, i, u, n):
                    return a[:, i].rearrange("p (t u) e -> p t u e", u=2)[:, 0:n, u, :]

                for i in range(2):
                    f = 2 * g + i
                    dve.wait_ge(S("qt_done"), f + 1)
                    tt(QT[:, i, :], psum[1 + 2 * i][:], rx[:, f, :], ALU.add).then_inc(D("qt_ready"), 1)
                for i in range(2):
                    f = 2 * g + i
                    dve.wait_ge(S("at_done"), f + 1)
                    for u, n in ((0, 4), (1, 3)):
                        tt(halves(AT, i, u, n), psum[(4, 0)[i] + 2 * u][:, 0:n * HD].rearrange("p (c e) -> p c e", c=n),
                           C("ident2").unsqueeze(1).broadcast_to([P, n, HD]), ALU.add).then_inc(D("at_ready"), 1)
                    dve.wait_ge(S("bc_done"), f + 1)
                    for u, n in ((0, 4), (1, 3)):
                        scale = sc[:, f, :].rearrange("p (t u) -> p t u", u=2)[:, 0:n, u].unsqueeze(2).broadcast_to([P, n, HD])
                        tt(halves(BC, i, u, n), psum[(5, 1)[i] + 2 * u][:, 0:n * HD].rearrange("p (c e) -> p c e", c=n),
                           scale, ALU.mult).then_inc(D("bc_ready"), 1)
                cp(ST[:, 1], BC[:, :, 0, :]).then_inc(D("state_ready"), 1)
                for c in range(1, NCH - 1):
                    dve.wait_ge(S("state_done"), 6 * g + c)
                    for i in range(2):
                        nc.vector.scalar_tensor_tensor(
                            out=ST[:, c + 1, i], in0=psum[0][:, i * HD:(i + 1) * HD], scalar=sc[:, 2 * g + i, c:c + 1],
                            in1=BC[:, i, c, :], op0=ALU.mult, op1=ALU.add).then_inc(D("state_ready"), 1)
            gain12 = params[:, par["norm_final"][0]:par["norm_final"][1]]
            tt(gain_12, gain12, params[:, par["norm_gain_2"][0]:par["norm_gain_2"][1]], ALU.mult).then_inc(D("gain_12_ready"), 1)

            def head_norm2(f):
                dve.wait_ge(S("gn_spread_done"), NF + f + 1)
                step(tt(kx[:, f, :], kx[:, f, :], psum[4 + f][:], ALU.mult))
                step(ts(kx[:, f, :], kx[:, f, :], V("gn_w", f), V("gn_b", f), ALU.mult, ALU.add))
                step(tt(kx[:, f, :], kx[:, f, :], bon[:, f, :], ALU.add))
                tt(kx[:, f, :], kx[:, f, :], gx[:, f, :], ALU.mult).then_inc(D("y_ready"), 1)

            def mixer_lo(c):
                dve.wait_ge(S("a_hi_ready"), KC + c + 1)
                y = rg[:, c, :] if c < 4 else kx[:, c - 4, :]
                tt(a_lo[:, c, :], y, a_hi[:, c, :].bitcast(F32), ALU.subtract).then_inc(D("a_lo_ready"), 1)

            dve.wait_ge(S("mem_rms"), 1)
            recip(mem_rs[:], mem_rs[:]).then_inc(D("mem_rstd"), 1)
            for n in range(KC):
                s = S_MK + n
                dve.wait_ge(S("slab_done"), s + 1)
                tt(mem_k[:, n, :], psum[s % 2][:, 0:MEM], mem_rs[:], ALU.mult).then_inc(D("tile_taken"), 1)
                if n == 1:
                    dve.wait_ge(S("sd_ready"), 2)
                    recip(hrn[0:8, :], hsd[0:8, :]).then_inc(D("rn_ready"), 1)
                if n >= 4:
                    head_norm2(n - 4)
            dve.wait_ge(S("column_done"), 1 + 1)
            cp(m_tok, psum[6][:, 0:4]).then_inc(D("column_ready"), 1)
            for c in range(KC):
                mixer_lo(c)
            dve.wait_ge(S("slab_done"), S_WOUT)
            for m in range(MEM // P):
                for k in range(2):
                    ts(mem_v[:, m, k * 512:(k + 1) * 512], psum[2 + 2 * m + k][:], m_tok[:, 2 * m:2 * m + 1], None,
                       ALU.mult).then_inc(D("tile_taken", 2), 2)

            def residual(s0, gain, k):
                for n in range(KC):
                    dve.wait_ge(S("slab_done"), s0 + n + 1)
                    if k == 0:
                        dve.wait_ge(S(f"x_loaded{n // 2}"), 32)
                    tt(x_res[:, n, :], psum[(s0 + n) % 2][:], x_res[:, n, :], ALU.add).then_inc(D("tile_taken"), 1)
                    dve.wait_ge(S("b_hi_ready"), KC * k + n + 1)
                    stt(b_lo[:, n, :], x_res[:, n, :], V(gain, n), b_hi[:, n, :].bitcast(F32),
                        ALU.mult, ALU.subtract).then_inc(D("b_lo_ready"), 1)

            residual(S_WOUT, "norm_xattn", 0)
            dve.wait_ge(S("rms_ready"), 1 + 1)
            recip(rstd[:], rstd[:]).then_inc(D("rstd_ready"), 1)

            def xattn_softmax(h):
                for k in range(2):
                    dve.wait_ge(S("xs_done"), 2 * h + k + 1)
                    hold()
                    nc.vector.tensor_reduce(neg_max[:, 2 * k:2 * k + 2], psum[2 + k][:].rearrange("p (t m) -> p t m", t=2),
                                            axis=AX.X, op=ALU.max, negate=True).then_inc(D("xmax_ready"), 1)
                dve.wait_ge(S("xexp_ready"), TT * (h + 1))
                step(recip(p_inv, p_sum))
                tt(prob[:, h % 2], prob[:, h % 2], p_inv.unsqueeze(2).broadcast_to([P, TT, MEM]), ALU.mult).then_inc(D("xprob_ready"), 1)

            def xattn_lo(h):
                for d in range(2):
                    dve.wait_ge(S("a_hi_ready"), 2 * KC + 2 * h + d + 1)
                    tt(a_lo[:, 2 * h + d, :], psum[6 + d][:], a_hi[:, 2 * h + d, :].bitcast(F32), ALU.subtract).then_inc(D("a_lo_ready"), 1)

            for s in range(S_XQ, S_XO):
                dve.wait_ge(S("slab_done"), s + 1)
                stt(xq[:, s - S_XQ, :], psum[s % 2][:], 256.0 ** -0.5, rstd[:], ALU.mult, ALU.mult).then_inc(D("tile_taken"), 1)
                if (s - S_XQ) % 2 == 1:
                    h = (s - S_XQ) // 2
                    xattn_softmax(h)
                    if h >= 1:
                        xattn_lo(h - 1)
            xattn_lo(XH - 1)
            residual(S_XO, "norm_mlp", 1)
            dve.wait_ge(S("rms_ready"), 1 + 2)
            recip(rstd[:], rstd[:]).then_inc(D("rstd_ready"), 1)

            for q in range(MLP_Q):
                for n in range(KC):
                    s = S_MLP + 16 * q + n
                    m = m_mid[:, n % 2, :]
                    dve.wait_ge(S("slab_done"), s + 1)
                    if KC * q + n >= 2:
                        dve.wait_ge(S("m_hi_ready"), KC * q + n - 1)
                    tt(m, psum[s % 2][:], rstd[:], ALU.mult).then_inc(D("tile_taken"), 1)
                    stt(m, m, 0.0, m, ALU.max, ALU.mult).then_inc(D("m_ready"), 1)
                    dve.wait_ge(S("m_hi_ready"), KC * q + n + 1)
                    tt(m_lo[:, n, :], m, m_hi[:, n, :].bitcast(F32), ALU.subtract).then_inc(D("m_lo_ready"), 1)
                for n in range(KC):
                    s = S_MLP + 16 * q + 8 + n
                    dve.wait_ge(S("slab_done"), s + 1)
                    tt(x_res[:, n, :], psum[s % 2][:], x_res[:, n, :], ALU.add).then_inc(D("tile_taken"), 1)
                    if q == MLP_Q - 1:
                        dve.wait_ge(S("a_hi_ready"), 3 * KC + n + 1)
                        stt(a_lo[:, n, :], x_res[:, n, :], gain_12[:, n:n + 1], a_hi[:, n, :].bitcast(F32),
                            ALU.mult, ALU.subtract).then_inc(D("a_lo_ready"), 1)
                        if n > 0:
                            dve.wait_ge(S("sqg_ready"), n + 1)
                            tt(sq_sum[:, 1, :], sqg[:, 0, :] if n == 1 else sq_sum[:, 1, :], sqg[:, n % 2, :], ALU.add).then_inc(D("sqg_used"), 1)
            dve.wait_ge(S("rms_ready"), 1 + 3)
            recip(rstd[:], rstd[:]).then_inc(D("rstd_ready"), 1)
            step(tt(rs_tmp[:], rstd[:], rstd[:], ALU.mult))
            dve.wait_ge(S("ssq_done"), 3 + 1)
            tt(rs_tmp[:], psum[6][:], rs_tmp[:], ALU.mult).then_inc(D("mid_var_ready"), 1)
            dve.wait_ge(S("rms3_ready"), 1)
            step(recip(rs_all[:], rs_all[:]))
            tt(rs_all[:], rs_all[:], rstd[:], ALU.mult).then_inc(D("rs_all_ready"), 1)
            dve.wait_ge(S("column_done"), 2 + 1)
            step(cp(r2_tok, psum[7][:, 0:8]))

            def axial_rope(f):
                dve.wait_ge(S("rot_done"), 8 + f + 1)
                step(tt(tmp2[:, 0, :], psum[2 + f % 2][:], axial[:, 1, :], ALU.mult))
                step(tt(qk2[:, f, :], qk2[:, f, :], axial[:, 0, :], ALU.mult))
                step(tt(qk2[:, f, :], qk2[:, f, :], tmp2[:, 0, :], ALU.add))
                dve.wait_ge(S("spread2_done"), f + 1)
                tt(qk2[:, f, :], qk2[:, f, :], psum[4 + f % 2][:], ALU.mult).then_inc(D("qk2_ready"), 1)

            def gated_mlp(f):
                dve.wait_ge(S("gelu_ready"), TT + f + 1)
                dve.wait_ge(S("silu_ready"), 2 * NF + f + 1)
                step(tt(u2[:, f, :], u2[:, f, :], gb[:, f, :], ALU.mult))
                dve.wait_ge(S("vmix_done"), f + 1)
                step(tt(t4(tmp2[:, f % 2, :]), t4(psum[6 + f % 2][:]), b_sp[:, f, :].unsqueeze(1).broadcast_to([P, TT, P]), ALU.add))
                tt(tmp2[:, f % 2, :], tmp2[:, f % 2, :], u2[:, f, :], ALU.mult).then_inc(D("gm_ready"), 1)

            def attn_softmax(i):
                for k in range(2):
                    dve.wait_ge(S("s2_done"), 2 * i + k + 1)
                    hold()
                    nc.vector.tensor_reduce(max2[:, k:k + 1], psum[2 + k][:], axis=AX.X, op=ALU.max, negate=True).then_inc(D("max2_ready"), 1)
                dve.wait_ge(S("exp2_ready"), 2 * i + 2)
                step(recip(inv2, sum2))
                for k in range(2):
                    ts(p2[:, i % 2, k, :], p2[:, i % 2, k, :], inv2[:, k:k + 1], None, ALU.mult).then_inc(D("p2_ready"), 1)

            def attn_gate(f):
                dve.wait_ge(S("o2_done"), 2 * f + 2)
                dve.wait_ge(S("silu_ready"), NF + f + 1)
                tt(ga[:, f, :], psum[6 + f % 2][:], ga[:, f, :], ALU.mult).then_inc(D("oa_ready"), 1)

            for s in range(S_VIN, S_PROJ):
                if s < S_V2 - 1:
                    continue
                dve.wait_ge(S("slab_done"), s + 1)
                bank = psum[s % 2]
                if s < S_V2:
                    for t in range(TT):
                        ts(vv[:, t, :], psum[2 + t][:], r2_tok[:, 2 * t:2 * t + 1], None, ALU.mult).then_inc(D("tile_taken"), 1)
                elif s == S_V2:
                    tt(v2f[:], bank[:], rs_all[:], ALU.mult).then_inc(D("tile_taken"), 1)
                    for n in range(KC):
                        step(stt(x_res[:, n, :], x_res[:, n, :], V("norm_final", n), rstd[:], ALU.mult, ALU.mult))
                elif s < S_U:
                    tt(qk2[:, (s - S_K2 + 4) % 5, :], bank[:], rs_all[:], ALU.mult).then_inc(D("tile_taken"), 1)
                    if s == S_K2:
                        dve.wait_ge(S("v2_done"), 1)
                        cp(v2[:].rearrange("p t e -> p (t e)"), psum[6][:]).then_inc(D("v2_ready"), 1)
                        for t in range(TT):
                            dve.wait_ge(S("gelu_ready"), t + 1)
                            hold()
                            step(nc.vector.bn_stats(ln_stats[:, 6 * t:6 * t + 6], vv[:, t, :]))
                            hold()
                            nc.vector.bn_aggr(ln_mv[:, 2 * t:2 * t + 2], ln_stats[:, 6 * t:6 * t + 6]).then_inc(D("ln_mv_ready"), 1)
                    if s == S_K2 + 2:
                        dve.wait_ge(S("sd_ready"), 3)
                        step(recip(ln_rs, ln_rs))
                        dve.wait_ge(S("tables_loaded"), 64)
                    for t in ((0, 1) if s == S_K2 + 2 else (2, 3) if s == S_K2 + 3 else ()):
                        step(ts(vv[:, t, :], vv[:, t, :], ln_mv[:, 2 * t:2 * t + 1], ln_rs[:, t:t + 1], ALU.subtract, ALU.mult))
                        step(tt(vv[:, t, :], vv[:, t, :], ln[:, 0, :], ALU.mult))
                        tt(vv[:, t, :], vv[:, t, :], ln[:, 1, :], ALU.add).then_inc(D("vv_ready"), 1)
                elif s < S_GA:
                    tt(u2[:, s - S_U, :], bank[:], rs_all[:], ALU.mult).then_inc(D("tile_taken"), 1)
                    if s == S_U:
                        dve.wait_ge(S("sq10_ready"), 5)
                        for f in range(5):
                            ts(qk2[:, f, :], qk2[:, f, :], V("k_gain" if f == 4 else "q_gain"), 1.0 if f == 4 else HD ** -0.5,
                               ALU.mult, ALU.mult).then_inc(D("qg_ready"), 1)
                    if s == S_U + 1:
                        dve.wait_ge(S("sd_ready"), 4)
                        recip(rn2[0:10, :], rn2[0:10, :]).then_inc(D("rn_ready"), 1)
                elif s < S_GB:
                    tt(ga[:, s - S_GA, :], bank[:], rs_all[:], ALU.mult).then_inc(D("tile_taken"), 1)
                elif s < S_MERGE:
                    tt(gb[:, s - S_GB, :], bank[:], rs_all[:], ALU.mult).then_inc(D("tile_taken"), 1)
                else:
                    m = s - S_MERGE
                    if m == 0:
                        dve.wait_ge(S("vmix_done"), NF)
                    tt(gate[m // KC][:, m % KC, :], bank[:], rs_all[:], ALU.mult).then_inc(D("tile_taken"), 1)
                for f in {S_U + 2: (0, 1), S_U + 3: (2,), S_GA: (3,), S_GA + 1: (4,)}.get(s, ()):
                    axial_rope(f)
                if S_GB < s <= S_MERGE:
                    f = s - S_GB - 1
                    gated_mlp(f)
                i = s - S_ATTN
                if 0 <= i < 2 * QH:
                    attn_softmax(i)
                if S_GB < s <= S_MERGE:
                    dve.wait_ge(S("branch_hi"), f + 1)
                    tt(b_lo[:, NF + f, :], tmp2[:, f % 2, :], b_hi[:, NF + f, :].bitcast(F32), ALU.subtract).then_inc(D("branch_lo"), 1)
                if i >= 5 and i % 4 == 1:
                    f = i // 4 - 1
                    attn_gate(f)
                    dve.wait_ge(S("branch_hi"), NF + f + 1)
                    tt(b_lo[:, f, :], ga[:, f, :], b_hi[:, f, :].bitcast(F32), ALU.subtract).then_inc(D("branch_lo"), 1)
            dve.wait_ge(S("gate_ready"), 2 * KC)
            for n in range(KC):
                s = S_PROJ + n
                dve.wait_ge(S("slab_done"), s + 1)
                if n >= 1:
                    dve.wait_ge(S("ym_hi"), n)
                step(tt(y_mid[:, 0, :], psum[s % 2][:], gate[0][:, n, :], ALU.mult))
                tt(y_mid[:, 1, :], psum[2 + s % 2][:], gate[1][:, n, :], ALU.mult).then_inc(D("tile_taken"), 1)
                tt(y_mid[:, 0, :], y_mid[:, 0, :], y_mid[:, 1, :], ALU.add).then_inc(D("y_mid_ready"), 1)
                dve.wait_ge(S("ym_hi"), n + 1)
                tt(y_lo[:, n, :], y_mid[:, 0, :], y_hi[:, n, :].bitcast(F32), ALU.subtract).then_inc(D("ym_lo"), 1)
            for n in range(KC):
                s = S_OUT2 + n
                dve.wait_ge(S("slab_done"), s + 1)
                tt(x_res[:, n, :], psum[s % 2][:], x_res[:, n, :], ALU.add).then_inc(D("tile_taken"), 1)
            dve.wait_ge(S("rms_ready"), 1 + 4)
            recip(rstd[:], rstd[:]).then_inc(D("rstd_ready"), 1)
            for n in range(N_DVE_OUT):
                dve.wait_ge(S("x_gained"), n + 1)
                tt(x_res[:, n, :], x_res[:, n, :], rstd[:], ALU.mult).then_inc(D("out_ready"), 1)

        @block.tensor
        def _(pe):
            mm = nc.tensor.matmul
            wide_slabs = set(range(S_RV, S_RG)) | set(range(S_MV, S_WOUT)) | set(range(S_VIN, S_V2))

            def begin(s):
                pe.wait_ge(S("w_lo_ready"), s + 1)
                before = s - 2
                while before in wide_slabs:
                    before -= 2
                if before >= 0:
                    pe.wait_ge(S("tile_taken"), before + 1)

            def part(s, hi, lo, kcs, ready=None, k=0, at=0, first=0, last=KC - 1):
                for kc in kcs:
                    if ready:
                        pe.wait_ge(S(ready), k + kc + 1)
                    w = slice(kc * P, (kc + 1) * P)
                    o = psum[s % 2 + at][:, 0:hi.shape[2]]
                    mm(o, w_hi[:, s % 2, w], hi[:, kc, :], start=kc == first, stop=False)
                    mm(o, w_hi[:, s % 2, w], lo[:, kc, :], start=False, stop=False)
                    done = mm(o, w_lo[:, s % 2, w], hi[:, kc, :], start=False, stop=kc == last)
                return done

            def slab(s, hi, lo, ready=None, k=0):
                begin(s)
                part(s, hi, lo, range(KC), ready, k).then_inc(S("slab_done"), 1)

            def wide(s, hi, lo, kcs, banks, total=KC):
                pe.wait_ge(S("w_lo_ready"), s + 1)
                halves = 2 // len(kcs)
                for i, kc in enumerate(kcs):
                    for t in range(hi.shape[2] // P):
                        for k in range(halves):
                            o = psum[banks[t * halves + k]][:]
                            w = slice((i + k) * 512, (i + k + 1) * 512)
                            c = slice(t * P, (t + 1) * P)
                            mm(o, hi[:, kc, c], w_hi[:, s % 2, w], start=kc == 0, stop=False)
                            mm(o, lo[:, kc, c], w_hi[:, s % 2, w], start=False, stop=False)
                            last = mm(o, hi[:, kc, c], w_lo[:, s % 2, w], start=False, stop=kc == KC - 1)
                last.then_inc(S("slab_done"), 1)

            def rot(j):
                pe.wait_ge(S("tile_taken"), j + 1)
                if j >= 2:
                    pe.wait_ge(S("rope_done"), j - 1)
                mm(psum[2 + j % 2][:], C("swap_ret"), qk[:, j, :], start=True, stop=True).then_inc(S("rot_done"), 1)

            def scores(h):
                f, b = h // 2, HD * (h % 2)
                if h >= 1:
                    pe.wait_ge(S("s_ret_ready"), 4 * h)
                for j in range(TT):
                    w = T - P * j
                    o = psum[(2, 3, 4, 3)[j]][:, (384 if j == 3 else 0):(384 if j == 3 else 0) + w]
                    last = mm(o, qk[b:b + HD, 4 + f, j * P:(j + 1) * P], qk[b:b + HD, f, j * P:T], start=True, stop=True)
                last.then_inc(S("s_ret_done"), 1)

            def ret_out(h):
                f, b = h // 2, HD * (h % 2)
                if f >= 2:
                    pe.wait_ge(S("y_ret_out"), f - 1)
                off = 0
                for j in range(TT):
                    w = T - P * j
                    pe.wait_ge(S("s_ret_ready"), 4 * h + j + 1)
                    last = mm(psum[6 + f % 2][b:b + HD, j * P:T], v_ret[:, j, h * HD:(h + 1) * HD], s_ret[:, h % 2, off:off + w],
                              start=j == 0, stop=j == TT - 1)
                    off += w
                last.then_inc(S("y_ret_step"), 1)

            def decay_rates(t):
                mm(psum[2 + t % 2][:], low[0:HD, 0, t * P:(t + 1) * P], lora[0:HD, :], start=True, stop=False)
                mm(psum[2 + t % 2][:], C("ones")[0:1, :], w0_row[0:1, :], start=False, stop=True).then_inc(S("lora_done"), 1)

            def learning_rates(f):
                mm(psum[4 + f % 2][:], lora[HD:P, f * P:(f + 1) * P], low[HD:P, 0, :], start=True, stop=True).then_inc(S("lora_done"), 1)

            def output_gates(f):
                mm(psum[6 + f % 2][:], g_up[:, 0, f * P:(f + 1) * P], low[:, 1, :], start=True, stop=False)
                mm(psum[6 + f % 2][:], g_up[0:32, 1, f * P:(f + 1) * P], low[0:32, 2, :], start=False, stop=True).then_inc(S("lora_done"), 1)

            def cumulate(f):
                for k, name in enumerate(("cum_inc", "cum_exc")):
                    for t in range(TT):
                        c = slice(t * P, (t + 1) * P)
                        last = mm(psum[2 + 2 * (f % 2) + k][:, c], lw[:, t, f * P:(f + 1) * P], C(name), start=True, stop=True)
                last.then_inc(S("cum_done"), 1)

            def spread(f, k, name):
                mm(psum[6 + f % 2][:], C("spread", (k + f) * P, P)[0:16, :], kg_rn[0:16, :], start=True, stop=True).then_inc(S(name), 1)

            def bonus(f):
                pe.wait_ge(S("rk_ready"), f + 1)
                mm(psum[6 + f % 2][:], C("blockones"), pt[:, 1, :], start=True, stop=True).then_inc(S("bonus_done"), 1)

            pe.wait_ge(S("first_loaded"), 48)
            for s in range(S_MK):
                if S_RV <= s < S_RG:
                    if s == S_RV:
                        pe.wait_ge(S("column_ready"), 1)
                    i = s - S_RV
                    wide(s, a_hi, a_lo, (2 * i, 2 * i + 1), (4, 5, 6, 7))
                else:
                    slab(s, a_hi, a_lo, "a_lo_ready" if s == 0 else None)
                if s == 0:
                    pe.wait_ge(S("x_sq_sum"), KC - 1)
                    mm(psum[7][:], C("ones"), sq_in[:, 0, :], start=True, stop=True).then_inc(S("ssq_done"), 1)
                    pe.wait_ge(S("masks_loaded"), 48)
                if 1 <= s <= S_RV:
                    rot(s - 1)
                if s == 4:
                    for t in range(TT):
                        last = mm(psum[5][:, 2 * t:2 * t + 2], rstd[0:1, t * P:(t + 1) * P], C("ones", 0, 2)[0:1, :],
                                  start=True, stop=True)
                    last.then_inc(S("column_done"), 1)
                if S_RG <= s < S_RG + RH:
                    h = s - S_RG
                    if h == 0:
                        pe.wait_ge(S("rope_done"), 8)
                        pe.wait_ge(S("tile_taken"), S_RG)
                    else:
                        ret_out(h - 1)
                    scores(h)
                if s == S_RG + RH:
                    ret_out(RH - 1)
                if s == S_K + 1:
                    pe.wait_ge(S("masks_loaded"), 48)
                    pe.wait_ge(S("decay_loaded"), 32)
                    pe.wait_ge(S("low_act"), 3)
                    pe.wait_ge(S("s_ret_ready"), 4 * RH)
                if s in (S_K + 1, S_K + 2):
                    for i in (2 * (s - S_K) - 2, 2 * (s - S_K) - 1):
                        if i >= 2:
                            pe.wait_ge(S("lora_ready"), 2 * i - 2)
                        decay_rates(i)
                        learning_rates(i)
                if s == S_K + 3:
                    pe.wait_ge(S("y_ret_out"), NF)
                    output_gates(0)
                    output_gates(1)
                    pe.wait_ge(S("lora_ready"), 2 * NF)
                    for f in range(NF):
                        mm(psum[2 + f][:], C("center"), qk[:, f, :], start=True, stop=True).then_inc(S("gn_cent_done"), 1)
                if s == S_K + 4:
                    pe.wait_ge(S("lora_ready"), 2 * NF + 2)
                    output_gates(2)
                    output_gates(3)
                if s == S_K + 5:
                    pe.wait_ge(S("lora_ready"), 3 * NF)
                    for f in range(NF):
                        pe.wait_ge(S("gn_sq"), f + 1)
                        mm(psum[6][0:16, :], C("sel_g", 16 * f, 16), qk[:, f, :], start=f == 0, stop=False)
                    for f in range(NF):
                        pe.wait_ge(S("sqk_ready"), f + 1)
                        last = mm(psum[6][0:16, :], C("sel_k", 16 * f, 16), sqk[:, f, :], start=False, stop=f == NF - 1)
                    last.then_inc(S("var_done"), 1)
                if s == S_K + 6:
                    cumulate(0)
                    cumulate(1)
                if s in (S_K + 7, S_K + 8):
                    f = 2 * (s - S_K) - 14
                    pe.wait_ge(S("rn_ready"), 1)
                    if f > 0:
                        pe.wait_ge(S("ret_ready"), f)
                    spread(f, NF, "gn_spread_done")
                    spread(f + 1, NF, "gn_spread_done")
                if s in (S_K + 8, S_K + 9):
                    f = s - S_K - 6
                    pe.wait_ge(S("exps_ready"), f - 1)
                    cumulate(f)
                if s == S_K + 9:
                    pe.wait_ge(S("ret_ready"), NF)
                    spread(0, 0, "kk_done")
                if s == S_K + 10:
                    bonus(0)
                    spread(1, 0, "kk_done")
                if s == S_K + 11:
                    bonus(1)
                    pe.wait_ge(S("prep_ready"), 1)
                    spread(2, 0, "kk_done")

            def tok(g, src, i, h):
                n = 8 * g + 2 * i + h
                bank = n % 4 + (2, 4)[g]
                if n % 8 >= 4:
                    pe.wait_ge(S("tok_ready"), n - 3)
                for t in range(2):
                    for f in range(2):
                        c = slice((2 * h + t) * P, (2 * h + t + 1) * P)
                        last = nc.tensor.transpose(psum[bank][:, (2 * t + f) * P:(2 * t + f + 1) * P], src[:, 2 * g + f, c], C("ident"))
                last.then_inc(S("tok_done"), 1)

            def blocks(o, lhsT, rhs, w=P):
                for t in range(TT):
                    c = slice(t * P, (t + 1) * P)
                    last = mm(o[:, t * w:(t + 1) * w], lhsT[:, c], rhs[:, t * w:(t + 1) * w], start=True, stop=True)
                return last

            pe.wait_ge(S("mix_ready"), 3 * NF)
            pe.wait_ge(S("exps_ready"), NF)
            tok(0, vx, 0, 0)
            tok(0, vx, 0, 1)
            pe.wait_ge(S("a_ready"), 2)
            tok(0, kk, 1, 0)
            tok(0, kk, 1, 1)
            bonus(2)
            pe.wait_ge(S("prep_ready"), 2)
            spread(3, 0, "kk_done")
            pe.wait_ge(S("decayed"), 3 * 2)
            for h in range(2):
                tok(0, ax, 2, h)
            for h in range(2):
                tok(0, kx, 3, h)
            bonus(3)
            pe.wait_ge(S("tok_ready"), 8)
            pe.wait_ge(S("prep_ready"), NF)

            for g in range(2):
                heads = [(j, (4 * g + j) // 2, HD * (j % 2), (4 * g + j) * HD) for j in range(4)]
                if g == 1:
                    pe.wait_ge(S("y_rwkv_out"), 2)
                    pe.wait_ge(S("tok_ready"), 16)
                for j, f, b, _ in heads:
                    blocks(psum[2 * j], ax[b:b + HD, f, :], kk[b:b + HD, f, :]).then_inc(S("ab_done"), 1)
                    blocks(psum[2 * j + 1], kx[b:b + HD, f, :], kk[b:b + HD, f, :]).then_inc(S("ak_done"), 1)
                for j, f, b, _ in heads:
                    pe.wait_ge(S("ab_ready"), 4 * g + j + 1)
                    blocks(psum[2 * j], ax[b:b + HD, f, :], rx[b:b + HD, f, :]).then_inc(S("rb_done"), 1)
                    pe.wait_ge(S("ak_ready"), 4 * g + j + 1)
                    blocks(psum[2 * j + 1], kx[b:b + HD, f, :], rx[b:b + HD, f, :]).then_inc(S("rk_mm_done"), 1)
                for j, f, b, e in heads:
                    pe.wait_ge(S("rb_ready"), 4 * g + j + 1)
                    for t in range(TT):
                        last = mm(psum[2 * j][:, t * HD:(t + 1) * HD], AK[:, j, t * P:(t + 1) * P], v_tok[:, t, e:e + HD],
                                  start=True, stop=True)
                    last.then_inc(S("u_done"), 1)
                    pe.wait_ge(S("xt0_ready"), 4 * g + j + 1)
                    pe.wait_ge(S("rkm_ready"), 4 * g + j + 1)
                    for t in range(TT):
                        c = slice(t * P, (t + 1) * P)
                        last = nc.tensor.transpose(psum[2 * j + 1][:, c], XT[:, j, c], C("ident"))
                    last.then_inc(S("x0_done"), 1)
                for lv in range(5):
                    k = 4 * (5 * g + lv)
                    for j in range(4):
                        if lv == 0:
                            pe.wait_ge(S("u_ready"), 4 * g + j + 1)
                            pe.wait_ge(S("x0_ready"), 4 * g + j + 1)
                            pe.wait_ge(S("tok_ready"), 8 * g + 8)
                        else:
                            pe.wait_ge(S("xt_ready"), 4 * (4 * g + lv - 1) + j + 1)
                        blocks(psum[2 * j], AB[:, j, :], X[:, j, :]).then_inc(S("nx_done"), 1)
                    for j in range(4):
                        pe.wait_ge(S("px_ready"), k + j + 1)
                        if lv < 4:
                            blocks(psum[2 * j + 1], XT[:, j, :], PX[:, j, :]).then_inc(S("xp_done"), 1)
                        else:
                            blocks(psum[2 * j + 1], PX[:, j, :], XT[:, j, :]).then_inc(S("xp_done"), 1)
                    for j in range(4 if lv < 4 else 0):
                        pe.wait_ge(S("xn_ready"), k + j + 1)
                        for t in range(TT):
                            c = slice(t * P, (t + 1) * P)
                            last = nc.tensor.transpose(psum[2 * j][:, c], X[:, j, c], C("ident"))
                        last.then_inc(S("xt_done"), 1)
                for j, f, b, e in heads:
                    pe.wait_ge(S("xn_ready"), 4 * (5 * g + 4) + j + 1)
                    blocks(psum[2 * j], XT[:, j, :], GH[:, j].rearrange("p t k e -> p (t k e)")).then_inc(S("gh_done"), 1)
                pe.wait_ge(S("gh_ready"), 4 * g + 4)
                for i in range(2):
                    for j, f, b, e in heads[2 * i:2 * i + 2]:
                        for t in range(TT):
                            c = slice(t * P, (t + 1) * P)
                            last = mm(psum[1 + 2 * i][b:b + HD, c], GH[:, j, t, 0, :], RB[:, j, c], start=True, stop=True)
                    last.then_inc(S("qt_done"), 1)
                for i in range(2):
                    pair = heads[2 * i:2 * i + 2]
                    for j, f, b, e in pair:
                        for c in range(NCH - 1):
                            t, r = c // 2, slice(CH * (c % 2), CH * (c % 2) + CH)
                            last = mm(psum[(4, 0)[i] + 2 * (c % 2)][b:b + HD, t * HD:(t + 1) * HD], GH[r, j, t, 0, :], b_tok[r, t, e:e + HD],
                                      start=True, stop=True)
                    last.then_inc(S("at_done"), 1)
                    if i == 1:
                        pe.wait_ge(S("qt_ready"), 2 * g + 2)
                    for j, f, b, e in pair:
                        for c in range(NCH - 1):
                            t, r = c // 2, slice(CH * (c % 2), CH * (c % 2) + CH)
                            o = psum[(5, 1)[i] + 2 * (c % 2)][b:b + HD, t * HD:(t + 1) * HD]
                            mm(o, b_tok[r, t, e:e + HD], GH[r, j, t, 1, :], start=True, stop=False)
                            last = mm(o, k_tok[r, t, e:e + HD], v_tok[r, t, e:e + HD], start=False, stop=True)
                    last.then_inc(S("bc_done"), 1)
                pe.wait_ge(S("at_ready"), 4 * g + 4)
                for c in range(1, NCH - 1):
                    pe.wait_ge(S("state_ready"), 13 * g + 2 * c - 1)
                    for j, f, b, e in heads:
                        i = j // 2
                        last = mm(psum[0][b:b + HD, i * HD:(i + 1) * HD], AT[b:b + HD, i, c, :], ST[b:b + HD, c, i, :],
                                  start=True, stop=True)
                    last.then_inc(S("state_done"), 1)
                    if g == 0:
                        if c == 1:
                            pe.wait_ge(S("a_ready"), NF)
                            pe.wait_ge(S("decayed"), 3 * NF)
                        if c <= 4:
                            for h in range(2):
                                tok(1, (vx, kk, ax, kx)[c - 1], c - 1, h)
                    elif c <= 4:
                        for kc in (2 * c - 2, 2 * c - 1):
                            pe.wait_ge(S("mem_sq_ready"), kc + 1)
                            last = mm(psum[3][:, 0:MEM], C("ones"), mem_in[:, kc, :], start=kc == 0, stop=kc == KC - 1)
                        if c == 4:
                            last.then_inc(S("mem_ssq_done"), 1)
                pe.wait_ge(S("state_ready"), 13 * g + 13)
                pe.wait_ge(S("tok_ready"), 16)
                pe.wait_ge(S("qt_ready"), 2 * g + 2)
                for i in range(2):
                    for j, f, b, e in heads[2 * i:2 * i + 2]:
                        o = psum[2 + 4 * i][b:b + HD, :]
                        for t in range(TT):
                            c = slice(t * P, (t + 1) * P)
                            mm(o[:, c], GH[:, j, t, 1, :], RB[:, j, c], start=True, stop=False)
                            mm(o[:, c], v_tok[:, t, e:e + HD], RK[:, j, c], start=False, stop=False)
                            for u in range(2):
                                k = 2 * t + u
                                if k > 0:
                                    cc = slice(k * CH, (k + 1) * CH)
                                    last = mm(o[:, cc], ST[b:b + HD, k, i, :], QT[b:b + HD, i, cc], start=False, stop=u == 1)
                    last.then_inc(S("y_rwkv_done"), 1)

            for f in range(NF):
                pe.wait_ge(S("y_rwkv_out"), NF if f == 2 else f + 1)
                mm(psum[4 + f][:], C("center"), rx[:, f, :], start=True, stop=True).then_inc(S("gn_cent_done"), 1)
            for s in range(S_MK, S_MV):
                slab(s, mem_hi, mem_lo, "mem_lo_ready" if s == S_MK else None)
                if s == S_MK + 1:
                    for f in range(NF):
                        pe.wait_ge(S("gn_sq"), NF + f + 1)
                        last = mm(psum[2][0:10, :], C("sel", 10 * f, 10), gsq[:, f, :], start=f == 0, stop=f == NF - 1)
                    last.then_inc(S("var_done"), 1)
                if s == S_MK + 3:
                    pe.wait_ge(S("rn_ready"), 2)
                    for f in range(NF):
                        mm(psum[4 + f][:], C("spread", f * P, P)[0:8, :], hrn[0:8, :], start=True, stop=True).then_inc(S("gn_spread_done"), 1)
            pe.wait_ge(S("y_ready"), 3)
            for m in range(MEM // P):
                last = mm(psum[6][:, 2 * m:2 * m + 2], mem_rs[0:1, m * P:(m + 1) * P], C("ones", 0, 2)[0:1, :], start=True, stop=True)
            last.then_inc(S("column_done"), 1)
            for s in range(S_MV, S_WOUT):
                wide(s, mem_hi, mem_lo, (s - S_MV,), (2, 3, 4, 5))

            def ssq(k):
                pe.wait_ge(S("sq_used"), (KC - 2) * (k + 1))
                mm(psum[7][:], C("ones"), sq_sum[:, 0, :], start=True, stop=False)
                pe.wait_ge(S("sq_ready"), KC * (k + 1))
                return mm(psum[7][:], C("ones"), sqb[:, 1, :], start=False, stop=True)

            for n in range(KC):
                slab(S_WOUT + n, a_hi, a_lo, "a_lo_ready" if n == 0 else None, KC)
            ssq(0).then_inc(S("ssq_done"), 1)

            def xscores(h):
                for k in range(2):
                    for t in (2 * k, 2 * k + 1):
                        o = psum[2 + k][:, (t % 2) * MEM:(t % 2 + 1) * MEM]
                        for d in range(2):
                            last = mm(o, xq[:, 2 * h + d, t * P:(t + 1) * P], mem_k[:, 2 * h + d, :], start=d == 0, stop=d == 1)
                    last.then_inc(S("xs_done"), 1)

            def xtransposes(h):
                pe.wait_ge(S("xprob_ready"), h + 1)
                for m in range(MEM // P):
                    for t in range(TT):
                        last = nc.tensor.transpose(psum[4 + m][:, t * P:(t + 1) * P], prob[:, h % 2, t, m * P:(m + 1) * P], C("ident"))
                    last.then_inc(S("xprob_t_done"), 1)

            def xout(h):
                if h >= 1:
                    pe.wait_ge(S("a_lo_ready"), 2 * KC + 2 * h)
                for d in range(2):
                    for m in range(MEM // P):
                        pe.wait_ge(S("xprob_t_ready"), 2 * h + m + 1)
                        last = mm(psum[6 + d][:], mem_v[:, m, h * MEM + d * P:h * MEM + (d + 1) * P], prob_t[:, h % 2, m, :],
                                  start=m == 0, stop=m == 1)
                    last.then_inc(S("xo_done"), 1)

            for s in range(S_XQ, S_XO):
                slab(s, b_hi, b_lo, "b_lo_ready" if s == S_XQ else None)
                if (s - S_XQ) % 2 == 1:
                    h = (s - S_XQ) // 2
                    if h >= 1:
                        xtransposes(h - 1)
                    pe.wait_ge(S("tile_taken"), s + 1)
                    xscores(h)
                    if h >= 1:
                        xout(h - 1)
            early, late = range(6), range(6, KC)
            for n in range(2):
                begin(S_XO + n)
                part(S_XO + n, a_hi, a_lo, early, "a_lo_ready", 2 * KC)
            xtransposes(XH - 1)
            xout(XH - 1)
            for n in range(2):
                part(S_XO + n, a_hi, a_lo, late, "a_lo_ready", 2 * KC).then_inc(S("slab_done"), 1)
            for n in range(2, KC):
                slab(S_XO + n, a_hi, a_lo)
            ssq(1).then_inc(S("ssq_done"), 1)

            for q in range(MLP_Q):
                for n in range(KC):
                    slab(S_MLP + 16 * q + n, b_hi, b_lo, "b_lo_ready" if q == n == 0 else None, KC)
                for n in range(KC):
                    slab(S_MLP + 16 * q + 8 + n, m_hi, m_lo, "m_lo_ready" if n == 0 else None, KC * q)
            ssq(2)
            pe.wait_ge(S("sqg_used"), KC - 1)
            mm(psum[6][:], C("ones"), sq_sum[:, 1, :], start=True, stop=True).then_inc(S("ssq_done"), 1)

            def qk_norm(f):
                if f >= 2:
                    pe.wait_ge(S("qk2_ready"), f - 1)
                mm(psum[2 + f % 2][:], C("swap_ax"), qk2[:, f, :], start=True, stop=True).then_inc(S("rot_done"), 1)
                mm(psum[4 + f % 2][:], C("spread", f * P, P)[0:10, :], rn2[0:10, :], start=True, stop=True).then_inc(S("spread2_done"), 1)

            def spatial_mix(f):
                if f >= 2:
                    pe.wait_ge(S("gm_ready"), f - 1)
                for k in range(2):
                    g, b = 2 * f + k, HD * k
                    for t in range(TT):
                        last = mm(psum[6 + f % 2][b:b + HD, t * P:(t + 1) * P], vv[:, t, g * HD:(g + 1) * HD], spatial[:, g, :],
                                  start=True, stop=True)
                last.then_inc(S("vmix_done"), 1)

            def scores2(i):
                f, b, t0 = i // 4, HD * ((i // 2) % 2), 2 * (i % 2)
                for k in range(2):
                    if i >= 1:
                        pe.wait_ge(S("exp2_ready"), 2 * (i - 1) + k + 1)
                    c = slice((t0 + k) * P, (t0 + k + 1) * P)
                    mm(psum[2 + k][:], qk2[b:b + HD, f, c], qk2[b:b + HD, 4, :], start=True, stop=True).then_inc(S("s2_done"), 1)

            def transposes2(i):
                pe.wait_ge(S("p2_ready"), 2 * i + 2)
                if i >= 1:
                    pe.wait_ge(S("p2_t_ready"), 2 * i)
                for c in range(TT):
                    for k in range(2):
                        last = nc.tensor.transpose(psum[4 + c // 2][:, (c % 2) * 256 + k * P:(c % 2) * 256 + (k + 1) * P],
                                                   p2[:, i % 2, k, c * P:(c + 1) * P], C("ident"))
                last.then_inc(S("p2_t_done"), 1)

            def out2(h):
                f, b = h // 2, HD * (h % 2)
                pe.wait_ge(S("p2_t_ready"), 4 * h + 4)
                if f >= 2:
                    pe.wait_ge(S("oa_ready"), f - 1)
                else:
                    pe.wait_ge(S("gm_ready"), 3 + f)
                for c in range(TT):
                    last = mm(psum[6 + f % 2][b:b + HD, :], v2[:, c, b:b + HD], p2_t[:, c, :], start=c == 0, stop=c == TT - 1)
                last.then_inc(S("o2_done"), 1)

            for s in range(S_VIN, S_PROJ):
                if s < S_V2:
                    i = s - S_VIN
                    if i == 0:
                        pe.wait_ge(S("a_lo_ready"), 3 * KC + KC)
                    wide(s, a_hi, a_lo, (2 * i, 2 * i + 1), (2, 3, 4, 5))
                    if i == 0:
                        pe.wait_ge(S("rs_all_ready"), 1)
                        for t in range(TT):
                            last = mm(psum[7][:, 2 * t:2 * t + 2], rs_all[0:1, t * P:(t + 1) * P], C("ones", 0, 2)[0:1, :],
                                      start=True, stop=True)
                        last.then_inc(S("column_done"), 1)
                else:
                    slab(s, a_hi, a_lo)
                if s == S_K2:
                    pe.wait_ge(S("tile_taken"), S_V2 + 1)
                    for t in range(TT):
                        last = nc.tensor.transpose(psum[6][:, t * P:(t + 1) * P], v2f[:, t * P:(t + 1) * P], C("ident"))
                    last.then_inc(S("v2_done"), 1)
                if s == S_U:
                    pe.wait_ge(S("v2_ready"), 1)
                    for f in range(5):
                        pe.wait_ge(S("sq10_ready"), 5)
                        last = mm(psum[6][0:10, :], C("sel", 10 * f, 10), sq10[:, f, :], start=f == 0, stop=f == 4)
                    last.then_inc(S("var_done"), 1)
                if s == S_U + 2:
                    pe.wait_ge(S("tile_taken"), S_V2)
                    pe.wait_ge(S("qg_ready"), 5)
                    pe.wait_ge(S("rn_ready"), 3)
                for f in {S_U + 2: (0, 1), S_U + 3: (2,), S_GA: (3,), S_GA + 1: (4,)}.get(s, ()):
                    qk_norm(f)
                if S_GB <= s < S_MERGE:
                    if s == S_GB:
                        pe.wait_ge(S("vv_ready"), TT)
                    spatial_mix(s - S_GB)
                i = s - S_ATTN
                if i >= 3 and i % 2 == 1:
                    out2(i // 2 - 1)
                if 0 <= i < 2 * QH:
                    if i == 0:
                        pe.wait_ge(S("qk2_ready"), 5)
                    scores2(i)
                if 1 <= i <= 2 * QH:
                    transposes2(i - 1)
            for n in range(KC):
                s = S_PROJ + n
                begin(s)
                if n == 0:
                    pe.wait_ge(S("branch_lo"), 2 * NF - 1)
                part(s, b_hi, b_lo, range(NF, KC), at=2, first=NF)
                if n == 0:
                    pe.wait_ge(S("branch_lo"), 2 * NF)
                part(s, b_hi, b_lo, range(NF), last=NF - 1).then_inc(S("slab_done"), 1)
            for n in range(KC):
                slab(S_OUT2 + n, y_hi, y_lo, "ym_lo" if n == 0 else None)
            ssq(3).then_inc(S("ssq_done"), 1)


def shape_constants():
    import numpy as np
    i = np.arange(P)
    row, col = i[:, None], i[None, :]
    chunk = (row // CH) == (col // CH)
    mid = (col // CH) * CH + CH // 2 - 1
    before_mid = chunk & (row <= mid)
    t = {}
    t["ident"] = row == col
    t["ones"] = np.ones((P, P))
    t["blockones"] = (row // HD) == (col // HD)
    t["center"] = (row == col) - ((row // HD) == (col // HD)) / HD
    half = HD // 2
    t["swap_ret"] = (1.0 * ((row // HD == col // HD) & (col % HD >= half) & (row == col - half))
                     - 1.0 * ((row // HD == col // HD) & (col % HD < half) & (row == col + half)))
    quart = HD // 4
    t["swap_ax"] = (1.0 * ((row // half == col // half) & (col % half >= quart) & (row == col - quart))
                    - 1.0 * ((row // half == col // half) & (col % half < quart) & (row == col + quart)))
    t["cum_inc"] = -EXP_HALF * (1.0 * (chunk & (row <= col)) - 1.0 * before_mid)
    t["cum_exc"] = -EXP_HALF * (1.0 * (chunk & (row < col)) - 1.0 * before_mid)
    t["mask_strict"] = chunk & (row < col)
    t["mask_inc"] = chunk & (row <= col)
    t["mask_pair"] = (row // 2 == col // 2) & (row < col)
    t["mask_level"] = np.concatenate([(row // (2 * b) == col // (2 * b)) & (row // b > col // b)
                                      for b in (2, 4, 8, 16, 32)], axis=1)
    t["sel"] = np.concatenate([np.arange(10)[None, :] == 2 * f + row // HD for f in range(5)], axis=1)
    t["sel_k"] = np.concatenate([np.arange(16)[None, :] == 2 * f + row // HD for f in range(NF)], axis=1)
    t["sel_g"] = np.concatenate([np.arange(16)[None, :] == 8 + 2 * f + row // HD for f in range(NF)], axis=1)
    t["spread"] = np.concatenate([row == 2 * f + col // HD for f in range(8)], axis=1)
    t["kg_scale"] = np.where(i < 8, 1.0, 1.0 / HD)[:, None]
    t["kg_eps"] = np.where(i < 8, 0.0, 1e-5)[:, None]
    t["kg_min"] = np.where(i < 8, 1e-12, 0.0)[:, None]
    t["ident2"] = (row % HD) == np.arange(HD)[None, :]
    for name, e in (("eps6", 1e-6), ("eps64", 64e-5)):
        t[name] = np.full((P, 1), e)
    f32 = np.float32
    t["inv_freq"] = (f32(10000.0) ** (-(i % half).astype(f32) / f32(half)))[:, None]
    consts = np.concatenate([np.asarray(t[name], f32) for name, _ in CONSTS], axis=1)

    heads = np.arange(RH, dtype=np.float64)
    log_g = np.log(1.0 - 2.0 ** (-5.0 - heads))
    diff = np.arange(T)[None, :] - i[:, None]
    decay = np.where(diff >= 0, np.exp(log_g[:, None, None] * np.maximum(diff, 0)), 0.0) * HD ** -0.5
    decay = np.ascontiguousarray(decay.transpose(1, 0, 2)).astype(f32)

    tok = np.arange(T)
    freq = f32(10000.0) ** (-np.arange(0, half, 2, dtype=f32) / f32(half))
    place = np.where((i % HD < half)[:, None], (tok // 64)[None, :], (tok % 64)[None, :]).astype(f32)
    ang = (place * freq[i % quart][:, None]).astype(f32)
    axial = np.stack([np.cos(ang), np.sin(ang)], axis=1).astype(f32)
    return consts, decay, axial


def lay_out(a):
    import numpy as np

    def slabs(w):
        k, n = w.shape
        return [w[r:r + DM, c:c + P].reshape(-1, P, P).transpose(1, 0, 2).reshape(P, -1)
                for r in range(0, k, DM) for c in range(0, n, P)]

    def wide(w):
        k, n = w.shape
        r = P * DM // n
        return [w[i:i + r].reshape(-1, P, n).transpose(1, 0, 2).reshape(P, -1) for i in range(0, k, r)]

    w_in, w2 = a["w_in"][0], a["w_in_2"][0]
    up, down = a["mlp_w_up"][0], a["mlp_w_down"][0]
    pad = np.zeros((DM, 96), np.float32)
    rw = 2048
    s = slabs(w_in[:, 0:1024]) + wide(w_in[:, 1024:1536]) + slabs(w_in[:, 1536:rw])
    s += slabs(w_in[:, rw + 1536:rw + 1792]) + slabs(np.concatenate([w_in[:, rw + 1792:], pad], axis=1))
    s += slabs(w_in[:, rw + 512:rw + 1024]) + slabs(w_in[:, rw:rw + 512]) + slabs(w_in[:, rw + 1024:rw + 1536])
    s += slabs(a["xattn_w_kv"][0][:, :DM]) + wide(a["xattn_w_kv"][0][:, DM:])
    s += slabs(a["w_out"][0]) + slabs(a["xattn_w_q"][0]) + slabs(a["xattn_w_o"][0])
    for q in range(MLP_Q):
        s += slabs(up[:, q * DM:(q + 1) * DM]) + slabs(down[q * DM:(q + 1) * DM, :])
    head = np.concatenate([np.arange(HD) + HD * (f + 4 * k) for f in range(NF) for k in range(2)])
    s += wide(w2[:, 1792:2304]) + slabs(w2[:, 640:768]) + slabs(w2[:, 512:640]) + slabs(w2[:, 0:512][:, head])
    s += slabs(w2[:, 1280:1792]) + slabs(w2[:, 768:1280][:, head]) + slabs(w2[:, 2304:2816])
    s += slabs(w2[:, 2816:4864])
    s += slabs(np.concatenate([a["w_proj_attn_2"][0][head], a["w_proj_gmlp_2"][0]], axis=0))
    s += slabs(a["w_out_2"][0])
    assert len(s) == NSLAB

    def cols(v):
        return np.asarray(v, np.float32).reshape(-1, P).T

    mu = a["rwkv_mu"][0]
    mu_pad = np.concatenate([mu[1536:1824], np.zeros(96, np.float32), mu[512:1024], mu[0:512], mu[1024:1536]])
    vec = {"norm_mix": a["norm_mix"], "ret_gn_w": a["ret_gn_w"], "ret_gn_b": a["ret_gn_b"], "mu": mu_pad,
           "a0": a["rwkv_a0"], "k_k": a["rwkv_k_k"], "k_a": a["rwkv_k_a"], "r_k": a["rwkv_r_k"],
           "gn_w": a["rwkv_gn_w"], "gn_b": a["rwkv_gn_b"], "norm_xattn": a["norm_xattn"], "norm_mem": a["norm_mem"],
           "norm_mlp": a["norm_mlp"], "norm_final": a["norm_final"], "norm_gain_2": a["norm_gain_2"],
           "q_gain": np.concatenate([a["q_gain_2"][0]] * 2), "k_gain": np.concatenate([a["k_gain_2"][0]] * 2),
           "b_merge": a["b_merge_2"], "final_gain": a["final_gain_2"]}
    params = np.concatenate([cols(vec[name]) for name, _ in PARAMS], axis=1)
    consts, decay, axial = shape_constants()

    def feature_major(x):
        return x[0].T.reshape(KC, P, -1).transpose(1, 0, 2)

    g_up = np.concatenate([a["rwkv_g_up"][0], np.zeros((96, 512), np.float32)])
    b_sp = a["b_spatial_2"][0].reshape(NF, 2, P).repeat(HD, axis=1).transpose(1, 0, 2)
    ln = np.stack([np.broadcast_to(a["ln_v_gain_2"][0], (P, 512)), np.broadcast_to(a["ln_v_bias_2"][0], (P, 512))], axis=1)
    arrays = {"weights": np.stack(s), "x": feature_major(a["x"]), "mem": feature_major(a["mem"]),
              "pos": np.broadcast_to(a["positions"], (P, T)), "params": params, "consts": consts, "decay": decay,
              "axial": axial, "lora": np.concatenate([a["rwkv_w_up"][0], a["rwkv_a_up"][0]]),
              "g_up": g_up.reshape(2, P, 512).transpose(1, 0, 2), "w0": a["rwkv_w0"], "b_sp": b_sp,
              "spatial": a["w_spatial_2"][0].transpose(2, 0, 1), "ln": ln}
    return {name: np.ascontiguousarray(v) for name, v in arrays.items()}


def kernel(**inputs):
    import numpy as np
    import concourse.bacc as bacc
    from concourse.bass_utils import run_bass_kernel_spmd

    arrays = lay_out({name: np.asarray(v) for name, v in inputs.items()})
    nc = bacc.Bacc("TRN2", target_bir_lowering=False, num_devices=1)
    ins = {name: nc.dram_tensor(f"in_{name}", v.shape, mybir.dt.from_np(v.dtype), kind="ExternalInput").ap()
           for name, v in arrays.items()}
    out = nc.dram_tensor("out_fm", (P, KC, T), mybir.dt.float32, kind="ExternalOutput").ap()
    hybrid_blocks(nc, ins, out)
    r = run_bass_kernel_spmd(nc, [{f"in_{name}": v for name, v in arrays.items()}], core_ids=[0])
    return np.ascontiguousarray(r.results[0]["out_fm"].transpose(2, 1, 0).reshape(1, T, DM))
```

```python
import concourse.bass as bass
from concourse import mybir
from concourse.alu_op_type import AluOpType as ALU
from contextlib import ExitStack

P = 128
T = 512
DM = 1024
KC = DM // P
TT = T // P
HD = 64
MEM = 256
XH = 4
CH = 64
NCH = T // CH
RH = 8
NF = 4
EXP_HALF = 0.6065306597126334
QH = 8
NGRP = 8
N_POOL_SQ = 3
N_DVE_OUT = 5
MLP_Q = 4

S_RQ, S_RK, S_RV = 0, 4, 8
S_WA, S_G0, S_G1 = 12, 13, 14
S_K, S_R, S_V, S_RG = 15, 19, 23, 27
S_RET = S_RV + 4
S_PREP = S_RET + RH - 1
S_MK, S_MV = 31, 39
S_WOUT = 47
S_XQ, S_XO = 55, 63
S_MLP = 71
S_VIN = S_MLP + MLP_Q * 16
S_V2, S_K2, S_Q2 = S_VIN + 4, S_VIN + 5, S_VIN + 6
S_U, S_GA, S_GB, S_MERGE = S_Q2 + 4, S_Q2 + 8, S_Q2 + 12, S_Q2 + 16
S_ATTN = S_GB + 1
S_PROJ = S_MERGE + 16
S_OUT2 = S_PROJ + 8
NSLAB = S_OUT2 + 8

PARAMS = [("norm_mix", 8), ("ret_gn_w", 4), ("ret_gn_b", 4), ("mu", 15), ("a0", 4), ("k_k", 4), ("k_a", 4),
          ("r_k", 4), ("gn_w", 4), ("gn_b", 4), ("norm_xattn", 8), ("norm_mem", 8), ("norm_mlp", 8),
          ("norm_final", 8), ("norm_gain_2", 8), ("q_gain", 1), ("k_gain", 1), ("b_merge", 16), ("final_gain", 8)]
CONSTS = [("eps6", 1), ("eps64", 1), ("inv_freq", 1), ("kg_scale", 1), ("kg_eps", 1), ("kg_min", 1),
          ("ident", 128), ("ones", 128), ("blockones", 128), ("center", 128), ("swap_ax", 128),
          ("cum_inc", 128), ("cum_exc", 128), ("mask_strict", 128), ("mask_inc", 128), ("mask_pair", 128),
          ("mask_level", 5 * 128), ("sel", 50), ("sel_k", 4 * 16), ("sel_g", 4 * 16), ("spread", 8 * 128),
          ("ident2", 64)]


def columns(table):
    at, out = 0, {}
    for name, n in table:
        out[name] = (at, at + n)
        at += n
    return out, at


def hybrid_blocks(nc, ins, out):
    F32, F32R = mybir.dt.float32, mybir.dt.float32r
    ACT = mybir.ActivationFunctionType
    AX = mybir.AxisListType
    cst, n_cst = columns(CONSTS)
    par, n_par = columns(PARAMS)

    ctx = ExitStack()
    with ctx:
        sems = {}

        def S(name):
            if name not in sems:
                sems[name] = ctx.enter_context(nc.semaphore(name))
            return sems[name]

        base = -(-nc.sbuf_base // 1024) * 1024

        def at(name, kib, shape, dtype=F32):
            return nc.alloc_sbuf_tensor_at(name, shape, dtype, offset=base + int(kib * 1024))

        fence = ctx.enter_context(nc.sbuf_tensor("fence", [P, (206 * 1024) // 4], F32))
        del fence
        psum = [ctx.enter_context(nc.psum_tensor(f"bank{i}", [P, 512], F32)) for i in range(8)]

        consts = at("consts", 0, [P, n_cst])
        params = at("params", 13.5, [P, n_par])
        spread_r = at("spread_r", cst["spread"][0] * 4 / 1024, [P, 8 * P], F32R)
        small = at("small", 14, [P, 512])

        def C(name, a=0, n=None):
            lo, hi = cst[name]
            return consts[:, lo + a:(hi if n is None else lo + a + n)]

        def V(name, j=0):
            return params[:, par[name][0] + j:par[name][0] + j + 1]

        w_raw = at("w_raw", 16, [P, 4, KC * P])
        w_lo = at("w_lo", 16, [P, 4, KC * P], F32R)
        w_hi = at("w_hi", 32, [P, 2, KC * P], F32R)
        rstd = at("rstd", 40, [P, T])
        w_hi_mem = at("w_hi_mem", 160, [P, 2, KC * P], F32R)
        w_hi_mlp = at("w_hi_mlp", 94, [P, 2, KC * P], F32R)

        def hi_slot(s):
            for lo, hi, more in ((S_MK, S_WOUT, w_hi_mem), (S_XO, S_VIN, w_hi_mlp)):
                if lo <= s < hi and (s - lo) % 4 >= 2:
                    return more[:, s % 2, :], s - 4
                if lo <= s < hi + 2 and s - 4 >= lo and (s - 4 - lo) % 4 < 2:
                    return w_hi[:, s % 2, :], s - 4
            return w_hi[:, s % 2, :], s - 2

        a_hi = at("a_hi", 62, [P, KC, T], F32R)
        a_lo = at("a_lo", 78, [P, KC, T], F32R)

        cos_r = at("cos_r", 42, [P, T])
        sin_r = at("sin_r", 44, [P, T])
        lora = at("lora", 46, [P, 512])
        g_up = at("g_up", 48, [P, 2, 512])
        w0 = at("w0", 150, [P, 512])
        decay = at("decay", 94, [P, RH, T])
        x_in = at("x_in", 110, [P, KC, T])
        qk = at("qk", 110, [P, 8, T])
        v_ret = at("v_ret", 126, [P, TT, 512])
        trig = at("trig", 126, [P, 4, T])
        pos = at("pos", 134, [P, T], mybir.dt.int32)
        rg = at("rg", 134, [P, NF, T])
        sq_in = at("sq_in", 142, [P, KC, T])
        low = at("low", 142, [P, 3, T])
        tmp = at("tmp", 148, [P, 1, T])
        rot = at("rot", 52, [P, 2, T])
        q_twice = [at("q_twice0", 134, [P, NF, T], F32R), at("q_twice1", 192, [P, NF, T], F32R)]
        k_stack = [at("k_stack0", 168, [P, NF, T], F32R), at("k_stack1", 184, [P, NF, T], F32R)]
        qk_lo = at("qk_lo", 110, [P, 8, T], F32R)
        s_ret = at("s_ret", 52, [P, 2, 1280])
        kx = at("kx", 152, [P, NF, T])
        rx = at("rx", 160, [P, NF, T])
        vx = at("vx", 168, [P, NF, T])
        ax = at("ax", 176, [P, NF, T])
        gx = at("gx", 184, [P, NF, T])
        lw = at("lw", 192, [P, TT, 512])
        shift = at("shift", 200, [P, 2, T + 1])
        kk = at("kk", 54, [P, NF, T])
        sqk = at("sqk", 94, [P, NF, T])
        e_inc = at("e_inc", 94, [P, NF, T])
        e_exc = at("e_exc", 102, [P, NF, T])
        e_neg = at("e_neg", 126, [P, NF, T])
        kg_sd = at("kg_sd", 42, [P, T])
        kg_rn = at("kg_rn", 44, [P, T])
        kg_hi = at("kg_hi", 42, [P, T], F32R)
        kg_lo = at("kg_lo", 44, [P, T], F32R)
        pt = at("pt", 46, [P, 2, T])
        bon = at("bon", 192, [P, NF, T])
        sc = small[:, 0:NF * NCH].rearrange("p (f c) -> p f c", f=NF)
        sr = small[:, 32:64].rearrange("p (f c) -> p f c", f=NF)
        one_ka = small[:, 64:68]
        r_tok = small[:, 68:76]
        GH = at("GH", 62, [P, 4, TT, 2, HD])
        QT = at("QT", 50, [P, 2, T])
        b_tok = at("b_tok", 70, [P, TT, 512])
        k_tok = at("k_tok", 78, [P, TT, 512])
        v_tok = at("v_tok", 86, [P, TT, 512])
        AB = at("AB", 94, [P, 4, T])
        X = at("X", 102, [P, 4, T])
        RB = at("RB", 110, [P, 4, T])
        RK = at("RK", 118, [P, 4, T])
        AK = at("AK", 126, [P, 4, T])
        PX = AK
        AT = at("AT", 126, [P, 2, NCH, HD])
        BC = at("BC", 130, [P, 2, NCH, HD])
        XT = at("XT", 142, [P, 4, T])
        ST = at("ST", 200, [P, NCH, 2, HD])
        gsq = at("gsq", 142, [P, NF, T])
        hsd = at("hsd", 150, [P, T])
        hrn = at("hrn", 52, [P, T])
        hrn_hi = at("hrn_hi", 150, [P, T], F32R)
        hrn_lo = at("hrn_lo", 52, [P, T], F32R)

        x_res = at("x_res", 110, [P, KC, T])
        b_hi = at("b_hi", 126, [P, KC, T], F32R)
        b_lo = at("b_lo", 142, [P, KC, T], F32R)
        sqb = at("sqb", 42, [P, 2, T])
        sq_sum = at("sq_sum", 202, [P, 2, T])
        sqg = at("sqg", 194, [P, 2, T])
        mem_in = at("mem_in", 168, [P, KC, MEM])
        mem_hi = at("mem_hi", 54, [P, KC, MEM], F32R)
        mem_lo = at("mem_lo", 176, [P, KC, MEM], F32R)
        mem_k = at("mem_k", 94, [P, KC, MEM])
        mem_v = at("mem_v", 102, [P, MEM // P, DM])
        mem_rs = at("mem_rs", 204, [P, MEM])
        xq = at("xq", 158, [P, KC, T])
        prob = at("prob", 190, [P, 2, TT, MEM])
        prob_t = at("prob_t", 198, [P, 2, MEM // P, T])
        m_hi = at("m_hi", 158, [P, KC, T], F32R)
        m_lo = at("m_lo", 174, [P, KC, T], F32R)
        m_mid = at("m_mid", 190, [P, 2, T])
        m_tok = small[:, 76:80]
        neg_max = small[:, 80:84]
        p_sum = small[:, 84:88]
        p_inv = small[:, 88:92]
        gain_12 = small[:, 92:100]
        rs_all = at("rs_all", 46, [P, T])
        rs_tmp = at("rs_tmp", 48, [P, T])
        rn2 = at("rn2", 48, [P, T])
        rn2_hi = at("rn2_hi", 188, [P, T], F32R)
        rn2_lo = at("rn2_lo", 48, [P, T], F32R)
        v2 = at("v2", 50, [P, TT, P])
        qk2 = at("qk2", 52, [P, 5, T])
        q_stack = [b_hi, b_lo]
        k_twice = [at("k_twice0", 40, [P, T], F32R), at("k_twice1", 48, [P, T], F32R)]
        qk2_lo = at("qk2_lo", 52, [P, 5, T], F32R)
        tmp2 = at("tmp2", 42, [P, 2, T])
        vv = at("vv", 94, [P, TT, 512])
        u2 = at("u2", 102, [P, NF, T])
        ga = at("ga", 158, [P, NF, T])
        gb = at("gb", 166, [P, NF, T])
        ln = at("ln", 174, [P, 2, 512])
        spatial = at("spatial", 178, [P, NGRP, P])
        axial = at("axial", 182, [P, 2, T])
        b_sp = at("b_sp", 186, [P, NF, P])
        v2f = at("v2f", 188, [P, T])
        sq10 = at("sq10", 190, [P, 5, T])
        p2 = at("p2", 190, [P, 2, 2, T])
        p2_t = at("p2_t", 198, [P, TT, T])
        r2_tok = small[:, 100:108]
        ln_stats = small[:, 108:132]
        ln_mv = small[:, 132:140]
        ln_rs = small[:, 140:144]
        max2 = small[:, 144:146]
        sum2 = small[:, 146:148]
        inv2 = small[:, 148:150]
        gate = [at("gate_attn", 94, [P, KC, T]), at("gate_gmlp", 174, [P, KC, T])]
        y_mid = at("y_mid", 166, [P, 2, T])
        y_hi = at("y_hi", 62, [P, KC, T], F32R)
        y_lo = at("y_lo", 78, [P, KC, T], F32R)

        TOK_BANKS = ((4, 5, 3), (4, 5, 6))

        def t4(a):
            return a.rearrange("p (t c) -> p t c", t=TT)

        pair_mask = C("mask_pair").unsqueeze(1).broadcast_to([P, TT, P])
        ident4 = C("ident").unsqueeze(1).broadcast_to([P, TT, P])
        n_first = cst["ones"][1]

        block = ctx.enter_context(nc.Block())
        W = ins["weights"]

        @block.sync
        def _(sp):
            def load_x(i):
                sp.dma_start(x_in[:, 2 * i:2 * i + 2, :], ins["x"][:, 2 * i:2 * i + 2, :]).then_inc(S(f"x_loaded{i}"), 16)

            sp.dma_start(params[:], ins["params"]).then_inc(S("first_loaded"), 16)
            sp.dma_start(consts[:, 0:n_first], ins["consts"][:, 0:n_first]).then_inc(S("first_loaded"), 16)
            for s in range(4):
                sp.dma_start(w_raw[:, s, :], W[s]).then_inc(S(f"w_loaded{s}"), 16)
                if s == 0:
                    for i in range(4):
                        load_x(i)
                if s == 1:
                    sp.dma_start(pos[:], ins["pos"]).then_inc(S("pos_loaded"), 16)
                if s == 3:
                    sp.dma_start(consts[:, n_first:], ins["consts"][:, n_first:]).then_inc(S("masks_loaded"), 16)
                    sp.dma_start(lora[:], ins["lora"]).then_inc(S("masks_loaded"), 16)
                    sp.dma_start(g_up[:], ins["g_up"]).then_inc(S("masks_loaded"), 16)
            with sp.Fori(1, NSLAB // 4) as r:
                for k in range(4):
                    sp.wait_ge(S("slab_done"), r * 4 + (k - 3))
                    sp.dma_start(w_raw[:, k, :], W[r * 4 + k]).then_inc(S(f"w_loaded{k}"), 16)
            for s in range(NSLAB - NSLAB % 4, NSLAB):
                sp.wait_ge(S("slab_done"), s - 3)
                sp.dma_start(w_raw[:, s % 4, :], W[s]).then_inc(S(f"w_loaded{s % 4}"), 16)
            for n, name in [(n, "out_ready") for n in range(N_DVE_OUT)] + [(n, "out_ready2") for n in range(N_DVE_OUT, KC)]:
                sp.wait_ge(S(name), n + 1 if n < N_DVE_OUT else n + 1 - N_DVE_OUT)
                sp.dma_start(out[:, n, :], x_res[:, n, :]).then_inc(S("out_stored"), 16)
            sp.wait_ge(S("out_stored"), 16 * KC)

        @block.gpsimd
        def _(pool):
            def mul(o, a, b, name, op=ALU.mult):
                nc.gpsimd.tensor_tensor(o, a, b, op).then_inc(S(name), 1)

            def x_squares(kc):
                pool.wait_ge(S(f"x_loaded{kc // 2}"), 16)
                mul(sq_in[:, kc, :], x_in[:, kc, :], x_in[:, kc, :], "x_sq_pool")

            for s in range(NSLAB + 2):
                if s < NSLAB:
                    pool.wait_ge(S("w_hi_ready"), s + 1)
                    mul(w_lo[:, s % 4, :], w_raw[:, s % 4, :], hi_slot(s)[0].bitcast(F32), "w_lo_ready", ALU.subtract)
                if s == 0:
                    for kc in range(N_POOL_SQ):
                        x_squares(kc)
                        if kc > 0:
                            pool.wait_ge(S("x_sq_pool"), 2 * kc)
                            mul(sq_in[:, 0, :], sq_in[:, 0, :], sq_in[:, kc, :], "x_sq_pool", ALU.add)
                for f in {S_MK - 2: (0,), S_MK - 1: (1, 2, 3)}.get(s, ()):
                    pool.wait_ge(S("rk_ready"), f + 1)
                    pool.wait_ge(S("exps_ready"), f + 1)
                    mul(ax[:, f, :], ax[:, f, :], e_neg[:, f, :], "decayed")
                    mul(kx[:, f, :], kx[:, f, :], e_neg[:, f, :], "decayed")
                    mul(rx[:, f, :], rx[:, f, :], e_inc[:, f, :], "decayed")
                if s == S_MK + 1:
                    for n in range(8):
                        j = n % 4
                        pool.wait_ge(S("ab_ready"), n + 1)
                        if n >= 4:
                            pool.wait_ge(S("gh_done"), 4)
                        mul(t4(XT[:, j, :]), t4(AB[:, j, :]), pair_mask, "pair_ready")
                        pool.wait_ge(S("pair_ready"), n + 1)
                        mul(t4(XT[:, j, :]), t4(XT[:, j, :]), ident4, "xt0_ready", ALU.add)
                for k, s0 in enumerate((S_WOUT, S_XO, S_MLP + 16 * MLP_Q - KC, S_OUT2)):
                    n = s - 2 - s0
                    if 1 <= n <= KC - 2:
                        pool.wait_ge(S("sq_ready"), KC * k + n + 1)
                        if n > 1:
                            pool.wait_ge(S("sq_used"), (KC - 2) * k + n - 1)
                        elif k > 0:
                            pool.wait_ge(S("ssq_done"), k + 1)
                        mul(sq_sum[:, 0, :], sqb[:, 0, :] if n == 1 else sq_sum[:, 0, :], sqb[:, n % 2, :], "sq_used", ALU.add)
            pool.wait_ge(S("rstd_ready"), 5)
            for n in range(N_DVE_OUT, KC):
                pool.wait_ge(S("x_gained"), n + 1)
                mul(x_res[:, n, :], x_res[:, n, :], rstd[:], "out_ready2")

        @block.scalar
        def _(act):
            copy, exp, sigmoid, square, sqrt = ACT.Copy, ACT.Exp, ACT.Sigmoid, ACT.Square, ACT.Sqrt
            marks, last = {}, []

            def A(name):
                marks[name] = marks.get(name, 0) + 1
                last[:] = [name, marks[name]]
                return S(name)

            def actv(o, a, f, **kw):
                if last:
                    act.wait_ge(S(last[0]), last[1])
                return nc.scalar.activation(o, a, f, **kw)

            def split_hi(s):
                if s >= NSLAB:
                    return
                act.wait_ge(S(f"w_loaded{s % 4}"), 16 * (s // 4 + 1))
                high, before = hi_slot(s)
                if before >= 0:
                    act.wait_ge(S("slab_done"), before + 1)
                actv(high, w_raw[:, s % 4, :], copy).then_inc(A("w_hi_ready"), 1)

            def x_hi(kc):
                act.wait_ge(S(f"x_loaded{kc // 2}"), 16)
                actv(a_hi[:, kc, :], x_in[:, kc, :], copy, scale=V("norm_mix", kc)).then_inc(A("a_hi_ready"), 1)

            def x_squares(kc):
                actv(sq_in[:, kc, :], x_in[:, kc, :], square).then_inc(A("xn_sq"), 1)

            def load_table(f):
                actv(small[:, 150:151], sc[:, 0, NCH - 1:NCH], f).then_inc(A("act_step"), 1)

            act.wait_ge(S("dve_step"), 1)
            load_table(copy)
            act.wait_ge(S("first_loaded"), 32)
            split_hi(0)
            for kc in range(KC):
                x_hi(kc)
            split_hi(1)
            for kc in range(N_POOL_SQ, KC):
                x_squares(kc)
            act.wait_ge(S("ssq_done"), 1)
            actv(rstd[:], psum[7][:], sqrt, bias=C("eps6"), scale=1.0 / DM).then_inc(A("rms_ready"), 1)

            def exps(f):
                act.wait_ge(S("cum_done"), f + 1)
                bi, be = psum[2 + 2 * (f % 2)], psum[3 + 2 * (f % 2)]
                actv(e_inc[:, f, :], bi[:], exp).then_inc(A("act_step"), 1)
                actv(e_neg[:, f, :], bi[:], exp, scale=-1.0).then_inc(A("act_step"), 1)
                actv(e_exc[:, f, :], be[:], exp).then_inc(A("exps_ready"), 1)

            def swap_halves(j):
                act.wait_ge(S("tile_taken"), j + 1)
                if j >= 2:
                    act.wait_ge(S("rope_done"), j - 1)
                for r in range(0, P, HD // 2):
                    o = r ^ (HD // 2)
                    act.dma_start(rot[o:o + HD // 2, j % 2, :], qk[r:r + HD // 2, j, :]).then_inc(S(f"rot_loaded{j % 2}"), 16)

            def ret_part(j, k):
                return q_twice[k][:, j, :] if j < NF else k_stack[k][:, j - NF, :]

            def ret_hi(j):
                act.wait_ge(S("rope_done"), j + 1)
                for k in range(2):
                    r = slice(HD * k, HD * k + HD)
                    actv(ret_part(j, k)[r], qk[r, j, :], copy).then_inc(A("q_hi_ready"), 1)

            def ret_stack(j):
                act.wait_ge(S("q_lo_ready"), 2 * j + 2)
                act.wait_ge(S("q_hi_ready"), 2 * j + 2)
                for k in range(2):
                    r, other = slice(HD * k, HD * k + HD), slice(HD - HD * k, P - HD * k)
                    src = ret_part(j, k)[r] if j < NF else qk_lo[r, j, :]
                    act.dma_start(ret_part(j, k)[other].bitcast(F32), src.bitcast(F32)).then_inc(S("q_stacked"), 16)

            def silu(f):
                act.wait_ge(S("tile_taken"), S_RG + f + 1)
                actv(rg[:, f, :], rg[:, f, :], ACT.Silu).then_inc(A("silu_ready"), 1)

            for s in range(S_MK):
                split_hi(s + 2)
                if s == 1:
                    swap_halves(0)
                    act.wait_ge(S("angle_ready"), 1)
                    actv(sin_r[:], trig[:, 0, :], ACT.Sin).then_inc(A("act_step"), 1)
                    actv(trig[:, 1, :], trig[:, 0, :], ACT.Sin, scale=0.5).then_inc(A("sines_ready"), 1)
                if s == S_RV:
                    act.dma_start(w0[:], ins["w0"]).then_inc(S("decay_loaded"), 16)
                    act.dma_start(decay[:], ins["decay"]).then_inc(S("decay_loaded"), 16)
                if 1 <= s < S_RV:
                    swap_halves(s)
                if 3 <= s < 11:
                    ret_hi(s - 3)
                if 4 <= s < 12:
                    ret_stack(s - 4)
                if s > S_RG:
                    silu(s - S_RG - 1)
                if s in (S_RET + 2, S_RET + 4, S_RET + 6, S_RET + 8):
                    f = (s - S_RET) // 2 - 1
                    act.wait_ge(S("y_ret_step"), f + 1)
                    actv(qk[:, f, :], psum[6 + f % 2][:], copy).then_inc(A("y_ret_out"), 1)
                if s == S_G1:
                    act.wait_ge(S("low_ready"), 1)
                    actv(low[0:HD, 0, :], low[0:HD, 0, :], ACT.Tanh).then_inc(A("low_act"), 1)
                    act.wait_ge(S("low_ready"), 2)
                    actv(low[:, 1, :], low[:, 1, :], sigmoid).then_inc(A("low_act"), 1)
                if s == S_K:
                    act.wait_ge(S("low_ready"), 3)
                    actv(low[:, 2, :], low[:, 2, :], sigmoid).then_inc(A("low_act"), 1)
                if s in (S_PREP + 1, S_PREP + 2):
                    for i in (2 * (s - S_PREP) - 2, 2 * (s - S_PREP) - 1):
                        act.wait_ge(S("w0_added"), i + 1)
                        actv(lw[:, i, :], lw[:, i, :], sigmoid).then_inc(A("lora_ready"), 1)
                        act.wait_ge(S("lora_done"), 2 * i + 2)
                        actv(ax[:, i, :], psum[4 + i % 2][:], sigmoid, bias=V("a0", i)).then_inc(A("lora_ready"), 1)
                if s in (S_PREP + 3, S_PREP + 4):
                    for f in (2 * (s - S_PREP) - 6, 2 * (s - S_PREP) - 5):
                        act.wait_ge(S("lora_done"), 2 * NF + f + 1)
                        actv(gx[:, f, :], psum[6 + f % 2][:], copy).then_inc(A("lora_ready"), 1)
                if s == S_PREP + 3:
                    for f in range(NF):
                        act.wait_ge(S("gn_cent_done"), f + 1)
                        actv(qk[:, 4 + f, :], psum[2 + f][:], copy).then_inc(A("gn_cent"), 1)
                        actv(qk[:, f, :], psum[2 + f][:], square).then_inc(A("gn_sq"), 1)
                if s == S_PREP + 4:
                    for f in range(NF):
                        act.wait_ge(S("kk0_ready"), f + 1)
                        actv(sqk[:, f, :], kk[:, f, :], square).then_inc(A("sqk_ready"), 1)
                if s == S_PREP + 5:
                    act.wait_ge(S("var_done"), 1)
                    actv(kg_sd[0:16, :], psum[6][0:16, :], sqrt, bias=C("kg_eps")[0:16], scale=C("kg_scale")[0:16]).then_inc(A("sd_ready"), 1)
                if s == S_PREP + 6:
                    exps(0)
                    exps(1)
                if s in (S_PREP + 7, S_PREP + 8):
                    exps(s - S_PREP - 5)

            def tok(g):
                n = 8 * g
                for dst in (v_tok, GH, b_tok, k_tok):
                    for h in range(2):
                        n += 1
                        act.wait_ge(S("tok_done"), n)
                        src = psum[TOK_BANKS[g][(n - 1 - 8 * g) % 3]][:]
                        if dst is GH:
                            actv(GH[:, :, 2 * h:2 * h + 2, 0, :].rearrange("p j t e -> p t j e"),
                                 src.rearrange("p (t j e) -> p t j e", t=2, j=4), copy).then_inc(A("tok_ready"), 1)
                        else:
                            actv(dst[:, 2 * h:2 * h + 2, 256 * g:256 * g + 256],
                                 src.rearrange("p (t e) -> p t e", t=2), copy).then_inc(A("tok_ready"), 1)

            def memory_hi(kc):
                if kc == 0:
                    act.wait_ge(S("mem_loaded"), 16)
                    act.wait_ge(S("rk_mm_done"), 8)
                actv(mem_hi[:, kc, :], mem_in[:, kc, :], copy, scale=V("norm_mem", kc)).then_inc(A("mem_hi_ready"), 1)

            tok(0)
            silu(NF - 1)
            for g in range(2):
                for j in range(4):
                    act.wait_ge(S("u_done"), 4 * g + j + 1)
                    actv(GH[:, j, :, 1, :], psum[2 * j][:, 0:256].rearrange("p (t e) -> p t e", t=TT),
                         copy).then_inc(A("u_ready"), 1)
                    act.wait_ge(S("x0_done"), 4 * g + j + 1)
                    actv(X[:, j, :], psum[2 * j + 1][:], copy).then_inc(A("x0_ready"), 1)
                for lv in range(4):
                    for j in range(4):
                        act.wait_ge(S("xt_done"), 4 * (4 * g + lv) + j + 1)
                        actv(XT[:, j, :], psum[2 * j][:], copy).then_inc(A("xt_ready"), 1)
                    if g == 1:
                        memory_hi(2 * lv)
                        memory_hi(2 * lv + 1)
                for j in range(4):
                    act.wait_ge(S("gh_done"), 4 * g + j + 1)
                    actv(GH[:, j].rearrange("p t k e -> p (t k e)"), psum[2 * j][:], copy).then_inc(A("gh_ready"), 1)
                if g == 0:
                    tok(1)
                    act.wait_ge(S("tok_done"), 16)
                    act.wait_ge(S("prep_ready"), NF)
                    act.dma_start(mem_in[:], ins["mem"]).then_inc(S("mem_loaded"), 16)
                else:
                    for kc in range(KC):
                        act.wait_ge(S("mem_lo_ready"), kc + 1)
                        actv(mem_in[:, kc, :], mem_in[:, kc, :], square).then_inc(A("mem_sq_ready"), 1)
                for i in range(2):
                    act.wait_ge(S("y_rwkv_done"), 2 * g + i + 1)
                    actv(rx[:, 2 * g + i, :], psum[2 + 5 * i][:], copy).then_inc(A("y_rwkv_out"), 1)
            for i in range(4):
                act.dma_start(x_res[:, 2 * i:2 * i + 2, :], ins["x"][:, 2 * i:2 * i + 2, :]).then_inc(S(f"x_loaded{i}"), 16)
            act.wait_ge(S("mem_ssq_done"), 1)
            actv(mem_rs[:], psum[3][:, 0:MEM], sqrt, bias=C("eps6"), scale=1.0 / DM).then_inc(A("mem_rms"), 1)
            for f in range(NF):
                act.wait_ge(S("gn_cent_done"), NF + f + 1)
                actv(kx[:, f, :], psum[4 + f][:], copy).then_inc(A("gn_cent"), 1)
                actv(gsq[:, f, :], psum[4 + f][:], square).then_inc(A("gn_sq"), 1)
            split_hi(S_MK + 2)
            split_hi(S_MK + 3)
            act.wait_ge(S("var_done"), 2)
            actv(hsd[0:8, :], psum[2][0:8, :], sqrt, bias=C("eps64")[0:8], scale=1.0 / HD).then_inc(A("sd_ready"), 1)
            split_hi(S_MK + 4)
            for s in range(S_MK + 2, S_WOUT - 1):
                split_hi(s + 3)
                c = s - S_MK - 2
                if c < 4:
                    actv(a_hi[:, c, :], rg[:, c, :], copy).then_inc(A("a_hi_ready"), 1)
                elif c < KC:
                    act.wait_ge(S("y_ready"), c - 3)
                    actv(a_hi[:, c, :], kx[:, c - 4, :], copy).then_inc(A("a_hi_ready"), 1)

            def squares(n, k):
                if n >= 2:
                    act.wait_ge(S("sq_used"), (KC - 2) * k + max(1, n - 2))
                actv(sqb[:, n % 2, :], x_res[:, n, :], square).then_inc(A("sq_ready"), 1)

            def residual(s0, gain, k, ahead):
                load_table(sqrt)
                for n in range(KC):
                    split_hi(s0 + n + ahead)
                    act.wait_ge(S("tile_taken"), s0 + n + 1)
                    actv(b_hi[:, n, :], x_res[:, n, :], copy, scale=V(gain, n)).then_inc(A("b_hi_ready"), 1)
                    squares(n, k)

            residual(S_WOUT, "norm_xattn", 0, 2)
            act.wait_ge(S("ssq_done"), 1 + 1)
            actv(rstd[:], psum[7][:], sqrt, bias=C("eps6"), scale=1.0 / DM).then_inc(A("rms_ready"), 1)

            def xattn_exp(h):
                for t in range(TT):
                    act.wait_ge(S("xmax_ready"), 2 * h + t // 2 + 1)
                    actv(prob[:, h % 2, t, :], psum[2 + t // 2][:, (t % 2) * MEM:(t % 2 + 1) * MEM], exp,
                         bias=neg_max[:, t:t + 1], accum_out=p_sum[:, t:t + 1]).then_inc(A("xexp_ready"), 1)

            def xattn_transposed(h):
                for m in range(MEM // P):
                    act.wait_ge(S("xprob_t_done"), 2 * h + m + 1)
                    actv(prob_t[:, h % 2, m, :], psum[4 + m][:], copy).then_inc(A("xprob_t_ready"), 1)

            def xattn_out(h):
                for d in range(2):
                    act.wait_ge(S("xo_done"), 2 * h + d + 1)
                    actv(a_hi[:, 2 * h + d, :], psum[6 + d][:], copy).then_inc(A("a_hi_ready"), 1)

            for s in range(S_XQ, S_XO):
                split_hi(s + 2)
                if (s - S_XQ) % 2 == 1:
                    h = (s - S_XQ) // 2
                    if h >= 1:
                        xattn_transposed(h - 1)
                    xattn_exp(h)
                    if h >= 1:
                        xattn_out(h - 1)
            act.wait_ge(S("xs_done"), 2 * XH)
            split_hi(S_XO + 2)
            xattn_transposed(XH - 1)
            xattn_out(XH - 1)
            residual(S_XO, "norm_mlp", 1, 3)
            act.wait_ge(S("ssq_done"), 1 + 2)
            actv(rstd[:], psum[7][:], sqrt, bias=C("eps6"), scale=1.0 / DM).then_inc(A("rms_ready"), 1)
            for q in range(MLP_Q):
                for n in range(KC):
                    split_hi(S_MLP + 16 * q + n + 3)
                    act.wait_ge(S("m_ready"), KC * q + n + 1)
                    actv(m_hi[:, n, :], m_mid[:, n % 2, :], copy).then_inc(A("m_hi_ready"), 1)
                if q == MLP_Q - 1:
                    load_table(sqrt)
                for n in range(KC):
                    if q < MLP_Q - 1 or n < KC - 1:
                        split_hi(S_MLP + 16 * q + 8 + n + 3)
                    if q == MLP_Q - 1:
                        act.wait_ge(S("tile_taken"), S_MLP + 16 * q + 8 + n + 1)
                        if n == 0:
                            act.wait_ge(S("column_ready"), 2)
                        actv(a_hi[:, n, :], x_res[:, n, :], copy, scale=gain_12[:, n:n + 1]).then_inc(A("a_hi_ready"), 1)
                        squares(n, 2)
                        if n >= 2:
                            act.wait_ge(S("sqg_used"), max(1, n - 2))
                        actv(sqg[:, n % 2, :], x_res[:, n, :], square, scale=V("norm_final", n)).then_inc(A("sqg_ready"), 1)
            act.dma_start(ln[:], ins["ln"]).then_inc(S("tables_loaded"), 16)
            act.dma_start(spatial[:], ins["spatial"]).then_inc(S("tables_loaded"), 16)
            act.dma_start(axial[:], ins["axial"]).then_inc(S("tables_loaded"), 16)
            act.dma_start(b_sp[:], ins["b_sp"]).then_inc(S("tables_loaded"), 16)

            def attn_exp(i):
                for k in range(2):
                    act.wait_ge(S("max2_ready"), 2 * i + k + 1)
                    if i >= 2 and k == 0:
                        act.wait_ge(S("p2_t_done"), i - 1)
                    actv(p2[:, i % 2, k, :], psum[2 + k][:], exp, bias=max2[:, k:k + 1],
                         accum_out=sum2[:, k:k + 1]).then_inc(A("exp2_ready"), 1)

            def attn_t(i):
                for k in range(2):
                    act.wait_ge(S("p2_t_done"), i + 1)
                    if i % 2 == 0 and i >= 2 and k == 0:
                        act.wait_ge(S("o2_done"), i // 2)
                    actv(p2_t[:, 2 * k:2 * k + 2, (i % 2) * 256:(i % 2) * 256 + 256],
                         psum[4 + k][:].rearrange("p (c t) -> p c t", c=2), copy).then_inc(A("p2_t_ready"), 1)

            def stack(f, k):
                return k_twice[k][:] if f == 4 else q_stack[k][:, f, :]

            def head_hi(f):
                act.wait_ge(S("qk2_ready"), f + 1)
                for k in range(2):
                    r = slice(HD * k, HD * k + HD)
                    actv(stack(f, k)[r], qk2[r, f, :], copy).then_inc(A("q_hi_ready"), 1)

            def head_stack(f):
                act.wait_ge(S("q_lo_ready"), 16 + 2 * f + 2)
                act.wait_ge(S("q_hi_ready"), 16 + 2 * f + 2)
                for k in range(2):
                    r, other = slice(HD * k, HD * k + HD), slice(HD - HD * k, P - HD * k)
                    src = stack(f, k)[r] if f == 4 else qk2_lo[r, f, :]
                    act.dma_start(stack(f, k)[other].bitcast(F32), src.bitcast(F32)).then_inc(S("q_stacked"), 16)

            for s in range(S_VIN, S_PROJ):
                split_hi(s + 2)
                for f in {S_U + 3: (0, 1), S_GA: (2,), S_GA + 1: (3,), S_GA + 2: (4,)}.get(s, ()):
                    head_hi(f)
                for f in {S_GA: (0, 1), S_GA + 1: (2,), S_GA + 2: (3,), S_GA + 3: (4,)}.get(s, ()):
                    head_stack(f)
                if s == S_VIN:
                    act.wait_ge(S("ssq_done"), 3 + 1)
                    actv(rstd[:], psum[7][:], sqrt, bias=C("eps6"), scale=1.0 / DM).then_inc(A("rms_ready"), 1)
                if s == S_VIN + 1:
                    act.wait_ge(S("mid_var_ready"), 1)
                    actv(rs_all[:], rs_tmp[:], sqrt, bias=C("eps6"), scale=1.0 / DM).then_inc(A("rms3_ready"), 1)
                if s == S_V2:
                    act.wait_ge(S("tile_taken"), S_V2)
                    for t in range(TT):
                        actv(vv[:, t, :], vv[:, t, :], ACT.Gelu_apprx_tanh).then_inc(A("gelu_ready"), 1)
                if s == S_K2 + 1:
                    act.wait_ge(S("ln_mv_ready"), TT)
                    actv(ln_rs, ln_mv.rearrange("p (t k) -> p t k", k=2)[:, :, 1], sqrt, bias=C("eps6")).then_inc(A("sd_ready"), 1)
                if S_K2 <= s < S_U:
                    f = (s - S_K2 + 4) % 5
                    act.wait_ge(S("tile_taken"), s + 1)
                    actv(sq10[:, f, :], qk2[:, f, :], square).then_inc(A("sq10_ready"), 1)
                if s == S_U:
                    act.wait_ge(S("var_done"), 3)
                    actv(rn2[0:10, :], psum[6][0:10, :], sqrt, bias=C("eps6")[0:10], scale=1.0 / HD).then_inc(A("sd_ready"), 1)
                if S_U < s <= S_GA:
                    f = s - S_U - 1
                    act.wait_ge(S("tile_taken"), S_U + f + 1)
                    actv(u2[:, f, :], u2[:, f, :], ACT.Gelu_apprx_tanh).then_inc(A("gelu_ready"), 1)
                if S_GA < s <= S_GB:
                    f = s - S_GA - 1
                    act.wait_ge(S("tile_taken"), S_GA + f + 1)
                    actv(ga[:, f, :], ga[:, f, :], ACT.Silu).then_inc(A("silu_ready"), 1)
                if S_GB < s <= S_MERGE:
                    f = s - S_GB - 1
                    act.wait_ge(S("tile_taken"), S_GB + f + 1)
                    actv(gb[:, f, :], gb[:, f, :], ACT.Silu).then_inc(A("silu_ready"), 1)
                i = s - S_ATTN
                if 1 <= i <= 2 * QH:
                    attn_t(i - 1)
                if 0 <= i < 2 * QH:
                    attn_exp(i)
                if s >= S_MERGE:
                    m = s - S_MERGE
                    act.wait_ge(S("tile_taken"), s + 1)
                    actv(gate[m // KC][:, m % KC, :], gate[m // KC][:, m % KC, :], sigmoid, bias=V("b_merge", m)).then_inc(A("gate_ready"), 1)
                if S_GB < s <= S_MERGE:
                    f = s - S_GB - 1
                    act.wait_ge(S("gm_ready"), f + 1)
                    actv(b_hi[:, NF + f, :], tmp2[:, f % 2, :], copy).then_inc(A("branch_hi"), 1)
                if i >= 5 and i % 4 == 1:
                    f = i // 4 - 1
                    act.wait_ge(S("oa_ready"), f + 1)
                    actv(b_hi[:, f, :], ga[:, f, :], copy).then_inc(A("branch_hi"), 1)
            for n in range(KC):
                split_hi(S_PROJ + n + 2)
                act.wait_ge(S("y_mid_ready"), n + 1)
                actv(y_hi[:, n, :], y_mid[:, 0, :], copy).then_inc(A("ym_hi"), 1)
            load_table(sqrt)
            for n in range(KC):
                split_hi(S_OUT2 + n + 2)
                act.wait_ge(S("tile_taken"), S_OUT2 + n + 1)
                squares(n, 3)
                actv(x_res[:, n, :], x_res[:, n, :], copy, scale=V("final_gain", n)).then_inc(A("x_gained"), 1)
            act.wait_ge(S("ssq_done"), 4 + 1)
            actv(rstd[:], psum[7][:], sqrt, bias=C("eps6"), scale=1.0 / DM).then_inc(A("rms_ready"), 1)

        @block.vector
        def _(dve):
            marks, last = {}, []

            def D(name, n=1):
                marks[name] = marks.get(name, 0) + n
                last[:] = [name, marks[name]]
                return S(name)

            def hold():
                if last:
                    dve.wait_ge(S(last[0]), last[1])

            def step(ins):
                return ins.then_inc(D("dve_step"), 1)

            def tt(o, a, b, op):
                hold()
                return nc.vector.tensor_tensor(o, a, b, op)

            def ts(o, a, s1, s2, op0, op1=ALU.bypass):
                hold()
                return nc.vector.tensor_scalar(o, a, s1, s2, op0, op1)

            def stt(o, a, s1, b, op0, op1):
                hold()
                return nc.vector.scalar_tensor_tensor(out=o, in0=a, scalar=s1, in1=b, op0=op0, op1=op1)

            def cp(o, a):
                hold()
                return nc.vector.tensor_copy(o, a)

            def recip(o, a):
                hold()
                return nc.vector.reciprocal(o, a)

            def split(hi, lo, a):
                step(cp(hi, a))
                return tt(lo, a, hi.bitcast(F32), ALU.subtract)

            def x_lo(kc):
                dve.wait_ge(S("a_hi_ready"), kc + 1)
                stt(a_lo[:, kc, :], x_in[:, kc, :], V("norm_mix", kc), a_hi[:, kc, :].bitcast(F32),
                    ALU.mult, ALU.subtract).then_inc(D("a_lo_ready"), 1)

            def x_square_sum(kc):
                dve.wait_ge(S("xn_sq"), kc - N_POOL_SQ + 1)
                total = sq_in[:, N_POOL_SQ, :]
                tt(total, total, sq_in[:, kc, :], ALU.add).then_inc(D("x_sq_sum"), 1)

            step(nc.vector.memset(sc[:, :, NCH - 1:NCH], 1.0))
            step(nc.vector.memset(shift[:, :, 0:1], 0.0))
            dve.wait_ge(S("first_loaded"), 32)
            ka = par["k_a"][0]
            step(ts(one_ka, params[:, ka:ka + 4], -1.0, 1.0, ALU.mult, ALU.add))
            for kc in range(KC):
                x_lo(kc)
            for kc in range(N_POOL_SQ + 1, KC):
                x_square_sum(kc)

            c1, two_pi = 6.28125, 6.283185307179586
            magic = 1.5 * 2.0 ** 23
            dve.wait_ge(S("pos_loaded"), 16)
            step(cp(trig[:, 0, :], pos[:]))
            step(ts(trig[:, 1, :], trig[:, 0, :], C("inv_freq"), None, ALU.mult))
            step(ts(trig[:, 2, :], trig[:, 1, :], 1.0 / two_pi, magic, ALU.mult, ALU.add))
            step(ts(trig[:, 3, :], trig[:, 2, :], -magic, None, ALU.add))
            dve.wait_ge(S("rms_ready"), 1)
            recip(rstd[:], rstd[:]).then_inc(D("rstd_ready"), 1)

            def rope(j):
                dve.wait_ge(S(f"rot_loaded{j % 2}"), 16 * 4 * (j // 2 + 1))
                step(tt(tmp[:, 0, :], rot[:, j % 2, :], sin_r[:], ALU.mult))
                step(tt(qk[:, j, :], qk[:, j, :], cos_r[:], ALU.mult))
                tt(qk[:, j, :], qk[:, j, :], tmp[:, 0, :], ALU.add).then_inc(D("rope_done"), 1)

            def ret_lo(j):
                for k in range(2):
                    r = slice(HD * k, HD * k + HD)
                    dve.wait_ge(S("q_hi_ready"), 2 * j + k + 1)
                    high = q_twice[k][r, j, :] if j < NF else k_stack[k][r, j - NF, :]
                    tt(qk_lo[r, j, :], qk[r, j, :], high.bitcast(F32), ALU.subtract).then_inc(D("q_lo_ready"), 1)

            def masked_scores(h):
                off = 0
                dve.wait_ge(S("s_ret_done"), h + 1)
                if h >= 2:
                    dve.wait_ge(S("y_ret_step"), h // 2)
                for j in range(TT):
                    w = T - P * j
                    src = psum[(2, 3, 4, 3)[j]][:, (384 if j == 3 else 0):(384 if j == 3 else 0) + w]
                    tt(s_ret[:, h % 2, off:off + w], src, decay[:, h, 0:w], ALU.mult).then_inc(D("s_ret_ready"), 1)
                    off += w

            def head_norm(f):
                dve.wait_ge(S("gn_spread_done"), f + 1)
                step(tt(qk[:, 4 + f, :], qk[:, 4 + f, :], psum[6 + f % 2][:], ALU.mult))
                ts(qk[:, 4 + f, :], qk[:, 4 + f, :], V("ret_gn_w", f), V("ret_gn_b", f), ALU.mult, ALU.add).then_inc(D("ret_ready"), 1)

            def ret_gate(f):
                dve.wait_ge(S("silu_ready"), f + 1)
                step(tt(rg[:, f, :], rg[:, f, :], qk[:, 4 + f, :], ALU.mult))

            def prep(f):
                dve.wait_ge(S("kk_done"), f + 1)
                tt(kk[:, f, :], kk[:, f, :], psum[6 + f % 2][:], ALU.mult).then_inc(D("kk_ready"), 1)
                step(ts(pt[:, 0, :], ax[:, f, :], V("k_a", f), one_ka[:, f:f + 1], ALU.mult, ALU.add))
                step(tt(ax[:, f, :], ax[:, f, :], kk[:, f, :], ALU.mult))
                step(tt(kx[:, f, :], kx[:, f, :], pt[:, 0, :], ALU.mult))
                if f > 0:
                    dve.wait_ge(S("bonus_done"), f)
                stt(pt[:, 1, :], rx[:, f, :], V("r_k", f), kx[:, f, :], ALU.mult, ALU.mult).then_inc(D("rk_ready"), 1)
                dve.wait_ge(S("exps_ready"), f + 1)
                stt(kk[:, f, :], kk[:, f, :], -1.0, e_exc[:, f, :], ALU.mult, ALU.mult).then_inc(D("a_ready"), 1)
                step(recip(sr[:, f, 0:NCH - 1], e_exc[:, f, :].rearrange("p (c t) -> p c t", c=NCH)[:, 1:NCH, 0]))
                step(tt(sc[:, f, 0:NCH - 1], e_inc[:, f, :].rearrange("p (c t) -> p c t", c=NCH)[:, 0:NCH - 1, CH - 1],
                        sr[:, f, 0:NCH - 1], ALU.mult))

            def bonus(f):
                dve.wait_ge(S("bonus_done"), f + 1)
                tt(bon[:, f, :], psum[6 + f % 2][:], vx[:, f, :], ALU.mult).then_inc(D("prep_ready"), 1)

            mixed = [(low, 0), (low, 1), (low, 2)] + [(d, f) for d in (kx, rx, vx) for f in range(NF)]
            for s in range(S_MK):
                if S_RV <= s < S_WA - 1:
                    if s == S_RV:
                        rope(7)
                    if s < S_RV + 3:
                        ret_lo(s - 3)
                    continue
                dve.wait_ge(S("slab_done"), s + 1)
                bank = psum[s % 2]
                if s < S_RV:
                    tt(qk[:, s, :], bank[:], rstd[:], ALU.mult).then_inc(D("tile_taken"), 1)
                    if s == 0:
                        step(stt(trig[:, 1, :], trig[:, 3, :], -c1, trig[:, 1, :], ALU.mult, ALU.add))
                        step(stt(trig[:, 1, :], trig[:, 3, :], c1 - two_pi, trig[:, 1, :], ALU.mult, ALU.add))
                        ts(trig[:, 0, :], trig[:, 1, :], -3.1415925, 3.1415925, ALU.max, ALU.min).then_inc(D("angle_ready"), 1)
                    if s == 1:
                        dve.wait_ge(S("sines_ready"), 1)
                        step(tt(trig[:, 2, :], trig[:, 1, :], trig[:, 1, :], ALU.mult))
                        step(ts(cos_r[:], trig[:, 2, :], -2.0, 1.0, ALU.mult, ALU.add))
                    if s >= 1:
                        rope(s - 1)
                    if s >= 3:
                        ret_lo(s - 3)
                    if s == 5:
                        dve.wait_ge(S("column_done"), 1)
                        cp(r_tok[:], psum[5][:, 0:8]).then_inc(D("column_ready"), 1)
                elif s < S_WA:
                    for t in range(TT):
                        ts(v_ret[:, t, :], psum[4 + t][:], r_tok[:, 2 * t:2 * t + 1], None, ALU.mult).then_inc(D("tile_taken"), 1)
                elif s >= S_RG:
                    tt(rg[:, s - S_RG, :], bank[:], rstd[:], ALU.mult).then_inc(D("tile_taken"), 1)
                else:
                    j = s - S_WA
                    cur, prev = shift[:, j % 2, 1:T + 1], shift[:, j % 2, 0:T]
                    tt(cur, bank[:], rstd[:], ALU.mult).then_inc(D("tile_taken"), 1)
                    step(tt(tmp[:, 0, :], prev, cur, ALU.subtract))
                    dst, f = mixed[j]
                    stt(dst[:, f, :], tmp[:, 0, :], V("mu", j), cur, ALU.mult, ALU.add).then_inc(
                        D("low_ready" if j < 3 else "mix_ready"), 1)
                if s == S_RET:
                    dve.wait_ge(S("masks_loaded"), 48)
                    step(cp(spread_r[:], C("spread")))
                    dve.wait_ge(S("decay_loaded"), 32)
                if S_RET <= s < S_RET + RH:
                    masked_scores(s - S_RET)
                for i in ((0, 1) if s == S_PREP + 1 else (2, 3) if s == S_PREP + 2 else ()):
                    dve.wait_ge(S("decay_loaded"), 32)
                    dve.wait_ge(S("lora_done"), 2 * i + 1)
                    tt(lw[:, i, :], psum[2 + i % 2][:], w0[:], ALU.add).then_inc(D("w0_added"), 1)
                if s == S_PREP + 2:
                    dve.wait_ge(S("y_ret_step"), NF)
                for f in ((0, 1, 2) if s == S_PREP + 2 else (3,) if s == S_PREP + 3 else ()):
                    ts(kk[:, f, :], kx[:, f, :], V("k_k", f), None, ALU.mult).then_inc(D("kk0_ready"), 1)
                if s == S_PREP + 5:
                    dve.wait_ge(S("sd_ready"), 1)
                    step(ts(kg_rn[0:16, :], kg_sd[0:16, :], C("kg_min")[0:16], None, ALU.max))
                    step(recip(kg_rn[0:16, :], kg_rn[0:16, :]))
                    split(kg_hi[0:16, :], kg_lo[0:16, :], kg_rn[0:16, :]).then_inc(D("rn_ready"), 1)
                if s in (S_PREP + 6, S_PREP + 7):
                    head_norm(2 * (s - S_PREP) - 12)
                    head_norm(2 * (s - S_PREP) - 11)
                if s >= S_RG:
                    f = s - S_RG
                    if f >= 1:
                        bonus(f - 1)
                    prep(f)
                    if f >= 1:
                        ret_gate(f - 1)
            bonus(NF - 1)

            strict = C("mask_strict").unsqueeze(1).broadcast_to([P, TT, P])
            inc = C("mask_inc").unsqueeze(1).broadcast_to([P, TT, P])

            for g in range(2):
                if g == 1:
                    dve.wait_ge(S("y_rwkv_done"), 2)
                for j in range(4):
                    n = 4 * g + j
                    if g == 0:
                        dve.wait_ge(S("decayed"), 3 * (j + 1))
                    dve.wait_ge(S("ab_done"), n + 1)
                    tt(t4(AB[:, j, :]), t4(psum[2 * j][:]), strict, ALU.mult).then_inc(D("ab_ready"), 1)
                    dve.wait_ge(S("ak_done"), n + 1)
                    tt(t4(AK[:, j, :]), t4(psum[2 * j + 1][:]), strict, ALU.mult).then_inc(D("ak_ready"), 1)
                if g == 0:
                    ret_gate(NF - 1)
                for j in range(4):
                    n = 4 * g + j
                    dve.wait_ge(S("rb_done"), n + 1)
                    tt(t4(RB[:, j, :]), t4(psum[2 * j][:]), inc, ALU.mult).then_inc(D("rb_ready"), 1)
                    dve.wait_ge(S("rk_mm_done"), n + 1)
                    tt(t4(RK[:, j, :]), t4(psum[2 * j + 1][:]), inc, ALU.mult).then_inc(D("rkm_ready"), 1)
                for lv in range(5):
                    mask = C("mask_level", lv * P, P).unsqueeze(1).broadcast_to([P, TT, P])
                    for j in range(4):
                        n = 4 * (5 * g + lv) + j
                        dve.wait_ge(S("nx_done"), n + 1)
                        tt(t4(PX[:, j, :]), t4(psum[2 * j][:]), mask, ALU.mult).then_inc(D("px_ready"), 1)
                    for j in range(4):
                        n = 4 * (5 * g + lv) + j
                        dve.wait_ge(S("xp_done"), n + 1)
                        dst = XT if lv == 4 else X
                        if lv == 4:
                            dve.wait_ge(S("xt_ready"), 4 * (4 * g + 3) + j + 1)
                        tt(dst[:, j, :], dst[:, j, :], psum[2 * j + 1][:], ALU.add).then_inc(D("xn_ready"), 1)
                    if g == 1 and lv >= 1:
                        for kc in (2 * lv - 2, 2 * lv - 1):
                            dve.wait_ge(S("mem_hi_ready"), kc + 1)
                            stt(mem_lo[:, kc, :], mem_in[:, kc, :], V("norm_mem", kc), mem_hi[:, kc, :].bitcast(F32),
                                ALU.mult, ALU.subtract).then_inc(D("mem_lo_ready"), 1)
                def halves(a, i, u, n):
                    return a[:, i].rearrange("p (t u) e -> p t u e", u=2)[:, 0:n, u, :]

                for i in range(2):
                    f = 2 * g + i
                    dve.wait_ge(S("qt_done"), f + 1)
                    tt(QT[:, i, :], psum[1 + 2 * i][:], rx[:, f, :], ALU.add).then_inc(D("qt_ready"), 1)
                for i in range(2):
                    f = 2 * g + i
                    dve.wait_ge(S("at_done"), f + 1)
                    for u, n in ((0, 4), (1, 3)):
                        tt(halves(AT, i, u, n), psum[(4, 0)[i] + 2 * u][:, 0:n * HD].rearrange("p (c e) -> p c e", c=n),
                           C("ident2").unsqueeze(1).broadcast_to([P, n, HD]), ALU.add).then_inc(D("at_ready"), 1)
                    dve.wait_ge(S("bc_done"), f + 1)
                    for u, n in ((0, 4), (1, 3)):
                        scale = sc[:, f, :].rearrange("p (t u) -> p t u", u=2)[:, 0:n, u].unsqueeze(2).broadcast_to([P, n, HD])
                        tt(halves(BC, i, u, n), psum[(5, 1)[i] + 2 * u][:, 0:n * HD].rearrange("p (c e) -> p c e", c=n),
                           scale, ALU.mult).then_inc(D("bc_ready"), 1)
                cp(ST[:, 1], BC[:, :, 0, :]).then_inc(D("state_ready"), 1)
                for c in range(1, NCH - 1):
                    dve.wait_ge(S("state_done"), 6 * g + c)
                    for i in range(2):
                        nc.vector.scalar_tensor_tensor(
                            out=ST[:, c + 1, i], in0=psum[0][:, i * HD:(i + 1) * HD], scalar=sc[:, 2 * g + i, c:c + 1],
                            in1=BC[:, i, c, :], op0=ALU.mult, op1=ALU.add).then_inc(D("state_ready"), 1)
            gain12 = params[:, par["norm_final"][0]:par["norm_final"][1]]
            tt(gain_12, gain12, params[:, par["norm_gain_2"][0]:par["norm_gain_2"][1]], ALU.mult).then_inc(D("column_ready"), 1)

            def head_norm2(f):
                dve.wait_ge(S("gn_spread_done"), NF + f + 1)
                step(tt(kx[:, f, :], kx[:, f, :], psum[4 + f][:], ALU.mult))
                step(ts(kx[:, f, :], kx[:, f, :], V("gn_w", f), V("gn_b", f), ALU.mult, ALU.add))
                step(tt(kx[:, f, :], kx[:, f, :], bon[:, f, :], ALU.add))
                tt(kx[:, f, :], kx[:, f, :], gx[:, f, :], ALU.mult).then_inc(D("y_ready"), 1)

            def mixer_lo(c):
                dve.wait_ge(S("a_hi_ready"), KC + c + 1)
                y = rg[:, c, :] if c < 4 else kx[:, c - 4, :]
                tt(a_lo[:, c, :], y, a_hi[:, c, :].bitcast(F32), ALU.subtract).then_inc(D("a_lo_ready"), 1)

            dve.wait_ge(S("mem_rms"), 1)
            recip(mem_rs[:], mem_rs[:]).then_inc(D("mem_rstd"), 1)
            for n in range(KC):
                s = S_MK + n
                dve.wait_ge(S("slab_done"), s + 1)
                tt(mem_k[:, n, :], psum[s % 2][:, 0:MEM], mem_rs[:], ALU.mult).then_inc(D("tile_taken"), 1)
                if n == 1:
                    dve.wait_ge(S("sd_ready"), 2)
                    step(recip(hrn[0:8, :], hsd[0:8, :]))
                    split(hrn_hi[0:8, :], hrn_lo[0:8, :], hrn[0:8, :]).then_inc(D("rn_ready"), 1)
                if n >= 4:
                    head_norm2(n - 4)
            for c in range(KC):
                mixer_lo(c)
            dve.wait_ge(S("column_done"), 1 + 1)
            cp(m_tok, psum[6][:, 0:4]).then_inc(D("column_ready"), 1)
            dve.wait_ge(S("slab_done"), S_WOUT)
            for m in range(MEM // P):
                for k in range(2):
                    ts(mem_v[:, m, k * 512:(k + 1) * 512], psum[2 + 2 * m + k][:], m_tok[:, 2 * m:2 * m + 1], None,
                       ALU.mult).then_inc(D("tile_taken", 2), 2)

            def residual(s0, gain, k):
                for n in range(KC):
                    dve.wait_ge(S("slab_done"), s0 + n + 1)
                    if k == 0:
                        dve.wait_ge(S(f"x_loaded{n // 2}"), 32)
                    tt(x_res[:, n, :], psum[(s0 + n) % 2][:], x_res[:, n, :], ALU.add).then_inc(D("tile_taken"), 1)
                    dve.wait_ge(S("b_hi_ready"), KC * k + n + 1)
                    stt(b_lo[:, n, :], x_res[:, n, :], V(gain, n), b_hi[:, n, :].bitcast(F32),
                        ALU.mult, ALU.subtract).then_inc(D("b_lo_ready"), 1)

            residual(S_WOUT, "norm_xattn", 0)
            dve.wait_ge(S("rms_ready"), 1 + 1)
            recip(rstd[:], rstd[:]).then_inc(D("rstd_ready"), 1)

            def xattn_softmax(h):
                for k in range(2):
                    dve.wait_ge(S("xs_done"), 2 * h + k + 1)
                    hold()
                    nc.vector.tensor_reduce(neg_max[:, 2 * k:2 * k + 2], psum[2 + k][:].rearrange("p (t m) -> p t m", t=2),
                                            axis=AX.X, op=ALU.max, negate=True).then_inc(D("xmax_ready"), 1)
                dve.wait_ge(S("xexp_ready"), TT * (h + 1))
                step(recip(p_inv, p_sum))
                tt(prob[:, h % 2], prob[:, h % 2], p_inv.unsqueeze(2).broadcast_to([P, TT, MEM]), ALU.mult).then_inc(D("xprob_ready"), 1)

            def xattn_lo(h):
                for d in range(2):
                    dve.wait_ge(S("a_hi_ready"), 2 * KC + 2 * h + d + 1)
                    tt(a_lo[:, 2 * h + d, :], psum[6 + d][:], a_hi[:, 2 * h + d, :].bitcast(F32), ALU.subtract).then_inc(D("a_lo_ready"), 1)

            for s in range(S_XQ, S_XO):
                dve.wait_ge(S("slab_done"), s + 1)
                stt(xq[:, s - S_XQ, :], psum[s % 2][:], 256.0 ** -0.5, rstd[:], ALU.mult, ALU.mult).then_inc(D("tile_taken"), 1)
                if (s - S_XQ) % 2 == 1:
                    h = (s - S_XQ) // 2
                    xattn_softmax(h)
                    if h >= 1:
                        xattn_lo(h - 1)
            xattn_lo(XH - 1)
            residual(S_XO, "norm_mlp", 1)
            dve.wait_ge(S("rms_ready"), 1 + 2)
            recip(rstd[:], rstd[:]).then_inc(D("rstd_ready"), 1)

            for q in range(MLP_Q):
                for n in range(KC):
                    s = S_MLP + 16 * q + n
                    m = m_mid[:, n % 2, :]
                    dve.wait_ge(S("slab_done"), s + 1)
                    if KC * q + n >= 2:
                        dve.wait_ge(S("m_hi_ready"), KC * q + n - 1)
                    tt(m, psum[s % 2][:], rstd[:], ALU.mult).then_inc(D("tile_taken"), 1)
                    stt(m, m, 0.0, m, ALU.max, ALU.mult).then_inc(D("m_ready"), 1)
                    dve.wait_ge(S("m_hi_ready"), KC * q + n + 1)
                    tt(m_lo[:, n, :], m, m_hi[:, n, :].bitcast(F32), ALU.subtract).then_inc(D("m_lo_ready"), 1)
                for n in range(KC):
                    s = S_MLP + 16 * q + 8 + n
                    dve.wait_ge(S("slab_done"), s + 1)
                    tt(x_res[:, n, :], psum[s % 2][:], x_res[:, n, :], ALU.add).then_inc(D("tile_taken"), 1)
                    if q == MLP_Q - 1:
                        dve.wait_ge(S("a_hi_ready"), 3 * KC + n + 1)
                        stt(a_lo[:, n, :], x_res[:, n, :], gain_12[:, n:n + 1], a_hi[:, n, :].bitcast(F32),
                            ALU.mult, ALU.subtract).then_inc(D("a_lo_ready"), 1)
                        if n > 0:
                            dve.wait_ge(S("sqg_ready"), n + 1)
                            tt(sq_sum[:, 1, :], sqg[:, 0, :] if n == 1 else sq_sum[:, 1, :], sqg[:, n % 2, :], ALU.add).then_inc(D("sqg_used"), 1)
            dve.wait_ge(S("rms_ready"), 1 + 3)
            recip(rstd[:], rstd[:]).then_inc(D("rstd_ready"), 1)
            step(tt(rs_tmp[:], rstd[:], rstd[:], ALU.mult))
            dve.wait_ge(S("ssq_done"), 3 + 1)
            tt(rs_tmp[:], psum[6][:], rs_tmp[:], ALU.mult).then_inc(D("mid_var_ready"), 1)
            dve.wait_ge(S("rms3_ready"), 1)
            step(recip(rs_all[:], rs_all[:]))
            tt(rs_all[:], rs_all[:], rstd[:], ALU.mult).then_inc(D("rs_all_ready"), 1)
            dve.wait_ge(S("column_done"), 2 + 1)
            step(cp(r2_tok, psum[7][:, 0:8]))

            def axial_rope(f):
                dve.wait_ge(S("rot_done"), f + 1)
                step(tt(tmp2[:, 0, :], psum[2 + f % 2][:], axial[:, 1, :], ALU.mult))
                step(tt(qk2[:, f, :], qk2[:, f, :], axial[:, 0, :], ALU.mult))
                step(tt(qk2[:, f, :], qk2[:, f, :], tmp2[:, 0, :], ALU.add))
                dve.wait_ge(S("spread2_done"), f + 1)
                tt(qk2[:, f, :], qk2[:, f, :], psum[4 + f % 2][:], ALU.mult).then_inc(D("qk2_ready"), 1)

            def head_lo(f):
                for k in range(2):
                    r = slice(HD * k, HD * k + HD)
                    dve.wait_ge(S("q_hi_ready"), 16 + 2 * f + k + 1)
                    high = k_twice[k][r] if f == 4 else q_stack[k][r, f, :]
                    tt(qk2_lo[r, f, :], qk2[r, f, :], high.bitcast(F32), ALU.subtract).then_inc(D("q_lo_ready"), 1)

            def gated_mlp(f):
                dve.wait_ge(S("gelu_ready"), TT + f + 1)
                dve.wait_ge(S("silu_ready"), 2 * NF + f + 1)
                step(tt(u2[:, f, :], u2[:, f, :], gb[:, f, :], ALU.mult))
                dve.wait_ge(S("vmix_done"), f + 1)
                step(tt(t4(tmp2[:, f % 2, :]), t4(psum[6 + f % 2][:]), b_sp[:, f, :].unsqueeze(1).broadcast_to([P, TT, P]), ALU.add))
                tt(tmp2[:, f % 2, :], tmp2[:, f % 2, :], u2[:, f, :], ALU.mult).then_inc(D("gm_ready"), 1)

            def attn_softmax(i):
                for k in range(2):
                    dve.wait_ge(S("s2_done"), 2 * i + k + 1)
                    hold()
                    nc.vector.tensor_reduce(max2[:, k:k + 1], psum[2 + k][:], axis=AX.X, op=ALU.max, negate=True).then_inc(D("max2_ready"), 1)
                dve.wait_ge(S("exp2_ready"), 2 * i + 2)
                step(recip(inv2, sum2))
                for k in range(2):
                    ts(p2[:, i % 2, k, :], p2[:, i % 2, k, :], inv2[:, k:k + 1], None, ALU.mult).then_inc(D("p2_ready"), 1)

            def attn_gate(f):
                dve.wait_ge(S("o2_done"), 2 * f + 2)
                dve.wait_ge(S("silu_ready"), NF + f + 1)
                tt(ga[:, f, :], psum[6 + f % 2][:], ga[:, f, :], ALU.mult).then_inc(D("oa_ready"), 1)

            for s in range(S_VIN, S_PROJ):
                if s < S_V2 - 1:
                    continue
                dve.wait_ge(S("slab_done"), s + 1)
                bank = psum[s % 2]
                if s < S_V2:
                    for t in range(TT):
                        ts(vv[:, t, :], psum[2 + t][:], r2_tok[:, 2 * t:2 * t + 1], None, ALU.mult).then_inc(D("tile_taken"), 1)
                elif s == S_V2:
                    tt(v2f[:], bank[:], rs_all[:], ALU.mult).then_inc(D("tile_taken"), 1)
                    for n in range(KC):
                        step(stt(x_res[:, n, :], x_res[:, n, :], V("norm_final", n), rstd[:], ALU.mult, ALU.mult))
                elif s < S_U:
                    tt(qk2[:, (s - S_K2 + 4) % 5, :], bank[:], rs_all[:], ALU.mult).then_inc(D("tile_taken"), 1)
                    if s == S_K2:
                        dve.wait_ge(S("v2_done"), 1)
                        cp(v2[:].rearrange("p t e -> p (t e)"), psum[6][:]).then_inc(D("column_ready"), 1)
                        for t in range(TT):
                            dve.wait_ge(S("gelu_ready"), t + 1)
                            hold()
                            step(nc.vector.bn_stats(ln_stats[:, 6 * t:6 * t + 6], vv[:, t, :]))
                            hold()
                            nc.vector.bn_aggr(ln_mv[:, 2 * t:2 * t + 2], ln_stats[:, 6 * t:6 * t + 6]).then_inc(D("ln_mv_ready"), 1)
                    if s == S_K2 + 2:
                        dve.wait_ge(S("sd_ready"), 3)
                        step(recip(ln_rs, ln_rs))
                        dve.wait_ge(S("tables_loaded"), 64)
                    for t in ((0, 1) if s == S_K2 + 2 else (2, 3) if s == S_K2 + 3 else ()):
                        step(ts(vv[:, t, :], vv[:, t, :], ln_mv[:, 2 * t:2 * t + 1], ln_rs[:, t:t + 1], ALU.subtract, ALU.mult))
                        step(tt(vv[:, t, :], vv[:, t, :], ln[:, 0, :], ALU.mult))
                        tt(vv[:, t, :], vv[:, t, :], ln[:, 1, :], ALU.add).then_inc(D("vv_ready"), 1)
                elif s < S_GA:
                    tt(u2[:, s - S_U, :], bank[:], rs_all[:], ALU.mult).then_inc(D("tile_taken"), 1)
                    if s == S_U:
                        dve.wait_ge(S("sq10_ready"), 5)
                        for f in range(5):
                            ts(qk2[:, f, :], qk2[:, f, :], V("k_gain" if f == 4 else "q_gain"), 1.0 if f == 4 else HD ** -0.5,
                               ALU.mult, ALU.mult).then_inc(D("qg_ready"), 1)
                    if s == S_U + 1:
                        dve.wait_ge(S("sd_ready"), 4)
                        step(recip(rn2[0:10, :], rn2[0:10, :]))
                        split(rn2_hi[0:10, :], rn2_lo[0:10, :], rn2[0:10, :]).then_inc(D("rn_ready"), 1)
                elif s < S_GB:
                    tt(ga[:, s - S_GA, :], bank[:], rs_all[:], ALU.mult).then_inc(D("tile_taken"), 1)
                elif s < S_MERGE:
                    tt(gb[:, s - S_GB, :], bank[:], rs_all[:], ALU.mult).then_inc(D("tile_taken"), 1)
                else:
                    m = s - S_MERGE
                    if m == 0:
                        dve.wait_ge(S("vmix_done"), NF)
                    tt(gate[m // KC][:, m % KC, :], bank[:], rs_all[:], ALU.mult).then_inc(D("tile_taken"), 1)
                for f in {S_U + 2: (0, 1), S_U + 3: (2,), S_GA: (3,), S_GA + 1: (4,)}.get(s, ()):
                    axial_rope(f)
                for f in {S_U + 3: (0, 1), S_GA: (2,), S_GA + 1: (3,), S_GA + 2: (4,)}.get(s, ()):
                    head_lo(f)
                if S_GB < s <= S_MERGE:
                    f = s - S_GB - 1
                    gated_mlp(f)
                i = s - S_ATTN
                if 0 <= i < 2 * QH:
                    attn_softmax(i)
                if S_GB < s <= S_MERGE:
                    dve.wait_ge(S("branch_hi"), f + 1)
                    tt(b_lo[:, NF + f, :], tmp2[:, f % 2, :], b_hi[:, NF + f, :].bitcast(F32), ALU.subtract).then_inc(D("branch_lo"), 1)
                if i >= 5 and i % 4 == 1:
                    f = i // 4 - 1
                    attn_gate(f)
                    dve.wait_ge(S("branch_hi"), NF + f + 1)
                    tt(b_lo[:, f, :], ga[:, f, :], b_hi[:, f, :].bitcast(F32), ALU.subtract).then_inc(D("branch_lo"), 1)
            dve.wait_ge(S("gate_ready"), 2 * KC)
            for n in range(KC):
                s = S_PROJ + n
                dve.wait_ge(S("slab_done"), s + 1)
                if n >= 1:
                    dve.wait_ge(S("ym_hi"), n)
                step(tt(y_mid[:, 0, :], psum[s % 2][:], gate[0][:, n, :], ALU.mult))
                tt(y_mid[:, 1, :], psum[2 + s % 2][:], gate[1][:, n, :], ALU.mult).then_inc(D("tile_taken"), 1)
                tt(y_mid[:, 0, :], y_mid[:, 0, :], y_mid[:, 1, :], ALU.add).then_inc(D("y_mid_ready"), 1)
                dve.wait_ge(S("ym_hi"), n + 1)
                tt(y_lo[:, n, :], y_mid[:, 0, :], y_hi[:, n, :].bitcast(F32), ALU.subtract).then_inc(D("ym_lo"), 1)
            for n in range(KC):
                s = S_OUT2 + n
                dve.wait_ge(S("slab_done"), s + 1)
                tt(x_res[:, n, :], psum[s % 2][:], x_res[:, n, :], ALU.add).then_inc(D("tile_taken"), 1)
            dve.wait_ge(S("rms_ready"), 1 + 4)
            recip(rstd[:], rstd[:]).then_inc(D("rstd_ready"), 1)
            for n in range(N_DVE_OUT):
                dve.wait_ge(S("x_gained"), n + 1)
                tt(x_res[:, n, :], x_res[:, n, :], rstd[:], ALU.mult).then_inc(D("out_ready"), 1)

        @block.tensor
        def _(pe):
            mm = nc.tensor.matmul
            wide_slabs = set(range(S_RV, S_WA)) | set(range(S_MV, S_WOUT)) | set(range(S_VIN, S_V2))

            def begin(s):
                pe.wait_ge(S("w_lo_ready"), s + 1)
                before = s - 2
                while before in wide_slabs:
                    before -= 2
                if before >= 0:
                    pe.wait_ge(S("tile_taken"), before + 1)

            def part(s, hi, lo, kcs, ready=None, k=0, at=0, first=0, last=KC - 1):
                high = hi_slot(s)[0]
                for kc in kcs:
                    if ready:
                        pe.wait_ge(S(ready), k + kc + 1)
                    w = slice(kc * P, (kc + 1) * P)
                    o = psum[s % 2 + at][:, 0:hi.shape[2]]
                    mm(o, high[:, w], hi[:, kc, :], start=kc == first, stop=False)
                    mm(o, high[:, w], lo[:, kc, :], start=False, stop=False)
                    done = mm(o, w_lo[:, s % 4, w], hi[:, kc, :], start=False, stop=kc == last)
                return done

            def slab(s, hi, lo, ready=None, k=0):
                begin(s)
                part(s, hi, lo, range(KC), ready, k).then_inc(S("slab_done"), 1)

            def wide(s, hi, lo, kcs, banks, total=KC):
                pe.wait_ge(S("w_lo_ready"), s + 1)
                halves = 2 // len(kcs)
                high = hi_slot(s)[0]
                for i, kc in enumerate(kcs):
                    for t in range(hi.shape[2] // P):
                        for k in range(halves):
                            o = psum[banks[t * halves + k]][:]
                            w = slice((i + k) * 512, (i + k + 1) * 512)
                            c = slice(t * P, (t + 1) * P)
                            mm(o, hi[:, kc, c], high[:, w], start=kc == 0, stop=False)
                            mm(o, lo[:, kc, c], high[:, w], start=False, stop=False)
                            last = mm(o, hi[:, kc, c], w_lo[:, s % 4, w], start=False, stop=kc == KC - 1)
                last.then_inc(S("slab_done"), 1)

            def scores(h):
                f, b = h // 2, HD * (h % 2)
                if h >= 1:
                    pe.wait_ge(S("s_ret_ready"), 4 * h)
                for j in range(TT):
                    w = T - P * j
                    o = psum[(2, 3, 4, 3)[j]][:, (384 if j == 3 else 0):(384 if j == 3 else 0) + w]
                    keys = k_stack[h % 2][:, f, j * P:(j + 1) * P]
                    mm(o, keys, q_twice[h % 2][:, f, j * P:T], start=True, stop=False)
                    last = mm(o, keys[b:b + HD], qk_lo[b:b + HD, f, j * P:T], start=False, stop=True)
                last.then_inc(S("s_ret_done"), 1)

            def ret_out(f):
                if f >= 2:
                    pe.wait_ge(S("y_ret_out"), f - 1)
                off = 0
                for j in range(TT):
                    w = T - P * j
                    pe.wait_ge(S("s_ret_ready"), 4 * (2 * f + 1) + j + 1)
                    for k in range(2):
                        h, b = 2 * f + k, HD * k
                        last = mm(psum[6 + f % 2][b:b + HD, j * P:T], v_ret[:, j, h * HD:(h + 1) * HD], s_ret[:, k, off:off + w],
                                  start=j == 0, stop=j == TT - 1)
                    off += w
                last.then_inc(S("y_ret_step"), 1)

            def decay_rates(t):
                mm(psum[2 + t % 2][:], low[0:HD, 0, t * P:(t + 1) * P], lora[0:HD, :], start=True, stop=True).then_inc(S("lora_done"), 1)

            def learning_rates(f):
                mm(psum[4 + f % 2][:], lora[HD:P, f * P:(f + 1) * P], low[HD:P, 0, :], start=True, stop=True).then_inc(S("lora_done"), 1)

            def output_gates(f):
                mm(psum[6 + f % 2][:], g_up[:, 0, f * P:(f + 1) * P], low[:, 1, :], start=True, stop=False)
                mm(psum[6 + f % 2][:], g_up[0:32, 1, f * P:(f + 1) * P], low[0:32, 2, :], start=False, stop=True).then_inc(S("lora_done"), 1)

            def cumulate(f):
                for k, name in enumerate(("cum_inc", "cum_exc")):
                    for t in range(TT):
                        c = slice(t * P, (t + 1) * P)
                        last = mm(psum[2 + 2 * (f % 2) + k][:, c], lw[:, t, f * P:(f + 1) * P], C(name), start=True, stop=True)
                last.then_inc(S("cum_done"), 1)

            def spread_parts(o, f, hi, lo):
                heads = spread_r[0:hi.shape[0], f * P:(f + 1) * P]
                mm(o, heads, hi, start=True, stop=False)
                return mm(o, heads, lo, start=False, stop=True)

            def spread(f, k, name):
                spread_parts(psum[6 + f % 2][:], k + f, kg_hi[0:16, :], kg_lo[0:16, :]).then_inc(S(name), 1)

            def bonus(f):
                pe.wait_ge(S("rk_ready"), f + 1)
                mm(psum[6 + f % 2][:], C("blockones"), pt[:, 1, :], start=True, stop=True).then_inc(S("bonus_done"), 1)

            pe.wait_ge(S("first_loaded"), 32)
            for s in range(S_MK):
                if S_RV <= s < S_WA:
                    if s == S_RV:
                        pe.wait_ge(S("column_ready"), 1)
                    i = s - S_RV
                    wide(s, a_hi, a_lo, (2 * i, 2 * i + 1), (4, 5, 6, 7))
                else:
                    slab(s, a_hi, a_lo, "a_lo_ready" if s == 0 else None)
                if s == 0:
                    pe.wait_ge(S("x_sq_pool"), 2 * N_POOL_SQ - 1)
                    mm(psum[7][:], C("ones"), sq_in[:, 0, :], start=True, stop=False)
                    pe.wait_ge(S("x_sq_sum"), KC - N_POOL_SQ - 1)
                    mm(psum[7][:], C("ones"), sq_in[:, N_POOL_SQ, :], start=False, stop=True).then_inc(S("ssq_done"), 1)
                if s == 4:
                    for t in range(TT):
                        last = mm(psum[5][:, 2 * t:2 * t + 2], rstd[0:1, t * P:(t + 1) * P], C("ones", 0, 2)[0:1, :],
                                  start=True, stop=True)
                    last.then_inc(S("column_done"), 1)
                if S_RET <= s < S_RET + RH:
                    h = s - S_RET
                    if h == 0:
                        pe.wait_ge(S("q_lo_ready"), 16)
                        pe.wait_ge(S("q_stacked"), 16 * 16)
                        pe.wait_ge(S("tile_taken"), S_RET)
                    elif h % 2 == 0:
                        ret_out(h // 2 - 1)
                    scores(h)
                if s == S_RET + RH:
                    ret_out(NF - 1)
                if s == S_PREP + 1:
                    pe.wait_ge(S("masks_loaded"), 48)
                    pe.wait_ge(S("masks_loaded"), 48)
                    pe.wait_ge(S("low_act"), 3)
                    pe.wait_ge(S("s_ret_ready"), 4 * RH)
                if s in (S_PREP + 1, S_PREP + 2):
                    for i in (2 * (s - S_PREP) - 2, 2 * (s - S_PREP) - 1):
                        if i >= 2:
                            pe.wait_ge(S("lora_ready"), 2 * i - 2)
                        decay_rates(i)
                        learning_rates(i)
                if s == S_PREP + 3:
                    pe.wait_ge(S("y_ret_out"), NF)
                    output_gates(0)
                    output_gates(1)
                    pe.wait_ge(S("lora_ready"), 2 * NF)
                    for f in range(NF):
                        mm(psum[2 + f][:], C("center"), qk[:, f, :], start=True, stop=True).then_inc(S("gn_cent_done"), 1)
                if s == S_PREP + 4:
                    pe.wait_ge(S("lora_ready"), 2 * NF + 2)
                    output_gates(2)
                    output_gates(3)
                if s == S_PREP + 5:
                    pe.wait_ge(S("lora_ready"), 3 * NF)
                    for f in range(NF):
                        pe.wait_ge(S("gn_sq"), f + 1)
                        mm(psum[6][0:16, :], C("sel_g", 16 * f, 16), qk[:, f, :], start=f == 0, stop=False)
                    for f in range(NF):
                        pe.wait_ge(S("sqk_ready"), f + 1)
                        last = mm(psum[6][0:16, :], C("sel_k", 16 * f, 16), sqk[:, f, :], start=False, stop=f == NF - 1)
                    last.then_inc(S("var_done"), 1)
                if s == S_PREP + 6:
                    cumulate(0)
                    cumulate(1)
                if s in (S_PREP + 6, S_PREP + 7):
                    f = 2 * (s - S_PREP) - 12
                    pe.wait_ge(S("rn_ready"), 1)
                    if f > 0:
                        pe.wait_ge(S("ret_ready"), f)
                    spread(f, NF, "gn_spread_done")
                    spread(f + 1, NF, "gn_spread_done")
                if s in (S_PREP + 7, S_PREP + 8):
                    f = s - S_PREP - 5
                    pe.wait_ge(S("exps_ready"), f - 1)
                    cumulate(f)
                if s >= S_RG:
                    f = s - S_RG
                    if f >= 1:
                        bonus(f - 1)
                    if f == 0:
                        pe.wait_ge(S("ret_ready"), NF)
                    if f >= 2:
                        pe.wait_ge(S("prep_ready"), f - 1)
                    spread(f, 0, "kk_done")

            def tok(g, src, i, h):
                n = 2 * i + h
                bank = TOK_BANKS[g][n % 3]
                if n >= 3:
                    pe.wait_ge(S("tok_ready"), 8 * g + n - 2)
                for t in range(2):
                    for f in range(2):
                        c = slice((2 * h + t) * P, (2 * h + t + 1) * P)
                        last = nc.tensor.transpose(psum[bank][:, (2 * t + f) * P:(2 * t + f + 1) * P], src[:, 2 * g + f, c], C("ident"))
                last.then_inc(S("tok_done"), 1)

            def blocks(o, lhsT, rhs, w=P):
                for t in range(TT):
                    c = slice(t * P, (t + 1) * P)
                    last = mm(o[:, t * w:(t + 1) * w], lhsT[:, c], rhs[:, t * w:(t + 1) * w], start=True, stop=True)
                return last

            pe.wait_ge(S("mix_ready"), 3 * NF)
            pe.wait_ge(S("exps_ready"), NF)
            tok(0, vx, 0, 0)
            tok(0, vx, 0, 1)
            pe.wait_ge(S("a_ready"), 2)
            tok(0, kk, 1, 0)
            tok(0, kk, 1, 1)
            pe.wait_ge(S("decayed"), 3 * 2)
            for h in range(2):
                tok(0, ax, 2, h)
            for h in range(2):
                tok(0, kx, 3, h)

            def pair_blocks(pair, k, lhsT, rhs, name):
                for t in range(TT):
                    c = slice(t * P, (t + 1) * P)
                    for j, f, b, _ in pair:
                        last = mm(psum[2 * j + k][:, c], lhsT[b:b + HD, f, c], rhs[b:b + HD, f, c], start=True, stop=True)
                        if t == TT - 1:
                            last.then_inc(S(name), 1)

            for g in range(2):
                heads = [(j, (4 * g + j) // 2, HD * (j % 2), (4 * g + j) * HD) for j in range(4)]
                pairs = [heads[0:2], heads[2:4]]
                for i, pair in enumerate(pairs):
                    if g == 0 and i == 0:
                        pe.wait_ge(S("tile_taken"), S_MK)
                    if g == 1:
                        pe.wait_ge(S("y_rwkv_out"), i + 1)
                    elif i == 1:
                        pe.wait_ge(S("tok_ready"), 8)
                    pair_blocks(pair, 0, ax, kk, "ab_done")
                    if g == 0 and i == 0:
                        bonus(NF - 1)
                    elif g == 0:
                        pe.wait_ge(S("prep_ready"), NF)
                    if g == 0 and i == 0:
                        pe.wait_ge(S("tok_ready"), 6)
                    pair_blocks(pair, 1, kx, kk, "ak_done")
                for i, pair in enumerate(pairs):
                    pe.wait_ge(S("ab_ready"), 4 * g + 2 * i + 2)
                    pair_blocks(pair, 0, ax, rx, "rb_done")
                    pe.wait_ge(S("ak_ready"), 4 * g + 2 * i + 2)
                    pair_blocks(pair, 1, kx, rx, "rk_mm_done")
                for j, f, b, e in heads:
                    pe.wait_ge(S("rb_ready"), 4 * g + j + 1)
                    for t in range(TT):
                        last = mm(psum[2 * j][:, t * HD:(t + 1) * HD], AK[:, j, t * P:(t + 1) * P], v_tok[:, t, e:e + HD],
                                  start=True, stop=True)
                    last.then_inc(S("u_done"), 1)
                    pe.wait_ge(S("xt0_ready"), 4 * g + j + 1)
                    pe.wait_ge(S("rkm_ready"), 4 * g + j + 1)
                    for t in range(TT):
                        c = slice(t * P, (t + 1) * P)
                        last = nc.tensor.transpose(psum[2 * j + 1][:, c], XT[:, j, c], C("ident"))
                    last.then_inc(S("x0_done"), 1)
                for lv in range(5):
                    k = 4 * (5 * g + lv)
                    for j in range(4):
                        if lv == 0:
                            pe.wait_ge(S("u_ready"), 4 * g + j + 1)
                            pe.wait_ge(S("x0_ready"), 4 * g + j + 1)
                            pe.wait_ge(S("tok_ready"), 8 * g + 8)
                        else:
                            pe.wait_ge(S("xt_ready"), 4 * (4 * g + lv - 1) + j + 1)
                        blocks(psum[2 * j], AB[:, j, :], X[:, j, :]).then_inc(S("nx_done"), 1)
                    for j in range(4):
                        pe.wait_ge(S("px_ready"), k + j + 1)
                        if lv < 4:
                            blocks(psum[2 * j + 1], XT[:, j, :], PX[:, j, :]).then_inc(S("xp_done"), 1)
                        else:
                            blocks(psum[2 * j + 1], PX[:, j, :], XT[:, j, :]).then_inc(S("xp_done"), 1)
                    for j in range(4 if lv < 4 else 0):
                        pe.wait_ge(S("xn_ready"), k + j + 1)
                        for t in range(TT):
                            c = slice(t * P, (t + 1) * P)
                            last = nc.tensor.transpose(psum[2 * j][:, c], X[:, j, c], C("ident"))
                        last.then_inc(S("xt_done"), 1)
                for j, f, b, e in heads:
                    pe.wait_ge(S("xn_ready"), 4 * (5 * g + 4) + j + 1)
                    blocks(psum[2 * j], XT[:, j, :], GH[:, j].rearrange("p t k e -> p (t k e)")).then_inc(S("gh_done"), 1)
                for i in range(2):
                    pe.wait_ge(S("gh_ready"), 4 * g + 2 * i + 2)
                    for t in range(TT):
                        c = slice(t * P, (t + 1) * P)
                        for j, f, b, e in heads[2 * i:2 * i + 2]:
                            last = mm(psum[1 + 2 * i][b:b + HD, c], GH[:, j, t, 0, :], RB[:, j, c], start=True, stop=True)
                    last.then_inc(S("qt_done"), 1)
                for i in range(2):
                    pair = heads[2 * i:2 * i + 2]
                    for c in range(NCH - 1):
                        t, r = c // 2, slice(CH * (c % 2), CH * (c % 2) + CH)
                        for j, f, b, e in pair:
                            last = mm(psum[(4, 0)[i] + 2 * (c % 2)][b:b + HD, t * HD:(t + 1) * HD], GH[r, j, t, 0, :], b_tok[r, t, e:e + HD],
                                      start=True, stop=True)
                    last.then_inc(S("at_done"), 1)
                    if i == 1:
                        pe.wait_ge(S("qt_ready"), 2 * g + 2)
                    for c in range(NCH - 1):
                        t, r = c // 2, slice(CH * (c % 2), CH * (c % 2) + CH)
                        o = psum[(5, 1)[i] + 2 * (c % 2)][:, t * HD:(t + 1) * HD]
                        for j, f, b, e in pair:
                            mm(o[b:b + HD], b_tok[r, t, e:e + HD], GH[r, j, t, 1, :], start=True, stop=False)
                        for j, f, b, e in pair:
                            last = mm(o[b:b + HD], k_tok[r, t, e:e + HD], v_tok[r, t, e:e + HD], start=False, stop=True)
                    last.then_inc(S("bc_done"), 1)
                def y_inputs(i, t):
                    o, c = psum[2 + 5 * i], slice(t * P, (t + 1) * P)
                    for j, f, b, e in pairs[i]:
                        mm(o[b:b + HD, c], GH[:, j, t, 1, :], RB[:, j, c], start=t == 0, stop=False)
                    for j, f, b, e in pairs[i]:
                        mm(o[b:b + HD, c], v_tok[:, t, e:e + HD], RK[:, j, c], start=False, stop=False)

                pe.wait_ge(S("bc_ready"), 4 * g + 2)
                for t in range(TT):
                    y_inputs(1, t)
                pe.wait_ge(S("at_ready"), 4 * g + 4)
                for c in range(1, NCH - 1):
                    pe.wait_ge(S("state_ready"), 13 * g + 2 * c - 1)
                    for j, f, b, e in heads:
                        i = j // 2
                        last = mm(psum[0][b:b + HD, i * HD:(i + 1) * HD], AT[b:b + HD, i, c, :], ST[b:b + HD, c, i, :],
                                  start=True, stop=True)
                    last.then_inc(S("state_done"), 1)
                    if g == 0:
                        if c == 1:
                            pe.wait_ge(S("a_ready"), NF)
                            pe.wait_ge(S("decayed"), 3 * NF)
                        if c <= 4:
                            for h in range(2):
                                tok(1, (vx, kk, ax, kx)[c - 1], c - 1, h)
                        else:
                            y_inputs(0, 2 * c - 10)
                            y_inputs(0, 2 * c - 9)
                    else:
                        if c <= 4:
                            y_inputs(0, c - 1)
                        if c >= 3:
                            for kc in (2 * c - 6, 2 * c - 5):
                                pe.wait_ge(S("mem_sq_ready"), kc + 1)
                                last = mm(psum[3][:, 0:MEM], C("ones"), mem_in[:, kc, :], start=kc == 0, stop=kc == KC - 1)
                        if c == 6:
                            last.then_inc(S("mem_ssq_done"), 1)
                pe.wait_ge(S("state_ready"), 13 * g + 13)
                pe.wait_ge(S("tok_ready"), 16)
                pe.wait_ge(S("qt_ready"), 2 * g + 2)
                for i, pair in enumerate(pairs):
                    for k in range(1, NCH):
                        cc = slice(k * CH, (k + 1) * CH)
                        for j, f, b, e in pair:
                            last = mm(psum[2 + 5 * i][b:b + HD, cc], ST[b:b + HD, k, i, :], QT[b:b + HD, i, cc],
                                      start=False, stop=k == NCH - 1)
                    last.then_inc(S("y_rwkv_done"), 1)

            for f in range(NF):
                pe.wait_ge(S("y_rwkv_out"), f + 1)
                mm(psum[4 + f][:], C("center"), rx[:, f, :], start=True, stop=True).then_inc(S("gn_cent_done"), 1)
            for s in range(S_MK, S_MV):
                slab(s, mem_hi, mem_lo, "mem_lo_ready" if s == S_MK else None)
                if s == S_MK + 1:
                    for f in range(NF):
                        pe.wait_ge(S("gn_sq"), NF + f + 1)
                        last = mm(psum[2][0:10, :], C("sel", 10 * f, 10), gsq[:, f, :], start=f == 0, stop=f == NF - 1)
                    last.then_inc(S("var_done"), 1)
                if s in (S_MK + 3, S_MK + 4):
                    pe.wait_ge(S("rn_ready"), 2)
                    for f in (0, 1) if s == S_MK + 3 else (2, 3):
                        spread_parts(psum[4 + f][:], f, hrn_hi[0:8, :], hrn_lo[0:8, :]).then_inc(S("gn_spread_done"), 1)
            pe.wait_ge(S("y_ready"), 2)
            for s in range(S_MV, S_WOUT):
                if s == S_MV + 3:
                    pe.wait_ge(S("y_ready"), 3)
                    for m in range(MEM // P):
                        last = mm(psum[6][:, 2 * m:2 * m + 2], mem_rs[0:1, m * P:(m + 1) * P], C("ones", 0, 2)[0:1, :],
                                  start=True, stop=True)
                    last.then_inc(S("column_done"), 1)
                wide(s, mem_hi, mem_lo, (s - S_MV,), (2, 3, 4, 5))

            def residual_sums(k):
                pe.wait_ge(S("sq_used"), (KC - 2) * (k + 1))
                mm(psum[7][:], C("ones"), sq_sum[:, 0, :], start=True, stop=False)
                pe.wait_ge(S("sq_ready"), KC * (k + 1))
                return mm(psum[7][:], C("ones"), sqb[:, 1, :], start=False, stop=True)

            def slab_and_sums(s, k):
                begin(s)
                part(s, b_hi, b_lo, range(KC - 2), "b_lo_ready", KC * k)
                residual_sums(k).then_inc(S("ssq_done"), 1)
                part(s, b_hi, b_lo, range(KC - 2, KC), "b_lo_ready", KC * k).then_inc(S("slab_done"), 1)

            for n in range(KC):
                slab(S_WOUT + n, a_hi, a_lo, "a_lo_ready" if n == 0 else None, KC)
            def xscores(h):
                for k in range(2):
                    for t in (2 * k, 2 * k + 1):
                        o = psum[2 + k][:, (t % 2) * MEM:(t % 2 + 1) * MEM]
                        for d in range(2):
                            last = mm(o, xq[:, 2 * h + d, t * P:(t + 1) * P], mem_k[:, 2 * h + d, :], start=d == 0, stop=d == 1)
                    last.then_inc(S("xs_done"), 1)

            def xtransposes(h):
                pe.wait_ge(S("xprob_ready"), h + 1)
                for m in range(MEM // P):
                    for t in range(TT):
                        last = nc.tensor.transpose(psum[4 + m][:, t * P:(t + 1) * P], prob[:, h % 2, t, m * P:(m + 1) * P], C("ident"))
                    last.then_inc(S("xprob_t_done"), 1)

            def xout(h):
                if h >= 1:
                    pe.wait_ge(S("a_lo_ready"), 2 * KC + 2 * h)
                for d in range(2):
                    for m in range(MEM // P):
                        pe.wait_ge(S("xprob_t_ready"), 2 * h + m + 1)
                        last = mm(psum[6 + d][:], mem_v[:, m, h * MEM + d * P:h * MEM + (d + 1) * P], prob_t[:, h % 2, m, :],
                                  start=m == 0, stop=m == 1)
                    last.then_inc(S("xo_done"), 1)

            for s in range(S_XQ, S_XO):
                if s == S_XQ:
                    slab_and_sums(s, 0)
                else:
                    slab(s, b_hi, b_lo)
                if (s - S_XQ) % 2 == 1:
                    h = (s - S_XQ) // 2
                    if h >= 1:
                        xtransposes(h - 1)
                    pe.wait_ge(S("tile_taken"), s + 1)
                    xscores(h)
                    if h >= 1:
                        xout(h - 1)
            early, late = range(6), range(6, KC)
            for n in range(2):
                begin(S_XO + n)
                part(S_XO + n, a_hi, a_lo, early, "a_lo_ready", 2 * KC)
            xtransposes(XH - 1)
            xout(XH - 1)
            for n in range(2):
                part(S_XO + n, a_hi, a_lo, late, "a_lo_ready", 2 * KC).then_inc(S("slab_done"), 1)
            for n in range(2, KC):
                slab(S_XO + n, a_hi, a_lo)
            for q in range(MLP_Q):
                for n in range(KC):
                    if q == n == 0:
                        slab_and_sums(S_MLP, 1)
                    else:
                        slab(S_MLP + 16 * q + n, b_hi, b_lo)
                for n in range(KC):
                    slab(S_MLP + 16 * q + 8 + n, m_hi, m_lo, "m_lo_ready" if n == 0 else None, KC * q)

            def qk_norm(f):
                if f >= 2:
                    pe.wait_ge(S("qk2_ready"), f - 1)
                mm(psum[2 + f % 2][:], C("swap_ax"), qk2[:, f, :], start=True, stop=True).then_inc(S("rot_done"), 1)
                spread_parts(psum[4 + f % 2][:], f, rn2_hi[0:10, :], rn2_lo[0:10, :]).then_inc(S("spread2_done"), 1)

            def spatial_mix(f):
                if f >= 2:
                    pe.wait_ge(S("gm_ready"), f - 1)
                for t in range(TT):
                    for k in range(2):
                        g, b = 2 * f + k, HD * k
                        last = mm(psum[6 + f % 2][b:b + HD, t * P:(t + 1) * P], vv[:, t, g * HD:(g + 1) * HD], spatial[:, g, :],
                                  start=True, stop=True)
                last.then_inc(S("vmix_done"), 1)

            def scores2(i):
                f, b, t0 = i // 4, HD * (i % 2), 2 * ((i // 2) % 2)
                for k in range(2):
                    if i >= 1:
                        pe.wait_ge(S("exp2_ready"), 2 * (i - 1) + k + 1)
                    c = slice((t0 + k) * P, (t0 + k + 1) * P)
                    q = q_stack[i % 2][:, f, c]
                    mm(psum[2 + k][:], q, k_twice[i % 2][:], start=True, stop=False)
                    mm(psum[2 + k][:], q[b:b + HD], qk2_lo[b:b + HD, 4, :], start=False, stop=True).then_inc(S("s2_done"), 1)

            def transposes2(i):
                pe.wait_ge(S("p2_ready"), 2 * i + 2)
                if i >= 1:
                    pe.wait_ge(S("p2_t_ready"), 2 * i)
                for c in range(TT):
                    for k in range(2):
                        last = nc.tensor.transpose(psum[4 + c // 2][:, (c % 2) * 256 + k * P:(c % 2) * 256 + (k + 1) * P],
                                                   p2[:, i % 2, k, c * P:(c + 1) * P], C("ident"))
                last.then_inc(S("p2_t_done"), 1)

            def out2(n):
                f, c0 = n // 2, 256 * (n % 2)
                pe.wait_ge(S("p2_t_ready"), 4 * n + 4)
                if f >= 2:
                    pe.wait_ge(S("oa_ready"), f - 1)
                else:
                    pe.wait_ge(S("gm_ready"), 3 + f)
                for c in range(TT):
                    for k in range(2):
                        b = HD * k
                        last = mm(psum[6 + f % 2][b:b + HD, c0:c0 + 256], v2[:, c, b:b + HD], p2_t[:, c, k * 256:(k + 1) * 256],
                                  start=c == 0, stop=c == TT - 1)
                last.then_inc(S("o2_done"), 1)

            for s in range(S_VIN, S_PROJ):
                if s < S_V2:
                    i = s - S_VIN
                    pe.wait_ge(S("a_lo_ready"), 3 * KC + 2 * i + 2)
                    wide(s, a_hi, a_lo, (2 * i, 2 * i + 1), (2, 3, 4, 5))
                    if i == 0:
                        residual_sums(2)
                        pe.wait_ge(S("sqg_used"), KC - 1)
                        mm(psum[6][:], C("ones"), sq_sum[:, 1, :], start=True, stop=True).then_inc(S("ssq_done"), 1)
                    if i == 3:
                        pe.wait_ge(S("rs_all_ready"), 1)
                        for t in range(TT):
                            last = mm(psum[7][:, 2 * t:2 * t + 2], rs_all[0:1, t * P:(t + 1) * P], C("ones", 0, 2)[0:1, :],
                                      start=True, stop=True)
                        last.then_inc(S("column_done"), 1)
                else:
                    slab(s, a_hi, a_lo)
                if s == S_K2:
                    pe.wait_ge(S("tile_taken"), S_V2 + 1)
                    for t in range(TT):
                        last = nc.tensor.transpose(psum[6][:, t * P:(t + 1) * P], v2f[:, t * P:(t + 1) * P], C("ident"))
                    last.then_inc(S("v2_done"), 1)
                if s == S_U:
                    pe.wait_ge(S("column_ready"), 4)
                    for f in range(5):
                        pe.wait_ge(S("sq10_ready"), 5)
                        last = mm(psum[6][0:10, :], C("sel", 10 * f, 10), sq10[:, f, :], start=f == 0, stop=f == 4)
                    last.then_inc(S("var_done"), 1)
                if s == S_U + 2:
                    pe.wait_ge(S("tile_taken"), S_V2)
                    pe.wait_ge(S("qg_ready"), 5)
                    pe.wait_ge(S("rn_ready"), 3)
                for f in {S_U + 2: (0, 1), S_U + 3: (2,), S_GA: (3,), S_GA + 1: (4,)}.get(s, ()):
                    qk_norm(f)
                if S_GB <= s < S_MERGE:
                    if s == S_GB:
                        pe.wait_ge(S("vv_ready"), TT)
                    spatial_mix(s - S_GB)
                i = s - S_ATTN
                if i >= 3 and i % 2 == 1:
                    out2(i // 2 - 1)
                if 0 <= i < 2 * QH:
                    if i == 0:
                        pe.wait_ge(S("q_lo_ready"), 16 + 10)
                        pe.wait_ge(S("q_stacked"), (16 + 10) * 16)
                    scores2(i)
                if 1 <= i <= 2 * QH:
                    transposes2(i - 1)
            for n in range(KC):
                s = S_PROJ + n
                begin(s)
                if n == 0:
                    pe.wait_ge(S("branch_lo"), 2 * NF - 1)
                part(s, b_hi, b_lo, range(NF, KC), at=2, first=NF)
                if n == 0:
                    pe.wait_ge(S("branch_lo"), 2 * NF)
                part(s, b_hi, b_lo, range(NF), last=NF - 1).then_inc(S("slab_done"), 1)
            for n in range(KC):
                slab(S_OUT2 + n, y_hi, y_lo, "ym_lo" if n == 0 else None)
            residual_sums(3).then_inc(S("ssq_done"), 1)


def shape_constants():
    import numpy as np
    i = np.arange(P)
    row, col = i[:, None], i[None, :]
    chunk = (row // CH) == (col // CH)
    mid = (col // CH) * CH + CH // 2 - 1
    before_mid = chunk & (row <= mid)
    t = {}
    t["ident"] = row == col
    t["ones"] = np.ones((P, P))
    t["blockones"] = (row // HD) == (col // HD)
    t["center"] = (row == col) - ((row // HD) == (col // HD)) / HD
    half = HD // 2
    quart = HD // 4
    t["swap_ax"] = (1.0 * ((row // half == col // half) & (col % half >= quart) & (row == col - quart))
                    - 1.0 * ((row // half == col // half) & (col % half < quart) & (row == col + quart)))
    t["cum_inc"] = -EXP_HALF * (1.0 * (chunk & (row <= col)) - 1.0 * before_mid)
    t["cum_exc"] = -EXP_HALF * (1.0 * (chunk & (row < col)) - 1.0 * before_mid)
    t["mask_strict"] = chunk & (row < col)
    t["mask_inc"] = chunk & (row <= col)
    t["mask_pair"] = (row // 2 == col // 2) & (row < col)
    t["mask_level"] = np.concatenate([(row // (2 * b) == col // (2 * b)) & (row // b > col // b)
                                      for b in (2, 4, 8, 16, 32)], axis=1)
    t["sel"] = np.concatenate([np.arange(10)[None, :] == 2 * f + row // HD for f in range(5)], axis=1)
    t["sel_k"] = np.concatenate([np.arange(16)[None, :] == 2 * f + row // HD for f in range(NF)], axis=1)
    t["sel_g"] = np.concatenate([np.arange(16)[None, :] == 8 + 2 * f + row // HD for f in range(NF)], axis=1)
    t["spread"] = np.concatenate([row == 2 * f + col // HD for f in range(8)], axis=1)
    t["kg_scale"] = np.where(i < 8, 1.0, 1.0 / HD)[:, None]
    t["kg_eps"] = np.where(i < 8, 0.0, 1e-5)[:, None]
    t["kg_min"] = np.where(i < 8, 1e-12, 0.0)[:, None]
    t["ident2"] = (row % HD) == np.arange(HD)[None, :]
    for name, e in (("eps6", 1e-6), ("eps64", 64e-5)):
        t[name] = np.full((P, 1), e)
    f32 = np.float32
    t["inv_freq"] = (np.where(i % HD < half, f32(-1.0), f32(1.0)) * f32(10000.0) ** (-(i % half).astype(f32) / f32(half)))[:, None]
    consts = np.concatenate([np.asarray(t[name], f32) for name, _ in CONSTS], axis=1)

    heads = np.arange(RH, dtype=np.float64)
    log_g = np.log(1.0 - 2.0 ** (-5.0 - heads))
    diff = np.arange(T)[None, :] - i[:, None]
    decay = np.where(diff >= 0, np.exp(log_g[:, None, None] * np.maximum(diff, 0)), 0.0) * HD ** -0.5
    decay = np.ascontiguousarray(decay.transpose(1, 0, 2)).astype(f32)

    tok = np.arange(T)
    freq = f32(10000.0) ** (-np.arange(0, half, 2, dtype=f32) / f32(half))
    place = np.where((i % HD < half)[:, None], (tok // 64)[None, :], (tok % 64)[None, :]).astype(f32)
    ang = (place * freq[i % quart][:, None]).astype(f32)
    axial = np.stack([np.cos(ang), np.sin(ang)], axis=1).astype(f32)
    return consts, decay, axial


def lay_out(a):
    import numpy as np

    def slabs(w):
        k, n = w.shape
        return [w[r:r + DM, c:c + P].reshape(-1, P, P).transpose(1, 0, 2).reshape(P, -1)
                for r in range(0, k, DM) for c in range(0, n, P)]

    def wide(w):
        k, n = w.shape
        r = P * DM // n
        return [w[i:i + r].reshape(-1, P, n).transpose(1, 0, 2).reshape(P, -1) for i in range(0, k, r)]

    w_in, w2 = a["w_in"][0], a["w_in_2"][0]
    up, down = a["mlp_w_up"][0], a["mlp_w_down"][0]
    pad = np.zeros((DM, 96), np.float32)
    rw = 2048
    s = slabs(w_in[:, 0:1024]) + wide(w_in[:, 1024:1536])
    s += slabs(w_in[:, rw + 1536:rw + 1792]) + slabs(np.concatenate([w_in[:, rw + 1792:], pad], axis=1))
    s += slabs(w_in[:, rw + 512:rw + 1024]) + slabs(w_in[:, rw:rw + 512]) + slabs(w_in[:, rw + 1024:rw + 1536])
    s += slabs(w_in[:, 1536:rw])
    s += slabs(a["xattn_w_kv"][0][:, :DM]) + wide(a["xattn_w_kv"][0][:, DM:])
    s += slabs(a["w_out"][0]) + slabs(a["xattn_w_q"][0]) + slabs(a["xattn_w_o"][0])
    for q in range(MLP_Q):
        s += slabs(up[:, q * DM:(q + 1) * DM]) + slabs(down[q * DM:(q + 1) * DM, :])
    head = np.concatenate([np.arange(HD) + HD * (f + 4 * k) for f in range(NF) for k in range(2)])
    s += wide(w2[:, 1792:2304]) + slabs(w2[:, 640:768]) + slabs(w2[:, 512:640]) + slabs(w2[:, 0:512][:, head])
    s += slabs(w2[:, 1280:1792]) + slabs(w2[:, 768:1280][:, head]) + slabs(w2[:, 2304:2816])
    s += slabs(w2[:, 2816:4864])
    s += slabs(np.concatenate([a["w_proj_attn_2"][0][head], a["w_proj_gmlp_2"][0]], axis=0))
    s += slabs(a["w_out_2"][0])
    assert len(s) == NSLAB

    def cols(v):
        return np.asarray(v, np.float32).reshape(-1, P).T

    mu = a["rwkv_mu"][0]
    mu_pad = np.concatenate([mu[1536:1824], np.zeros(96, np.float32), mu[512:1024], mu[0:512], mu[1024:1536]])
    vec = {"norm_mix": a["norm_mix"], "ret_gn_w": a["ret_gn_w"], "ret_gn_b": a["ret_gn_b"], "mu": mu_pad,
           "a0": a["rwkv_a0"], "k_k": a["rwkv_k_k"], "k_a": a["rwkv_k_a"], "r_k": a["rwkv_r_k"],
           "gn_w": a["rwkv_gn_w"], "gn_b": a["rwkv_gn_b"], "norm_xattn": a["norm_xattn"], "norm_mem": a["norm_mem"],
           "norm_mlp": a["norm_mlp"], "norm_final": a["norm_final"], "norm_gain_2": a["norm_gain_2"],
           "q_gain": np.concatenate([a["q_gain_2"][0]] * 2), "k_gain": np.concatenate([a["k_gain_2"][0]] * 2),
           "b_merge": a["b_merge_2"], "final_gain": a["final_gain_2"]}
    params = np.concatenate([cols(vec[name]) for name, _ in PARAMS], axis=1)
    consts, decay, axial = shape_constants()

    def feature_major(x):
        return x[0].T.reshape(KC, P, -1).transpose(1, 0, 2)

    g_up = np.concatenate([a["rwkv_g_up"][0], np.zeros((96, 512), np.float32)])
    b_sp = a["b_spatial_2"][0].reshape(NF, 2, P).repeat(HD, axis=1).transpose(1, 0, 2)
    ln = np.stack([np.broadcast_to(a["ln_v_gain_2"][0], (P, 512)), np.broadcast_to(a["ln_v_bias_2"][0], (P, 512))], axis=1)
    arrays = {"weights": np.stack(s), "x": feature_major(a["x"]), "mem": feature_major(a["mem"]),
              "pos": np.broadcast_to(a["positions"], (P, T)), "params": params, "consts": consts, "decay": decay,
              "axial": axial, "lora": np.concatenate([a["rwkv_w_up"][0], a["rwkv_a_up"][0]]),
              "g_up": g_up.reshape(2, P, 512).transpose(1, 0, 2), "w0": np.broadcast_to(a["rwkv_w0"], (P, 512)), "b_sp": b_sp,
              "spatial": a["w_spatial_2"][0].transpose(2, 0, 1), "ln": ln}
    return {name: np.ascontiguousarray(v) for name, v in arrays.items()}


def kernel(**inputs):
    import numpy as np
    import concourse.bacc as bacc
    from concourse.bass_utils import run_bass_kernel_spmd

    arrays = lay_out({name: np.asarray(v) for name, v in inputs.items()})
    nc = bacc.Bacc("TRN2", target_bir_lowering=False, num_devices=1)
    ins = {name: nc.dram_tensor(f"in_{name}", v.shape, mybir.dt.from_np(v.dtype), kind="ExternalInput").ap()
           for name, v in arrays.items()}
    out = nc.dram_tensor("out_fm", (P, KC, T), mybir.dt.float32, kind="ExternalOutput").ap()
    hybrid_blocks(nc, ins, out)
    r = run_bass_kernel_spmd(nc, [{f"in_{name}": v for name, v in arrays.items()}], core_ids=[0])
    return np.ascontiguousarray(r.results[0]["out_fm"].transpose(2, 1, 0).reshape(1, T, DM))
```
